# Optimizing a Trainium2 kernel written in Bass

```python
import jax, jax.numpy as jnp
from jax import lax
import numpy as np
import math

D_MODEL = 1024
BATCH = 1
SEQ = 512
DEPTH = 1

HEAD_DIM = 64
D_MIX = D_MODEL
RG_WIDTH = 3 * D_MIX // 8
HG_WIDTH = 3 * D_MIX // 8
SC_WIDTH = D_MIX - RG_WIDTH - HG_WIDTH
RG_HEADS = RG_WIDTH // HEAD_DIM
HG_HEADS = HG_WIDTH // HEAD_DIM
RG_CONV = 4
SC_CONV = 3
FFN_CONV = 3
RG_C = 8.0
HG_CHUNK = 64
D_FF = 2816
PLE_DIM = 256
EPS = 1e-6
PROJ_SIZES = [RG_WIDTH, RG_WIDTH,
              HG_WIDTH, HG_WIDTH, HG_WIDTH, HG_WIDTH,
              SC_WIDTH, SC_WIDTH, SC_WIDTH]
N_PROJ = sum(PROJ_SIZES)
PROJ_SPLITS = [int(s) for s in np.cumsum(PROJ_SIZES)[:-1]]


def rmsnorm(x, gain):
    xf = x.astype(jnp.float32)
    y = xf * lax.rsqrt(jnp.mean(xf * xf, axis=-1, keepdims=True) + EPS)
    return (y * gain.astype(jnp.float32)).astype(x.dtype)

def head_rmsnorm(y, gain):
    b, t, w = y.shape
    yh = y.reshape(b, t, w // HEAD_DIM, HEAD_DIM)
    yh = yh * lax.rsqrt(jnp.mean(yh * yh, axis=-1, keepdims=True) + EPS)
    return yh.reshape(b, t, w) * gain.astype(jnp.float32)

def causal_dwconv(x, w):
    k = w.shape[0]
    return lax.conv_general_dilated(
        x, w[:, None, :].astype(x.dtype), window_strides=(1,), padding=[(k - 1, 0)],
        dimension_numbers=('NWC', 'WIO', 'NWC'), feature_group_count=x.shape[-1])

def _linear_combine(c1, c2):
    a1, b1 = c1
    a2, b2 = c2
    return a1 * a2, a2 * b1 + b2

def rglru_group(u_in, gate_in, conv_w, conv_b, w_r, b_r, w_i, b_i, lam, gain):
    b, t, _ = u_in.shape
    u = (causal_dwconv(u_in, conv_w) + conv_b.astype(u_in.dtype)).astype(jnp.float32)
    uh = u.reshape(b, t, RG_HEADS, HEAD_DIM)
    r = jax.nn.sigmoid(jnp.einsum('btnd,nde->btne', uh, w_r.astype(jnp.float32))
                       + b_r.astype(jnp.float32)).reshape(b, t, RG_WIDTH)
    ig = jax.nn.sigmoid(jnp.einsum('btnd,nde->btne', uh, w_i.astype(jnp.float32))
                        + b_i.astype(jnp.float32)).reshape(b, t, RG_WIDTH)
    log_a = -RG_C * r * jax.nn.softplus(-lam.astype(jnp.float32))
    a = jnp.exp(log_a)
    beta = jnp.sqrt(-jnp.expm1(2.0 * log_a))
    _, h = lax.associative_scan(_linear_combine, (a, beta * ig * u), axis=1)
    return head_rmsnorm(h * jax.nn.gelu(gate_in.astype(jnp.float32)), gain)

def hgrn2_group(q, f_raw, v, g, lb, gain):
    b, t, _ = q.shape
    nc = t // HG_CHUNK
    qf = jax.nn.silu(q.astype(jnp.float32)) * HEAD_DIM ** -0.5
    f = lb + (1.0 - lb) * jax.nn.sigmoid(f_raw.astype(jnp.float32))
    log_f = jnp.log(f)
    k = 1.0 - f

    def to_chunks(u):
        return u.reshape(b, nc, HG_CHUNK, HG_HEADS, HEAD_DIM).transpose(1, 0, 3, 2, 4)

    mask = jnp.tril(jnp.ones((HG_CHUNK, HG_CHUNK), dtype=bool))[:, :, None]

    def step(S, inp):
        qc, kc, vc, lfc = inp
        G = jnp.cumsum(lfc, axis=2)
        o_inter = jnp.einsum('bhtk,bhkv->bhtv', qc * jnp.exp(G), S)
        diff = G[:, :, :, None, :] - G[:, :, None, :, :]
        decay = jnp.where(mask, jnp.exp(jnp.minimum(diff, 0.0)), 0.0)
        scores = jnp.einsum('bhtk,bhsk,bhtsk->bhts', qc, kc, decay)
        o_intra = jnp.einsum('bhts,bhsv->bhtv', scores, vc)
        G_last = G[:, :, -1:, :]
        S_new = (jnp.exp(G_last[:, :, 0, :])[..., None] * S
                 + jnp.einsum('bhsk,bhsv->bhkv', kc * jnp.exp(G_last - G), vc))
        return S_new, o_inter + o_intra

    S0 = jnp.zeros((b, HG_HEADS, HEAD_DIM, HEAD_DIM), jnp.float32)
    _, o = lax.scan(step, S0, (to_chunks(qf), to_chunks(k),
                               to_chunks(v.astype(jnp.float32)), to_chunks(log_f)))
    o = o.transpose(1, 0, 3, 2, 4).reshape(b, t, HG_WIDTH)
    return head_rmsnorm(o, gain) * jax.nn.silu(g.astype(jnp.float32))

def shortconv_group(bg, cg, v, conv_w, gain):
    y = bg * causal_dwconv(cg * v, conv_w)
    return head_rmsnorm(y.astype(jnp.float32), gain)

def conv_ffn(h, w_up, conv_w, w_down):
    gu = causal_dwconv(h @ w_up, conv_w)
    g, u = jnp.split(gu, 2, axis=-1)
    return (jax.nn.silu(g) * u) @ w_down

def first_inputs(seed: int = 0) -> dict:
    key = jax.random.key(seed)
    ks = jax.random.split(key, 24)
    n = jax.random.normal
    f32 = jnp.float32
    u = jax.random.uniform(ks[10], (DEPTH, RG_WIDTH), f32, 0.9, 0.999)
    a0 = u ** (1.0 / RG_C)
    rg_lambda = jnp.log(a0) - jnp.log1p(-a0)
    return {
        'x': n(ks[0], (BATCH, SEQ, D_MODEL), f32),
        'p': n(ks[1], (DEPTH, BATCH, SEQ, PLE_DIM), f32),
        'norm_mix_gain': 1.0 + 0.02 * n(ks[2], (DEPTH, D_MODEL), f32),
        'w_in': n(ks[3], (DEPTH, D_MODEL, N_PROJ), f32) * D_MODEL ** -0.5,
        'rg_conv_w': n(ks[4], (DEPTH, RG_CONV, RG_WIDTH), f32) * RG_CONV ** -0.5,
        'rg_conv_b': 0.01 * n(ks[5], (DEPTH, RG_WIDTH), f32),
        'rg_w_r': n(ks[6], (DEPTH, RG_HEADS, HEAD_DIM, HEAD_DIM), f32) * HEAD_DIM ** -0.5,
        'rg_b_r': 0.01 * n(ks[7], (DEPTH, RG_HEADS, HEAD_DIM), f32),
        'rg_w_i': n(ks[8], (DEPTH, RG_HEADS, HEAD_DIM, HEAD_DIM), f32) * HEAD_DIM ** -0.5,
        'rg_b_i': 0.01 * n(ks[9], (DEPTH, RG_HEADS, HEAD_DIM), f32),
        'rg_lambda': rg_lambda,
        'hg_lower_bounds': 0.1 * n(ks[11], (DEPTH, HG_WIDTH), f32),
        'sc_conv_w': n(ks[12], (DEPTH, SC_CONV, SC_WIDTH), f32) * SC_CONV ** -0.5,
        'mix_out_gain': 1.0 + 0.02 * n(ks[13], (DEPTH, D_MIX), f32),
        'w_out': n(ks[14], (DEPTH, D_MIX, D_MODEL), f32) * D_MIX ** -0.5,
        'norm_ffn_gain': 1.0 + 0.02 * n(ks[15], (DEPTH, D_MODEL), f32),
        'ffn_w_up': n(ks[16], (DEPTH, D_MODEL, 2 * D_FF), f32) * D_MODEL ** -0.5,
        'ffn_conv_w': n(ks[17], (DEPTH, FFN_CONV, 2 * D_FF), f32) * FFN_CONV ** -0.5,
        'ffn_w_down': n(ks[18], (DEPTH, D_FF, D_MODEL), f32) * D_FF ** -0.5,
        'ple_w_proj': n(ks[19], (DEPTH, PLE_DIM, D_MODEL), f32) * PLE_DIM ** -0.5,
        'ple_w_gate': n(ks[20], (DEPTH, D_MODEL, D_MODEL), f32) * D_MODEL ** -0.5,
        'final_norm_gain': 1.0 + 0.02 * n(ks[21], (D_MODEL,), f32),
    }

def first_block(x, p, norm_mix_gain, w_in, rg_conv_w, rg_conv_b, rg_w_r, rg_b_r, rg_w_i, rg_b_i,
              rg_lambda, hg_lower_bounds, sc_conv_w, mix_out_gain, w_out, norm_ffn_gain,
              ffn_w_up, ffn_conv_w, ffn_w_down, ple_w_proj, ple_w_gate, final_norm_gain):
    dt = x.dtype
    sm = jax.nn.softmax(hg_lower_bounds.astype(jnp.float32), axis=0)
    lower_bound = jnp.cumsum(sm, axis=0) - sm[0:1]
    for i in range(DEPTH):
        h = rmsnorm(x, norm_mix_gain[i])
        z = h @ w_in[i]
        a_u, a_gate, b_q, b_f, b_v, b_g, c_b, c_c, c_v = jnp.split(z, PROJ_SPLITS, axis=-1)
        g_a, g_b, g_c = jnp.split(mix_out_gain[i], [RG_WIDTH, RG_WIDTH + HG_WIDTH])
        y_a = rglru_group(a_u, a_gate, rg_conv_w[i], rg_conv_b[i], rg_w_r[i], rg_b_r[i],
                          rg_w_i[i], rg_b_i[i], rg_lambda[i], g_a)
        y_b = hgrn2_group(b_q, b_f, b_v, b_g, lower_bound[i], g_b)
        y_c = shortconv_group(c_b, c_c, c_v, sc_conv_w[i], g_c)
        y = jnp.concatenate([y_a, y_b, y_c], axis=-1).astype(dt)
        x = x + y @ w_out[i]
        x = x + conv_ffn(rmsnorm(x, norm_ffn_gain[i]), ffn_w_up[i], ffn_conv_w[i], ffn_w_down[i])
        gate = jax.nn.sigmoid((x @ ple_w_gate[i]).astype(jnp.float32))
        x = x + (gate * (p[i] @ ple_w_proj[i]).astype(jnp.float32)).astype(dt)
    return rmsnorm(x, final_norm_gain)


CHUNK = 64
Q_BLOCK = 128
NORM_EPS = 1e-6

MLA_HEADS = 8
MLA_Q_RANK = 384
MLA_KV_RANK = 256
MLA_NOPE = 64
MLA_ROPE = 32
MLA_QK_DIM = MLA_NOPE + MLA_ROPE
MLA_V = 64
ROPE_THETA = 10000.0

FOX_HEADS = 8
FOX_HEAD_DIM = 64
FOX_WIDTH = FOX_HEADS * FOX_HEAD_DIM

SSM_HEADS = 16
SSM_HEAD_DIM = 64
SSM_INNER = SSM_HEADS * SSM_HEAD_DIM
SSM_GROUPS = 2
SSM_STATE = 128
SSM_CONV = 4
SSM_XBC = SSM_INNER + 2 * SSM_GROUPS * SSM_STATE


N_BRANCH = 3
MLA_OUT = MLA_HEADS * MLA_V
MLA_IN = MLA_Q_RANK + MLA_KV_RANK + MLA_ROPE
FOX_IN = 3 * FOX_WIDTH + FOX_HEADS
SSM_IN = SSM_INNER + SSM_XBC + SSM_HEADS
GATE_IN = N_BRANCH * D_MODEL
D_IN = MLA_IN + FOX_IN + SSM_IN + GATE_IN


def rms_norm(x, gain):
    xf = x.astype(jnp.float32)
    y = xf * lax.rsqrt(jnp.mean(xf * xf, axis=-1, keepdims=True) + NORM_EPS)
    return (y * gain.astype(jnp.float32)).astype(x.dtype)

def causal_dwconv_2(x, w, b):
    K, C = w.shape
    y = lax.conv_general_dilated(x, w[:, None, :].astype(x.dtype), window_strides=(1,),
                                 padding=[(K - 1, 0)], dimension_numbers=('NWC', 'WIO', 'NWC'),
                                 feature_group_count=C)
    return y + b

def rope_tables(positions):
    inv = 1.0 / (ROPE_THETA ** (jnp.arange(0, MLA_ROPE, 2, dtype=jnp.float32) / MLA_ROPE))
    ang = positions.astype(jnp.float32)[..., None] * inv
    return jnp.cos(ang)[:, :, None, :], jnp.sin(ang)[:, :, None, :]

def rope_tail(x, cos, sin):
    x_nope, x_rope = jnp.split(x, [MLA_NOPE], axis=-1)
    x1, x2 = jnp.split(x_rope.astype(jnp.float32), 2, axis=-1)
    rot = jnp.concatenate([x1 * cos - x2 * sin, x1 * sin + x2 * cos], axis=-1).astype(x.dtype)
    return jnp.concatenate([x_nope, rot], axis=-1)

def blocked_attention(q, k, v, bias_mask):
    Bsz, S, H, Dk = q.shape
    nb = S // Q_BLOCK
    qb = jnp.moveaxis(q.reshape(Bsz, nb, Q_BLOCK, H, Dk), 1, 0)
    scale = Dk ** -0.5

    def one_block(args):
        i, q_blk = args
        s = jnp.einsum('bqhd,bkhd->bhqk', q_blk, k).astype(jnp.float32) * scale
        p = jax.nn.softmax(bias_mask(i, s), axis=-1).astype(v.dtype)
        return jnp.einsum('bhqk,bkhd->bqhd', p, v)

    out = lax.map(one_block, (jnp.arange(nb), qb))
    return jnp.moveaxis(out, 0, 1).reshape(Bsz, S, H, v.shape[-1])

def mla_branch(u, cos, sin, q_norm_g, w_uq, kv_norm_g, w_ukv, q_gain, k_gain):
    Bsz, S, _ = u.shape
    c_q, c_kv, k_rope = jnp.split(u, [MLA_Q_RANK, MLA_Q_RANK + MLA_KV_RANK], axis=-1)
    q = (rms_norm(c_q, q_norm_g) @ w_uq).reshape(Bsz, S, MLA_HEADS, MLA_QK_DIM)
    kv = (rms_norm(c_kv, kv_norm_g) @ w_ukv).reshape(Bsz, S, MLA_HEADS, MLA_NOPE + MLA_V)
    k_nope, v = jnp.split(kv, [MLA_NOPE], axis=-1)
    k_rope = jnp.broadcast_to(k_rope[:, :, None, :], (Bsz, S, MLA_HEADS, MLA_ROPE))
    k = jnp.concatenate([k_nope, k_rope], axis=-1)
    q = rope_tail(rms_norm(q, q_gain), cos, sin)
    k = rope_tail(rms_norm(k, k_gain), cos, sin)

    def chunk_mask(i, s):
        q_idx = i * Q_BLOCK + jnp.arange(Q_BLOCK)
        k_idx = jnp.arange(S)
        allowed = (k_idx[None, :] // CHUNK) <= (q_idx[:, None] // CHUNK)
        return jnp.where(allowed, s, -jnp.inf)

    return blocked_attention(q, k, v, chunk_mask).reshape(Bsz, S, MLA_OUT)

def fox_branch(u, q_gain, k_gain, b_f):
    Bsz, S, _ = u.shape
    q, k, v, f_raw = jnp.split(u, [FOX_WIDTH, 2 * FOX_WIDTH, 3 * FOX_WIDTH], axis=-1)
    q = rms_norm(q.reshape(Bsz, S, FOX_HEADS, FOX_HEAD_DIM), q_gain)
    k = rms_norm(k.reshape(Bsz, S, FOX_HEADS, FOX_HEAD_DIM), k_gain)
    v = v.reshape(Bsz, S, FOX_HEADS, FOX_HEAD_DIM)
    log_f = jax.nn.log_sigmoid(f_raw.astype(jnp.float32) + b_f.astype(jnp.float32))
    F = jnp.transpose(jnp.cumsum(log_f, axis=1), (0, 2, 1))

    def decay_mask(i, s):
        q_idx = i * Q_BLOCK + jnp.arange(Q_BLOCK)
        k_idx = jnp.arange(S)
        Fq = lax.dynamic_slice_in_dim(F, i * Q_BLOCK, Q_BLOCK, axis=2)
        s = s + Fq[..., :, None] - F[..., None, :]
        return jnp.where(k_idx[None, :] <= q_idx[:, None], s, -jnp.inf)

    return blocked_attention(q, k, v, decay_mask).reshape(Bsz, S, FOX_WIDTH)

def ssd_scan(x, dt, A, Bm, Cm):
    Bsz, L, H, P = x.shape
    G, N = Bm.shape[-2:]
    Hg = H // G
    nc = L // CHUNK
    xf = x.astype(jnp.float32).reshape(Bsz, nc, CHUNK, G, Hg, P)
    dtc = dt.reshape(Bsz, nc, CHUNK, G, Hg)
    Bc = Bm.astype(jnp.float32).reshape(Bsz, nc, CHUNK, G, N)
    Cc = Cm.astype(jnp.float32).reshape(Bsz, nc, CHUNK, G, N)
    a_cum = jnp.cumsum(dtc * A.astype(jnp.float32).reshape(G, Hg), axis=2)
    xdt = xf * dtc[..., None]
    causal = jnp.tril(jnp.ones((CHUNK, CHUNK), dtype=bool))[None, None, :, :, None, None]
    seg = a_cum[:, :, :, None] - a_cum[:, :, None, :]
    decay = jnp.where(causal, jnp.exp(jnp.where(causal, seg, 0.0)), 0.0)
    cb = jnp.einsum('bcign,bcjgn->bcijg', Cc, Bc)
    y_diag = jnp.einsum('bcijg,bcijgh,bcjghp->bcighp', cb, decay, xdt)
    decay_to_end = jnp.exp(a_cum[:, :, -1:] - a_cum)
    states = jnp.einsum('bcjgn,bcjgh,bcjghp->bcghpn', Bc, decay_to_end, xdt)
    chunk_decay = jnp.exp(a_cum[:, :, -1])

    def step(h, inp):
        st, dec = inp
        return h * dec[..., None, None] + st, h

    h0 = jnp.zeros((Bsz, G, Hg, P, N), jnp.float32)
    _, h_in = lax.scan(step, h0, (jnp.moveaxis(states, 1, 0), jnp.moveaxis(chunk_decay, 1, 0)))
    h_in = jnp.moveaxis(h_in, 0, 1)
    y_off = jnp.einsum('bcign,bcghpn,bcigh->bcighp', Cc, h_in, jnp.exp(a_cum))
    return (y_diag + y_off).reshape(Bsz, L, H, P).astype(x.dtype)

def ssm_branch(u, conv_w, conv_b, dt_bias, A_log, D, norm_g):
    Bsz, S, _ = u.shape
    z, xBC, dt_raw = jnp.split(u, [SSM_INNER, SSM_INNER + SSM_XBC], axis=-1)
    xBC = jax.nn.silu(causal_dwconv_2(xBC, conv_w, conv_b))
    xs, Bm, Cm = jnp.split(xBC, [SSM_INNER, SSM_INNER + SSM_GROUPS * SSM_STATE], axis=-1)
    dt = jax.nn.softplus(dt_raw.astype(jnp.float32) + dt_bias.astype(jnp.float32))
    A = -jnp.exp(A_log.astype(jnp.float32))
    xh = xs.reshape(Bsz, S, SSM_HEADS, SSM_HEAD_DIM)
    y = ssd_scan(xh, dt, A, Bm.reshape(Bsz, S, SSM_GROUPS, SSM_STATE),
                 Cm.reshape(Bsz, S, SSM_GROUPS, SSM_STATE))
    y = (y + xh * D[:, None]).reshape(Bsz, S, SSM_INNER)
    return rms_norm(y * jax.nn.silu(z), norm_g)

def conv_ffn_2(h, w_up, conv_w, conv_b, w_down):
    a = causal_dwconv_2(h @ w_up, conv_w, conv_b)
    gate, val = jnp.split(a, 2, axis=-1)
    return (jax.nn.silu(gate) * val) @ w_down

def second_inputs(seed: int = 0) -> dict:
    key = jax.random.key(seed)
    ks = iter(jax.random.split(key, 48))
    f32 = jnp.float32
    L = DEPTH

    def nrm(shape, scale):
        return scale * jax.random.normal(next(ks), shape, f32)

    def gain(shape):
        return 1.0 + 0.02 * jax.random.normal(next(ks), shape, f32)

    x = jax.random.normal(next(ks), (BATCH, SEQ, D_MODEL), f32)
    steps = jax.random.randint(next(ks), (BATCH, SEQ), 1, 3, dtype=jnp.int32)
    positions = (jnp.cumsum(steps, axis=1) - 1).astype(jnp.int32)
    dt0 = jnp.exp(jax.random.uniform(next(ks), (L, SSM_HEADS), f32, math.log(1e-3), math.log(1e-1)))
    return {
        'x': x,
        'positions': positions,
        'norm_mix_g': gain((L, D_MODEL)),
        'w_in': nrm((L, D_MODEL, D_IN), D_MODEL ** -0.5),
        'b_gate': nrm((L, GATE_IN), 0.01),
        'mla_q_norm_g': gain((L, MLA_Q_RANK)),
        'mla_w_uq': nrm((L, MLA_Q_RANK, MLA_HEADS * MLA_QK_DIM), MLA_Q_RANK ** -0.5),
        'mla_kv_norm_g': gain((L, MLA_KV_RANK)),
        'mla_w_ukv': nrm((L, MLA_KV_RANK, MLA_HEADS * (MLA_NOPE + MLA_V)), MLA_KV_RANK ** -0.5),
        'mla_q_gain': gain((L, MLA_QK_DIM)),
        'mla_k_gain': gain((L, MLA_QK_DIM)),
        'fox_q_gain': gain((L, FOX_HEAD_DIM)),
        'fox_k_gain': gain((L, FOX_HEAD_DIM)),
        'fox_b_f': jax.random.uniform(next(ks), (L, FOX_HEADS), f32, 2.0, 6.0),
        'ssm_conv_w': nrm((L, SSM_CONV, SSM_XBC), SSM_CONV ** -0.5),
        'ssm_conv_b': nrm((L, SSM_XBC), 0.01),
        'ssm_dt_bias': dt0 + jnp.log(-jnp.expm1(-dt0)),
        'ssm_A_log': jnp.log(jax.random.uniform(next(ks), (L, SSM_HEADS), f32, 1.0, 16.0)),
        'ssm_D': gain((L, SSM_HEADS)),
        'ssm_norm_g': gain((L, SSM_INNER)),
        'w_br_mla': nrm((L, MLA_OUT, D_MODEL), MLA_OUT ** -0.5),
        'w_br_fox': nrm((L, FOX_WIDTH, D_MODEL), FOX_WIDTH ** -0.5),
        'w_br_ssm': nrm((L, SSM_INNER, D_MODEL), SSM_INNER ** -0.5),
        'w_out': nrm((L, D_MODEL, D_MODEL), D_MODEL ** -0.5),
        'norm_ffn_g': gain((L, D_MODEL)),
        'ffn_w_up': nrm((L, D_MODEL, 2 * D_FF), D_MODEL ** -0.5),
        'ffn_conv_w': nrm((L, FFN_CONV, 2 * D_FF), FFN_CONV ** -0.5),
        'ffn_conv_b': nrm((L, 2 * D_FF), 0.01),
        'ffn_w_down': nrm((L, D_FF, D_MODEL), D_FF ** -0.5),
    }

def second_block(x, positions, norm_mix_g, w_in, b_gate, mla_q_norm_g, mla_w_uq, mla_kv_norm_g,
              mla_w_ukv, mla_q_gain, mla_k_gain, fox_q_gain, fox_k_gain, fox_b_f, ssm_conv_w,
              ssm_conv_b, ssm_dt_bias, ssm_A_log, ssm_D, ssm_norm_g, w_br_mla, w_br_fox, w_br_ssm,
              w_out, norm_ffn_g, ffn_w_up, ffn_conv_w, ffn_conv_b, ffn_w_down):
    Bsz, S, _ = x.shape
    cos, sin = rope_tables(positions)
    split_at = [MLA_IN, MLA_IN + FOX_IN, MLA_IN + FOX_IN + SSM_IN]
    for l in range(DEPTH):
        hn = rms_norm(x, norm_mix_g[l])
        u = hn @ w_in[l]
        u_mla, u_fox, u_ssm, u_gate = jnp.split(u, split_at, axis=-1)
        y_a = mla_branch(u_mla, cos, sin, mla_q_norm_g[l], mla_w_uq[l], mla_kv_norm_g[l],
                         mla_w_ukv[l], mla_q_gain[l], mla_k_gain[l]) @ w_br_mla[l]
        y_b = fox_branch(u_fox, fox_q_gain[l], fox_k_gain[l], fox_b_f[l]) @ w_br_fox[l]
        y_c = ssm_branch(u_ssm, ssm_conv_w[l], ssm_conv_b[l], ssm_dt_bias[l], ssm_A_log[l],
                         ssm_D[l], ssm_norm_g[l]) @ w_br_ssm[l]
        g = jax.nn.sigmoid(u_gate + b_gate[l]).reshape(Bsz, S, N_BRANCH, D_MODEL)
        merged = g[:, :, 0] * y_a + g[:, :, 1] * y_b + g[:, :, 2] * y_c
        x = x + merged @ w_out[l]
        x = x + conv_ffn_2(rms_norm(x, norm_ffn_g[l]), ffn_w_up[l], ffn_conv_w[l], ffn_conv_b[l],
                         ffn_w_down[l])
    return x


def setup_inputs(seed=0):
    out = dict(first_inputs(seed))
    for name, value in second_inputs(seed + 1).items():
        if name != "x":
            out[name + "_2"] = value
    return out


def reference(
    x, p, norm_mix_gain, w_in, rg_conv_w, rg_conv_b, rg_w_r, rg_b_r, rg_w_i, rg_b_i, rg_lambda,
    hg_lower_bounds, sc_conv_w, mix_out_gain, w_out, norm_ffn_gain, ffn_w_up, ffn_conv_w,
    ffn_w_down, ple_w_proj, ple_w_gate, final_norm_gain, positions_2, norm_mix_g_2, w_in_2,
    b_gate_2, mla_q_norm_g_2, mla_w_uq_2, mla_kv_norm_g_2, mla_w_ukv_2, mla_q_gain_2,
    mla_k_gain_2, fox_q_gain_2, fox_k_gain_2, fox_b_f_2, ssm_conv_w_2, ssm_conv_b_2,
    ssm_dt_bias_2, ssm_A_log_2, ssm_D_2, ssm_norm_g_2, w_br_mla_2, w_br_fox_2, w_br_ssm_2,
    w_out_2, norm_ffn_g_2, ffn_w_up_2, ffn_conv_w_2, ffn_conv_b_2, ffn_w_down_2,
):
    x = first_block(
        x, p, norm_mix_gain, w_in, rg_conv_w, rg_conv_b, rg_w_r, rg_b_r, rg_w_i, rg_b_i,
        rg_lambda, hg_lower_bounds, sc_conv_w, mix_out_gain, w_out, norm_ffn_gain, ffn_w_up,
        ffn_conv_w, ffn_w_down, ple_w_proj, ple_w_gate, final_norm_gain,
    )
    return second_block(
        x, positions_2, norm_mix_g_2, w_in_2, b_gate_2, mla_q_norm_g_2, mla_w_uq_2,
        mla_kv_norm_g_2, mla_w_ukv_2, mla_q_gain_2, mla_k_gain_2, fox_q_gain_2, fox_k_gain_2,
        fox_b_f_2, ssm_conv_w_2, ssm_conv_b_2, ssm_dt_bias_2, ssm_A_log_2, ssm_D_2,
        ssm_norm_g_2, w_br_mla_2, w_br_fox_2, w_br_ssm_2, w_out_2, norm_ffn_g_2, ffn_w_up_2,
        ffn_conv_w_2, ffn_conv_b_2, ffn_w_down_2,
    )


_drawn_inputs = setup_inputs


def setup_inputs(seed=0):
    import zlib

    import numpy as np

    out = dict(_drawn_inputs(seed))
    spreads = {}
    factors = {'rg_b_r': 8.0,
     'rg_b_i': 8.0,
     'mix_out_gain': 3.052,
     'norm_ffn_gain': 3.954,
     'norm_mix_g_2': 3.354,
     'b_gate_2': 8.0,
     'mla_q_norm_g_2': 8.0,
     'mla_kv_norm_g_2': 8.0,
     'mla_q_gain_2': 8.0,
     'mla_k_gain_2': 8.0,
     'fox_q_gain_2': 8.0,
     'fox_k_gain_2': 8.0,
     'ssm_conv_b_2': 22.966,
     'ssm_D_2': 200.0,
     'ssm_norm_g_2': 18.958,
     'norm_ffn_g_2': 12.221,
     'ffn_conv_b_2': 23.913}
    for name, (base, spread) in spreads.items():
        noise = np.random.default_rng([zlib.crc32(name.encode()), seed]).standard_normal(out[name].shape)
        drawn = base * np.exp(spread * noise) if base else spread * noise
        out[name] = __import__('jax').numpy.asarray(drawn.astype(out[name].dtype))
    for name, factor in factors.items():
        out[name] = (out[name] * factor).astype(out[name].dtype)
    return out
```

```python
from contextlib import ExitStack

import numpy as np
import concourse.bass as bass
from concourse import mybir

F32 = mybir.dt.float32
F32R = mybir.dt.float32r
I32 = mybir.dt.int32
ACT = mybir.ActivationFunctionType
ALU = mybir.AluOpType
AX = mybir.AxisListType.X

P = 128
S = 512
NT = S // P
D = 1024
KD = D // P
DFF = 2816
NF = DFF // P
EPS = 1e-6
HD = 64
RG, HG, SC = 3, 3, 2
A_U, A_GATE, B_Q, B_F, B_V, B_G, C_B, C_C, C_V = 0, 3, 6, 9, 12, 15, 18, 20, 22
N_PROJ = 24
PLE = 256
MLA_Q, MLA_KV, ROPE = 384, 256, 32
NOPE, QK = 64, 96
COL_KROPE = MLA_Q + MLA_KV
COL_FOX = COL_KROPE + ROPE
FOX = 512
COL_F = COL_FOX + 3 * FOX
COL_Z = COL_F + 8
SSM = 1024
COL_XBC = COL_Z + SSM
NXBC = 12
COL_DT = COL_XBC + NXBC * P
COL_GATE = COL_DT + 16
HEADS = 16
NEG = -1e30
WT = 2048

INPUTS = [
    "x", "p", "norm_mix_gain", "w_in", "rg_conv_w", "rg_conv_b", "rg_w_r", "rg_b_r", "rg_w_i", "rg_b_i",
    "rg_lambda", "hg_lower_bounds", "sc_conv_w", "mix_out_gain", "w_out", "norm_ffn_gain", "ffn_w_up",
    "ffn_conv_w", "ffn_w_down", "ple_w_proj", "ple_w_gate", "final_norm_gain", "positions_2", "norm_mix_g_2",
    "w_in_2", "b_gate_2", "mla_q_norm_g_2", "mla_w_uq_2", "mla_kv_norm_g_2", "mla_w_ukv_2", "mla_q_gain_2",
    "mla_k_gain_2", "fox_q_gain_2", "fox_k_gain_2", "fox_b_f_2", "ssm_conv_w_2", "ssm_conv_b_2",
    "ssm_dt_bias_2", "ssm_A_log_2", "ssm_D_2", "ssm_norm_g_2", "w_br_mla_2", "w_br_fox_2", "w_br_ssm_2",
    "w_out_2", "norm_ffn_g_2", "ffn_w_up_2", "ffn_conv_w_2", "ffn_conv_b_2", "ffn_w_down_2",
]

PARAM_ROWS = [
    (0, "norm_mix_gain", 8, 0), (0, "rg_conv_w", 12, 0), (0, "rg_conv_b", 3, 0), (0, "rg_b_r", 3, 0),
    (0, "rg_b_i", 3, 0), (0, "rg_lambda", 3, 0), (0, "hg_lower_bounds", 3, 0), (0, "sc_conv_w", 6, 0),
    (0, "mix_out_gain", 8, 0), (0, "norm_ffn_gain", 8, 0), (0, "final_norm_gain", 8, 0),
    (0, "norm_mix_g_2", 8, 0), (0, "b_gate_2", 24, 0), (0, "mla_q_norm_g_2", 3, 0), (0, "mla_kv_norm_g_2", 2, 0),
    (0, "ssm_conv_b_2", 12, 0), (0, "ssm_norm_g_2", 8, 0),
    (1, "ssm_conv_w_2", 48, 0), (1, "norm_ffn_g_2", 8, 0), (1, "ffn_conv_b_2", 44, 0),
    (2, "ffn_conv_w", 88, 0), (3, "ffn_conv_w", 44, 88), (3, "ffn_conv_w_2", 44, 0), (4, "ffn_conv_w_2", 88, 44),
]


def param_columns():
    col, used = {}, [0] * 5
    for tile, name, rows, first in PARAM_ROWS:
        col[name, first] = tile * P + used[tile]
        used[tile] += rows
    return col, used


PCOL, PUSED = param_columns()


def pc(name, first=0):
    return PCOL[name, first]


FFN_TAP = {
    1: [pc("ffn_conv_w"), pc("ffn_conv_w") + 44, pc("ffn_conv_w", 88)],
    2: [pc("ffn_conv_w_2"), pc("ffn_conv_w_2", 44), pc("ffn_conv_w_2", 44) + 44],
}

STAGES = [
    ("proj1", 12, 24), ("wout1", 4, 8), ("up1", 22, 44), ("down1", 12, 8), ("pleproj", 1, 8), ("plegate", 4, 8),
    ("xbc", 6, 12), ("z", 4, 8), ("small", 1, 1), ("foxqk", 4, 8), ("foxv", 2, 8), ("mlac", 3, 5),
    ("mlahead", 4, 0), ("merge", 20, 48), ("wout2", 4, 8), ("up2", 22, 44), ("down2", 12, 8),
]


def stage_bases():
    tile, chunk, t, c = {}, {}, 0, 0
    for name, tiles, chunks in STAGES:
        tile[name], chunk[name] = t, c
        t, c = t + tiles, c + chunks
    return tile, chunk, t


TILE0, CHUNK0, N_TILES = stage_bases()
TILES = {name: tiles for name, tiles, _ in STAGES}
PER_LOAD = 32
DOWN_PARTS = ((0, 8), (8, 8), (16, 6))
SUFFIX = {1: "", 2: "_2"}

LEVELS = 7


def counted(names):
    return {n: i + 1 for i, n in enumerate(names.split())}


SMALL_W = 80
SS_DVE = counted("v dl packed tok xdw0 h0 yt0 ysum0 y0 xdw1 h1 yt1 ysum1 y1")
SS_ACT = counted("raw silu e pexp dec bt0 bt1")
SS_PE = counted("tok turned0 states0 yoff0 yturned0 turned1 states1 yoff1 yturned1")
MP_ACT = counted("krope trig")
MP_DVE = counted("swaps angles krot")
MP_PE = counted("kswap")
MH_PE = counted("heads ms0 ms1")
MH_ACT = counted("raw r0 r1")
MH_DVE = counted("qk0 qk1")
TWO_PI = 2 * np.pi
TWO_PI_PARTS = [6.28125, 0.0019340515136718750, 1.255665914e-06]
PI_BELOW = 3.1415925
ROUNDING = 12582912.0


def inv_freq():
    inv = (1.0 / (np.float32(10000.0) ** (np.arange(0, ROPE, 2, dtype=np.float32) / np.float32(ROPE)))).astype(np.float32)
    return np.ascontiguousarray(np.concatenate([inv, inv])[:, None])
SMALL_LOADS = 16 * 16


NORMS = [("mix1", 8), ("ffn1", 8), ("final", 8), ("mix2", 8), ("ssm", 8), ("mlaq", 3), ("mlakv", 2), ("ffn2", 8)]
NORM_USE = {name: i for i, (name, _) in enumerate(NORMS)}
NORM_N = dict(NORMS)
LO_BEFORE = {name: sum(n for m, n in NORMS[:i] if m != "final") for i, (name, _) in enumerate(NORMS)}
NORM_BASE = {name: sum(n for _, n in NORMS[:i]) for i, (name, _) in enumerate(NORMS)}
X_IN, X_WOUT1, X_DOWN1, X_PLE, X_WOUT2, X_DOWN2 = 0, 8, 16, 24, 32, 40

RG_DVE = counted("u b2 recurrence gated")
RG_ACT = counted("sigmoids exps beta gelus")
RG_PE = counted("r_gate i_gate")
HG_ACT = counted("q_sigmoid logf e0 e1 e2 e3 e4 e5 e6 decays v_turned out")
HG_DVE = counted("qk d0 d1 m0 d2 m1 c0 d3 m2 c1 d4 m3 c2 d5 m4 c3 d6 m5 c4 m6 c5 dk c6 gated c7 state")
HG_PE = counted("g0 g1 g2 g3 g4 g5 g6 g7 turned states out")


def build(nc, dram, out):
    ctx = ExitStack()
    with ctx:
        def sem(name):
            return ctx.enter_context(nc.semaphore(name))

        base = -(-nc.sbuf_base // 64) * 64
        place = {"at": base}

        def fixed(name, shape, dt=F32):
            words = int(np.prod(shape[1:]))
            t = nc.alloc_sbuf_tensor_at(name, shape, dt, offset=place["at"])
            place["at"] += -(-words * 4 // 64) * 64
            return t

        X = fixed("X", [P, KD, S])
        WRAW = fixed("WRAW", [P, 2, WT])
        WHI = fixed("WHI", [P, 2, WT], F32R)
        WLO = fixed("WLO", [P, 2, WT], F32R)
        HHI = fixed("HHI", [P, KD, S], F32R)
        HLO = fixed("HLO", [P, KD, S], F32R)
        IDENT = fixed("IDENT", [P, P])
        ONES = fixed("ONES", [P, P])
        gb_at = place["at"]
        BONES = fixed("BONES", [P, P])
        TRI = fixed("TRI", [P, P])
        CAUSAL = fixed("CAUSAL", [P, P])
        CHUNKED = fixed("CHUNKED", [P, P])
        RESET = fixed("RESET", [P, S])
        PRM = fixed("PRM", [P, 5 * P])
        EPSC = fixed("EPSC", [P, 1])
        CNEG = fixed("CNEG", [P, 2, RG])
        LOWB = fixed("LOWB", [P, 2, HG])
        SOFT = fixed("SOFT", [P, 4, RG])
        QKG = fixed("QKG", [P, 4])
        DSKIP = fixed("DSKIP", [P, KD])
        SMB = fixed("SMB", [P, 3])
        INVF = fixed("INVF", [P, 1])
        r_at = place["at"]
        R = fixed("R", [P, S])
        LNT = fixed("LNT", [P, S])
        arena = place["at"]

        def at(name, kb, shape, dt=F32):
            return nc.alloc_sbuf_tensor_at(name, shape, dt, offset=arena + int(kb * 1024))

        NRM = at("NRM", 0, [P, KD, S])
        PROWS = at("PROWS", 16, [P, 5, P])
        XTOK = at("XTOK", 20, [P, NT, D])
        Z = at("Z", 0, [P, N_PROJ, S])
        YP = at("YP", 48, [P, KD, S])
        HMASK = at("HMASK", 64, [P, LEVELS + 1, P], I32)
        WR = at("WR", 68, [P, RG, P])
        WI = at("WI", 69.5, [P, RG, P])
        RR = at("RR", 71, [P, RG, S])
        IG = at("IG", 77, [P, RG, S])
        TH = at("TH", 83, [P, RG, S])
        AD = at("AD", 89, [P, RG, S])
        MSCR = at("MSCR", 71, [P, 10, P])
        MSCRI = at("MSCRI", 77, [P, 2, P], I32)
        HQ = at("HQ", 71, [P, S])
        HK = at("HK", 73, [P, S])
        HG_ = at("HG_", 75, [P, S])
        HDD = at("HDD", 77, [P, 2, S])
        HM = at("HM", 81, [P, 2, S])
        HST = at("HST", 85, [P, 2, S])
        HVT = at("HVT", 89, [P, NT, P])
        HKD = at("HKD", 91, [P, S])
        HKDT = at("HKDT", 93, [P, NT, P])
        HQG = at("HQG", 95, [P, S])
        HVS = at("HVS", 97, [P, S])
        HS = at("HS", 0, [P, 3, P])
        HEGL = at("HEGL", 1.5, [P, NT])
        SQ1 = at("SQ1", 0, [P, KD, S])
        FHI = at("FHI", 0, [P, NF, S], F32R)
        FLO = at("FLO", 44, [P, NF, S], F32R)
        FG = at("FG", 88, [P, 2, S])
        FU = at("FU", 92, [P, 2, S])
        PTOK = at("PTOK", 92, [P, NT, PLE])
        PHI = at("PHI", 16, [P, 2, S], F32R)
        PLO = at("PLO", 20, [P, 2, S], F32R)
        PP = at("PP", 24, [P, KD, S])
        PG = at("PG", 40, [P, 2, S])
        OTOK = at("OTOK", 16, [P, NT, D])

        YSHI = at("YSHI", 0, [P, KD, S], F32R)
        YSLO = at("YSLO", 16, [P, KD, S], F32R)
        XD = at("XD", 0, [P, NT, S])
        XW = at("XW", 8, [P, NT, S])
        SH = at("SH", 16, [P, 3, S])
        YT = at("YT", 22, [P, NT, S])
        SMT = at("SMT", 0, [P, 5, S])
        XBC = at("XBC", 32, [P, NXBC, S])
        ZS = at("ZS", 56, [P, KD, S])
        CBM = at("CBM", 72, [P, S])
        BT = at("BT", 74, [P, NT, P])
        ABC = at("ABC", 76, [P, 2, S])
        DM = at("DM", 80, [P, 2, S])
        TOK = at("TOK", 84, [P, NT, P])
        PACK = at("PACK", 86, [P, S])
        DEC = at("DEC", 88, [P, HEADS, NT])
        SMC = at("SMC", 90, [P, S])
        CUM = at("CUM", 92, [P, S])
        NS = at("NS", 72, [P, KD, S])
        YFHI = at("YFHI", 0, [P, 4, S], F32R)
        YFLO = at("YFLO", 8, [P, 4, S], F32R)
        CQHI = at("CQHI", 16, [P, 5, S], F32R)
        CQLO = at("CQLO", 26, [P, 5, S], F32R)
        YMHI = at("YMHI", 16, [P, 4, S], F32R)
        YMLO = at("YMLO", 24, [P, 4, S], F32R)
        QKR = at("QKR", 32, [P, 8, S])
        CR = at("CR", 36, [P, 5, S])
        KRR = at("KRR", 46, [P, S])
        QS = at("QS", 48, [P, 2, S])
        KS = at("KS", 52, [P, 2, S])
        PR = at("PR", 56, [P, 2, S])
        PT = at("PT", 60, [P, 2, S])
        ANG = at("ANG", 56, [P, 4, S])
        OH = at("OH", 64, [P, NT, S])
        VF = at("VF", 72, [P, NT, S])
        SQF = at("SQF", 80, [P, 2, S])
        NC = at("NC", 84, [P, 3, S])
        VM = at("VM", 72, [P, NT, P])
        CG = at("CG", 74, [P, S])
        KROT = at("KROT", 76, [P, S])
        SIN = at("SIN", 78, [P, S])
        SQM = at("SQM", 80, [P, 4, S])
        QR = at("QR", 88, [P, 2, S])
        MR = at("MR", 92, [P, S])
        POSI = at("POSI", 94, [P, S], I32)
        SW = at("SW", 96, [P, 2, ROPE])
        NMX = at("NMX", 96.5, [P, 3, 8])
        RS2 = nc.alloc_sbuf_tensor_at("RS2", [P, 2, S], F32, offset=r_at)
        YS2HI = at("YS2HI", 32, [P, KD, S], F32R)
        YS2LO = at("YS2LO", 48, [P, KD, S], F32R)
        MGHI = at("MGHI", 64, [P, KD, S], F32R)
        MGLO = at("MGLO", 80, [P, KD, S], F32R)
        GA = nc.alloc_sbuf_tensor_at("GA", [P, 2, S], F32, offset=r_at)
        GB = nc.alloc_sbuf_tensor_at("GB", [P, 2, S], F32, offset=gb_at)

        acum_d = nc.dram_tensor("acum_d", (HEADS, S), F32).ap()
        alast_d = nc.dram_tensor("alast_d", (HEADS, NT), F32).ap()
        fsum_d = nc.dram_tensor("fsum_d", (2, 8, S), F32).ap()
        yshi_d = nc.dram_tensor("yshi_d", (P, KD, S), F32R).ap()
        yslo_d = nc.dram_tensor("yslo_d", (P, KD, S), F32R).ap()

        x_acc, s_signs = sem("x_acc"), sem("s_signs")
        ss_dve, ss_act, ss_pe = sem("ss_dve"), sem("ss_act"), sem("ss_pe")
        s_rows, s_dec, s_spill, s_pos = sem("s_rows"), sem("s_dec"), sem("s_spill"), sem("s_pos")
        s_abc = [sem("s_abc0"), sem("s_abc1")]
        h_dfree, h_d, h_e, h_m, h_y = (sem(f"h_{x}") for x in "dfree d e m y".split())
        a_s, a_mx, a_exp, a_t, a_pt, a_pv, a_o, a_qk = (
            sem(x) for x in "a_s a_mx a_exp a_t a_pt a_pv a_o a_qk".split())
        q_sq, q_ms, q_r, s_frow, q_rowfree, v_out = (sem(x) for x in "q_sq q_ms q_r s_frow q_rowfree v_out".split())
        o_t, o_hi, o_lo = sem("o_t"), sem("o_hi"), sem("o_lo")
        mp_act, mp_dve, mp_pe = sem("mp_act"), sem("mp_dve"), sem("mp_pe")
        mh_act, mh_dve, mh_pe = sem("mh_act"), sem("mh_dve"), sem("mh_pe")
        g_sig, g_mid, g_sum, g_hi, g_lo = (sem(f"g_{x}") for x in "sig mid sum hi lo".split())
        s_oa = sem("s_oa")
        s_reload, s_fcols = sem("s_reload"), sem("s_fcols")

        PS = ctx.enter_context(nc.psum_tensor("PS", [P, 8, S], F32))

        s_raw = [sem("s_raw0"), sem("s_raw1")]
        s_hi, s_lo, s_started = sem("s_hi"), sem("s_lo"), sem("s_started")
        s_chunk, s_bank_free = sem("s_chunk"), sem("s_bank_free")
        n_sq, n_ms, n_r, n_h, n_hi, n_lo = (sem(f"n_{x}") for x in "sq ms r h hi lo".split())
        s_x = sem("s_x")
        s_const, s_mask, s_zeroed, s_params, s_pt, s_ptc, s_setup_a, s_setup_v = (
            sem(x) for x in "s_const s_mask s_zeroed s_params s_pt s_ptc s_setup_a s_setup_v".split())
        s_xin, s_xt, s_small = sem("s_xin"), sem("s_xt"), sem("s_small")
        rg_dve, rg_act, rg_pe = sem("rg_dve"), sem("rg_act"), sem("rg_pe")
        sc_done = sem("sc_done")
        hg_act, hg_dve, hg_pe = sem("hg_act"), sem("hg_dve"), sem("hg_pe")
        hn_sq, hn_ps, hn_r, hn_g, hn_y, hn_hi, hn_lo = (sem(f"hn_{x}") for x in "sq ps r g y hi lo".split())
        f_acc, f_tap, f_silu, f_prod, f_hi, f_lo = (sem(f"f_{x}") for x in "acc tap silu prod hi lo".split())
        e_hi, e_lo, e_p, e_pt, e_phi, e_plo, e_pp, e_g = (
            sem(f"e_{x}") for x in "hi lo p pt phi plo pp g".split())
        s_ot, s_oc, s_out = sem("s_ot"), sem("s_oc"), sem("s_out")

        def f32(t):
            return t.bitcast(F32)

        def wtile(tensor, slot, kts, cols, offset=0):
            return tensor[:, slot, offset:offset + kts * cols].rearrange("p (k n) -> p k n", n=cols)

        def rows(w):
            return w.rearrange("o (k p) n -> p (o k) n", p=P)

        block = ctx.enter_context(nc.Block())

        @block.sync
        def _(sp):
            def load(t, slot, kts, cols, src):
                if not isinstance(t, int) or t >= 2:
                    sp.wait_ge(s_lo, t - 1)
                half = kts // 2
                for k in (slice(0, half), slice(half, kts)):
                    sp.dma_start(wtile(WRAW, slot, kts, cols)[:, k, :], src[:, k, :]).then_inc(s_raw[slot], 16)

            def columns(name, w, at=0, skip=0):
                t0 = TILE0[name]
                with sp.Fori(skip // 2, TILES[name] // 2) as i:
                    for j in range(2):
                        col = sp.snap(i * 512 + (at + j * 256))
                        load(i * 2 + (t0 + j), (t0 + j) % 2, KD, 256, w[:, :, bass.ds(col, 256)])

            def ffn(n):
                up, down = rows(dram["ffn_w_up" + SUFFIX[n]]), rows(dram["ffn_w_down" + SUFFIX[n]])
                t0 = TILE0[f"up{n}"]
                with sp.Fori(0, NF // 2) as i:
                    for j in range(2):
                        col = sp.snap(i * 256 + j * DFF)
                        load(i * 2 + (t0 + j), (t0 + j) % 2, KD, 256, up[:, :, bass.ds(col, 256)])
                t0 = TILE0[f"down{n}"]
                with sp.Fori(0, 2) as i:
                    for half in range(2):
                        for part, (k0, kts) in enumerate(DOWN_PARTS):
                            j = 3 * half + part
                            col = sp.snap(i * 512 + half * 256)
                            load(i * 6 + (t0 + j), (t0 + j) % 2, kts, 256, down[:, k0:k0 + kts, bass.ds(col, 256)])

            for tile, name, n, first in PARAM_ROWS:
                a = dram[name]
                form, sizes = {1: "(r p) -> r p", 2: "o (c p) -> (o c) p", 3: "o k (c p) -> (o k c) p"}[len(a.shape)], {"p": P}
                if name in ("rg_b_r", "rg_b_i"):
                    form, sizes = "o (c a) d -> (o c) (a d)", {"a": 2}
                row = pc(name, first) - tile * P
                sp.dma_start(PROWS[row:row + n, tile, :], a.rearrange(form, **sizes)[first:first + n, :]
                             ).then_inc(s_params, 16)
            for q in range(NT):
                sp.dma_start(XTOK[:, q, :], dram["x"][0, q * P:(q + 1) * P, :]).then_inc(s_xin, 16)
            w_in = rows(dram["w_in"])
            sp.wait_ge(s_zeroed, 1)
            for t in range(2):
                load(t, t, KD, 256, w_in[:, :, t * 256:(t + 1) * 256])
            for h in range(2):
                for to, name in ((WR, "rg_w_r"), (WI, "rg_w_i")):
                    sp.dma_start(to[h * HD:(h + 1) * HD, :, h * HD:(h + 1) * HD],
                                 dram[name].rearrange("o (c a) d e -> a d (o c) e", a=2)[h]).then_inc(s_small, 16)
            sp.wait_ge(s_signs, 1)
            one_column = "o d -> d o"
            for to, name in ((SMB[32:40, 0:1], "fox_b_f_2"), (SMB[64:80, 0:1], "ssm_dt_bias_2"), (SMB[64:80, 2:3], "ssm_A_log_2"),
                             (QKG[0:64, 0:1], "fox_q_gain_2"), (QKG[64:128, 0:1], "fox_q_gain_2"),
                             (QKG[0:64, 1:2], "fox_k_gain_2"), (QKG[64:128, 1:2], "fox_k_gain_2"),
                             (QKG[0:QK, 2:3], "mla_q_gain_2"), (QKG[0:QK, 3:4], "mla_k_gain_2")):
                sp.dma_start(to, dram[name].rearrange(one_column)).then_inc(s_small, 16)
            for h in range(2):
                with nc.allow_non_contiguous_dma("16 words in all"):
                    sp.dma_start(DSKIP[h * HD:(h + 1) * HD, :],
                                 dram["ssm_D_2"].rearrange("o (c h) -> h o c", h=2)[h].broadcast_to([HD, KD])
                                 ).then_inc(s_small, 16)
            sp.dma_start(INVF[NOPE:QK, :], dram["inv_freq"]).then_inc(s_small, 16)
            columns("proj1", w_in, skip=2)
            columns("wout1", rows(dram["w_out"]))
            ffn(1)
            for q in range(NT):
                sp.dma_start(PTOK[:, q, :], dram["p"][0, 0, q * P:(q + 1) * P, :]).then_inc(e_p, 16)
            t = TILE0["pleproj"]
            load(t, t % 2, 2, D, rows(dram["ple_w_proj"]))
            columns("plegate", rows(dram["ple_w_gate"]))
            w_in2 = rows(dram["w_in_2"])
            columns("xbc", w_in2, at=COL_XBC)
            columns("z", w_in2, at=COL_Z)
            t = TILE0["small"]
            sp.wait_ge(s_lo, t - 1)
            small = wtile(WRAW, t % 2, KD, SMALL_W)
            sp.dma_start(small[:, :, ROPE:64], w_in2[:, :, COL_F:COL_F + 32]).then_inc(s_fcols, 16)
            sp.wait_ge(s_fcols, 16)
            sp.dma_start(small[:, :, 0:ROPE], w_in2[:, :, COL_KROPE:COL_KROPE + ROPE]).then_inc(s_raw[t % 2], 16)
            sp.dma_start(small[:, :, 64:80], w_in2[:, :, COL_DT:COL_DT + 16]).then_inc(s_raw[t % 2], 16)
            columns("foxqk", w_in2, at=COL_FOX)
            columns("foxv", w_in2, at=COL_FOX + 2 * FOX)
            t = TILE0["mlac"]
            for j, width in enumerate((256, 256, 128)):
                load(t + j, (t + j) % 2, KD, width, w_in2[:, :, j * 256:j * 256 + width])
            uq, ukv = rows(dram["mla_w_uq_2"]), rows(dram["mla_w_ukv_2"])
            t0 = TILE0["mlahead"]
            with sp.Fori(0, 2) as i:
                for j in range(2):
                    t, slot = i * 2 + (t0 + j), (t0 + j) % 2
                    q_col, kv_col = sp.snap(i * 384 + j * 192), sp.snap(i * 512 + j * 256)
                    t_free = sp.snap(t - 1)
                    sp.wait_ge(s_lo, t_free)
                    sp.dma_start(wtile(WRAW, slot, 3, 192), uq[:, :, bass.ds(q_col, 192)]).then_inc(s_raw[slot], 16)
                    sp.dma_start(wtile(WRAW, slot, 2, 256, offset=576), ukv[:, :, bass.ds(kv_col, 256)]
                                 ).then_inc(s_raw[slot], 16)
            br_mla, br_fox, br_ssm = (rows(dram[f"w_br_{n}_2"]) for n in ("mla", "fox", "ssm"))
            t0 = TILE0["merge"]
            with sp.Fori(1, 3) as i:
                for pair in range(2):
                    col = sp.snap(i * 512 + (pair * 256 - 512))
                    for j, b in ((0, 0), (1, 1), (2, None), (3, 2), (4, None)):
                        n = t0 + 5 * pair + j
                        t, slot = i * 10 + (n - 10), n % 2
                        if b is not None:
                            gate_col = sp.snap(i * 512 + (COL_GATE + b * D + pair * 256 - 512))
                            load(t, slot, KD, 256, w_in2[:, :, bass.ds(gate_col, 256)])
                        elif j == 4:
                            load(t, slot, KD, 256, br_ssm[:, :, bass.ds(col, 256)])
                        else:
                            sp.wait_ge(s_lo, t - 1)
                            for k, w in enumerate((br_mla, br_fox)):
                                sp.dma_start(wtile(WRAW, slot, 4, 256, offset=k * 1024), w[:, :, bass.ds(col, 256)]
                                             ).then_inc(s_raw[slot], 16)
            columns("wout2", rows(dram["w_out_2"]))
            ffn(2)
            for q in range(NT):
                sp.wait_ge(s_oc, q + 1)
                sp.wait_ge(s_oa, q + 1)
                sp.dma_start(out[0, q * P:(q + 1) * P, :], OTOK[:, q, :]).then_inc(s_out, 16)
            sp.wait_ge(s_out, 16 * NT)

        @block.gpsimd
        def _(pool):
            def select(t, pattern, fill, op=ALU.is_ge, cm=1, base=0):
                return pool.affine_select(out=t, in_=t, compare_op=op, fill=fill, base=base, pattern=pattern,
                                          channel_multiplier=cm)

            for t in (WRAW, WR, WI, SMB, QKG, INVF, DSKIP):
                pool.memset(t[:], 0.0)
            pool.drain().then_inc(s_zeroed, 1)
            for t, v in ((SMB[0:64, 1:3], -1.0), (SMB[64:P, 1:2], 1.0)):
                pool.memset(t, v)
                pool.drain()
            pool.drain().then_inc(s_signs, 1)
            pool.drain().then_inc(s_bank_free, 4)
            for t, v in ((IDENT, 0.0), (ONES, 1.0), (BONES, 0.0), (TRI, 1.0), (CAUSAL, 0.0), (CHUNKED, 0.0),
                         (RESET, 1.0), (EPSC, EPS)):
                pool.memset(t[:], v)
            pool.iota(MSCRI[:, 0, :], pattern=[[1, P]], base=0, channel_multiplier=0)
            pool.iota(MSCRI[:, 1, :], pattern=[[0, P]], base=0, channel_multiplier=1)
            pool.drain()
            select(IDENT[:], [[-1, P]], 1.0, op=ALU.not_equal)
            select(TRI[:], [[1, P]], 0.0, cm=-1)
            select(CAUSAL[:], [[-1, P]], NEG)
            for t, v in ((CHUNKED[0:HD, HD:P], NEG), (BONES[0:HD, 0:HD], 1.0), (BONES[HD:P, HD:P], 1.0)):
                pool.drain()
                pool.memset(t, v)
            pool.drain()
            for q in range(NT):
                pool.memset(RESET[:, q * P:q * P + 1], 0.0)
            pool.drain().then_inc(s_const, 1)
            pool.wait_ge(s_mask, 1)
            select(MSCR[:, 9, :], [[1, P]], 4096.0, cm=-1).then_inc(s_mask, 1)

            pool.wait_ge(e_pt, 1)
            pool.dma_start(POSI[NOPE:QK, :], dram["positions_2"].broadcast_to([ROPE, S])).then_inc(s_pos, 16)
            pool.wait_ge(ss_dve, SS_DVE["dl"])
            pool.dma_start(acum_d, CUM[64:80, :]).then_inc(s_rows, 16)
            with nc.allow_non_contiguous_dma("64 words"):
                pool.dma_start(alast_d, CUM[64:80, P - 1:S:P]).then_inc(s_rows, 16)
            pool.dma_start(fsum_d[0], CUM[32:40, :]).then_inc(s_rows, 16)
            pool.dma_start(fsum_d[1], SMT[32:40, 4, :]).then_inc(s_rows, 16)
            pool.wait_ge(s_rows, 64)
            pool.dma_start(DEC[:].rearrange("p h q -> p (h q)"),
                           alast_d.rearrange("h q -> (h q)").unsqueeze(0).broadcast_to([P, HEADS * NT])
                           ).then_inc(s_dec, 16)
            with pool.Fori(0, HEADS // 2) as i:
                for b in range(2):
                    pool.wait_ge(h_dfree, i * 2 + (b + 1))
                    pool.dma_start(ABC[:, b, :], acum_d[bass.ds(i * 2 + b, 1), :].broadcast_to([P, S])).then_inc(s_abc[b], 16)
            pool.wait_ge(n_lo, LO_BEFORE["ssm"] + KD)
            pool.dma_start(yshi_d, YSHI[:]).then_inc(s_spill, 16)
            pool.dma_start(yslo_d, YSLO[:]).then_inc(s_spill, 16)
            with pool.Fori(0, 4) as i:
                pool.wait_ge(q_rowfree, i + 1)
                pool.dma_start(QS[65:66, :, :], fsum_d[0:1, bass.ds(i * 2, 2), :]).then_inc(s_frow, 16)
                pool.dma_start(KS[64:65, :, :], fsum_d[1:2, bass.ds(i * 2, 2), :]).then_inc(s_frow, 16)
            pool.wait_ge(a_o, 64)
            pool.wait_ge(s_spill, 32)
            pool.dma_start(YS2HI[:], yshi_d).then_inc(s_reload, 16)
            pool.dma_start(YS2LO[:], yslo_d).then_inc(s_reload, 16)

        @block.scalar
        def _(act):
            def hi_at(t):
                act.wait_ge(s_raw[t % 2], PER_LOAD * (t // 2 + 1))
                if t:
                    act.wait_ge(s_started, t)
                act.activation(WHI[:, t % 2, :], WRAW[:, t % 2, :], ACT.Copy).then_inc(s_hi, 1)

            def hi_in_loop(i, per, t):
                act.wait_ge(s_raw[t % 2], i * (per // 2 * PER_LOAD) + PER_LOAD * (t // 2 + 1))
                act.wait_ge(s_started, i * per + t)
                act.activation(WHI[:, t % 2, :], WRAW[:, t % 2, :], ACT.Copy).then_inc(s_hi, 1)

            def norm(name, src, ready, scratch, width, to=None):
                use, first, n = NORM_USE[name], NORM_BASE[name], NORM_N[name]
                if first:
                    act.wait_ge(n_h, first)
                    act.wait_ge(n_lo, LO_BEFORE[name])
                for c in range(n):
                    act.wait_ge(*ready(c))
                    act.activation(scratch[:, c, :], src(c), ACT.Square).then_inc(n_sq, 1)
                act.wait_ge(n_ms, use + 1)
                act.activation(LNT[:], PS[:, 4, :], ACT.Ln, bias=EPSC[:, 0:1], scale=1.0 / width)
                act.drain()
                act.activation(R[:], LNT[:], ACT.Exp, scale=-0.5).then_inc(n_r, 1)
                if to is not None:
                    for c in range(n):
                        act.wait_ge(n_h, first + c + 1)
                        act.activation(to[:, c, :], scratch[:, c, :], ACT.Copy).then_inc(n_hi, 1)

            def evacuate(name, to, func=ACT.Copy):
                t0, c0 = TILE0[name], CHUNK0[name]
                with act.Fori(0, TILES[name] // 2) as i:
                    for j in range(2):
                        hi_in_loop(i, 2, t0 + j + 1)
                        for m in range(2):
                            c = 2 * j + m
                            bank = (c0 + c) % 4
                            act.wait_ge(s_chunk, i * 4 + (c0 + c + 1))
                            act.activation(to[:, bass.ds(i * 4 + c, 1), :], PS[:, bank:bank + 1, :], func
                                           ).then_inc(s_bank_free, 1)

            def split_ahead(name, per):
                with act.Fori(0, TILES[name] // per) as i:
                    for j in range(per):
                        hi_in_loop(i, per, TILE0[name] + j + 1)

            def ffn(n):
                t0, c0, tap, first = TILE0[f"up{n}"], CHUNK0[f"up{n}"], FFN_TAP[n][2], (n - 1) * NF
                bias = pc("ffn_conv_b_2")
                with act.Fori(0, NF // 2) as i:
                    def newest(c, acc, chunk):
                        act.wait_ge(s_chunk, i * 4 + (c0 + c + 1))
                        act.activation(acc, PS[:, (c0 + c) % 4, :], ACT.Identity,
                                       bias=PRM[:, bass.ds(chunk + bias, 1)] if n == 2 else 0.0,
                                       scale=PRM[:, bass.ds(chunk + tap, 1)]).then_inc(f_acc, 1)

                    hi_in_loop(i, 2, t0 + 1)
                    for m in range(2):
                        newest(m, FG[:, m, :], i * 2 + m)
                    hi_in_loop(i, 2, t0 + 2)
                    for m in range(2):
                        act.wait_ge(f_tap, i * 4 + (2 * first + m + 1))
                        act.activation(FG[:, m, :], FG[:, m, :], ACT.Silu).then_inc(f_silu, 1)
                    for m in range(2):
                        newest(2 + m, FU[:, m, :], i * 2 + (NF + m))
                    for m in range(2):
                        act.wait_ge(f_prod, i * 2 + (first + m + 1))
                        act.activation(FHI[:, bass.ds(i * 2 + m, 1), :], FU[:, m:m + 1, :], ACT.Copy).then_inc(f_hi, 1)
                    act.wait_ge(f_lo, i * 2 + (first + 2))
                t0 = TILE0[f"down{n}"]
                if n == 1:
                    split_ahead("down1", 6)
                else:
                    for t in range(t0 + 1, t0 + TILES["down2"]):
                        hi_at(t)

            act.wait_ge(s_const, 1)
            hi_at(0)
            act.wait_ge(s_ptc, 5)
            act.activation(SOFT[:, 0, :], PRM[:, pc("rg_lambda"):pc("rg_lambda") + RG], ACT.Abs)
            act.drain()
            act.activation(SOFT[:, 0, :], SOFT[:, 0, :], ACT.Exp, scale=-1.0).then_inc(s_setup_a, 1)
            act.wait_ge(s_setup_v, 1)
            act.activation(LOWB[:, 0, :], LOWB[:, 1, :], ACT.Exp).then_inc(s_setup_a, 1)

            norm("mix1", lambda c: X[:, c, :], lambda c: (s_x, X_IN + c + 1), NRM, D, HHI)
            act.wait_ge(n_lo, KD)
            evacuate("proj1", Z)

            act.wait_ge(rg_pe, RG_PE["r_gate"])
            for c in range(RG):
                act.activation(RR[:, c, :], PS[:, 4 + c, :], ACT.Sigmoid, bias=PRM[:, pc("rg_b_r") + c:pc("rg_b_r") + c + 1])
            act.wait_ge(rg_pe, RG_PE["i_gate"])
            for c, bank in zip(range(RG), (7, 0, 1)):
                last = act.activation(IG[:, c, :], PS[:, bank, :], ACT.Sigmoid,
                                      bias=PRM[:, pc("rg_b_i") + c:pc("rg_b_i") + c + 1])
            last.then_inc(rg_act, 1)
            act.drain()
            for c in range(RG):
                act.activation(TH[:, c, :], RR[:, c, :], ACT.Tanh, scale=CNEG[:, 0, c:c + 1])
                act.activation(AD[:, c, :], RR[:, c, :], ACT.Exp, scale=CNEG[:, 0, c:c + 1])
                last = act.activation(Z[:, A_U + c, :], RR[:, c, :], ACT.Exp, scale=CNEG[:, 1, c:c + 1])
            last.then_inc(rg_act, 1)
            act.wait_ge(rg_dve, RG_DVE["b2"])
            act.activation(TH[:], TH[:], ACT.Sqrt, scale=-1.0).then_inc(rg_act, 1)
            act.activation(Z[:, A_GATE:A_GATE + RG, :], Z[:, A_GATE:A_GATE + RG, :], ACT.Gelu_apprx_tanh
                           ).then_inc(rg_act, 1)

            act.wait_ge(rg_dve, RG_DVE["gated"])
            with act.Fori(0, HG) as i:
                def dve(name):
                    act.wait_ge(hg_dve, i * len(HG_DVE) + HG_DVE[name])

                def pe(name):
                    act.wait_ge(hg_pe, i * len(HG_PE) + HG_PE[name])

                act.activation(HG_[:], Z[:, bass.ds(i + B_F, 1), :], ACT.Sigmoid)
                act.activation(HQ[:], Z[:, bass.ds(i + B_Q, 1), :], ACT.Silu)
                act.activation(HVS[:], Z[:, bass.ds(i + B_V, 1), :], ACT.Copy).then_inc(hg_act, 1)
                dve("qk")
                act.activation(HG_[:], HG_[:], ACT.Ln).then_inc(hg_act, 1)
                for b in range(LEVELS):
                    dve(f"d{b}")
                    act.activation(HDD[:, b % 2, :], HDD[:, b % 2, :], ACT.Exp).then_inc(hg_act, 1)
                dve("dk")
                act.activation(HKD[:], HKD[:], ACT.Exp)
                act.activation(HQG[:], HG_[:], ACT.Exp)
                act.activation(HEGL[:], HG_[:, P - 1:S:P], ACT.Exp).then_inc(hg_act, 1)
                pe("turned")
                act.activation(HVT[:], PS[:, 0, :].rearrange("p (q n) -> p q n", n=P), ACT.Copy)
                act.activation(HKDT[:], PS[:, 1, :].rearrange("p (q n) -> p q n", n=P), ACT.Copy
                               ).then_inc(hg_act, 1)
                pe("out")
                act.activation(YP[:, bass.ds(i + RG, 1), :], PS[:, 3:4, :], ACT.Copy).then_inc(hg_act, 1)

            act.activation(Z[:, B_G:B_G + HG, :], Z[:, B_G:B_G + HG, :], ACT.Silu).then_inc(hn_g, 1)
            act.wait_ge(sc_done, 1)
            act.drain()
            act.activation(SQ1[:], YP[:], ACT.Square).then_inc(hn_sq, 1)
            for half in range(2):
                four = slice(4 * half, 4 * half + 4)
                act.wait_ge(hn_ps, half + 1)
                act.activation(SQ1[:, four, :], PS[:, 4:8, :], ACT.Ln, bias=EPSC[:, 0:1], scale=1.0 / HD)
                act.drain()
                act.activation(SQ1[:, four, :], SQ1[:, four, :], ACT.Exp, scale=-0.5).then_inc(hn_r, 1)
            for c in range(KD):
                act.wait_ge(hn_y, c + 1)
                act.activation(HHI[:, c, :], YP[:, c, :], ACT.Copy).then_inc(hn_hi, 1)

            split_ahead("wout1", 2)
            norm("ffn1", lambda c: X[:, c, :], lambda c: (s_x, X_WOUT1 + c + 1), NRM, D, HHI)
            ffn(1)

            for c in range(KD):
                act.wait_ge(s_x, X_DOWN1 + c + 1)
                act.activation(HHI[:, c, :], X[:, c, :], ACT.Copy).then_inc(e_hi, 1)
            act.wait_ge(e_pt, 1)
            act.activation(PHI[:], PS[:, 6:8, :], ACT.Copy).then_inc(e_phi, 1)
            t0, c0 = TILE0["pleproj"], CHUNK0["pleproj"]
            hi_at(t0 + 1)
            for c in range(KD):
                act.wait_ge(s_chunk, c0 + c + 1)
                act.activation(PP[:, c, :], PS[:, (c0 + c) % 4, :], ACT.Copy).then_inc(s_bank_free, 1)
            act.drain().then_inc(e_pp, 1)
            t0, c0 = TILE0["plegate"], CHUNK0["plegate"]
            for c in range(KD):
                if c % 2 == 0:
                    hi_at(t0 + c // 2 + 1)
                act.wait_ge(s_chunk, c0 + c + 1)
                if c >= 2:
                    act.wait_ge(s_x, X_PLE + c - 1)
                act.activation(PG[:, c % 2, :], PS[:, (c0 + c) % 4, :], ACT.Sigmoid).then_inc(s_bank_free, 1)
                act.drain().then_inc(e_g, 1)
            norm("final", lambda c: X[:, c, :], lambda c: (s_x, X_PLE + c + 1), NRM, D)
            norm("mix2", lambda c: X[:, c, :], lambda c: (n_h, NORM_BASE["mix2"]), NRM, D, HHI)
            t0, c0 = TILE0["xbc"], CHUNK0["xbc"]
            w, b = pc("ssm_conv_w_2") + 3 * NXBC, pc("ssm_conv_b_2")
            with act.Fori(0, 3) as i:
                for j in range(2):
                    hi_in_loop(i, 2, t0 + j + 1)
                    for m in range(2):
                        c = 2 * j + m
                        bank = (c0 + c) % 4
                        act.wait_ge(s_chunk, i * 4 + (c0 + c + 1))
                        act.activation(XBC[:, bass.ds(i * 4 + c, 1), :], PS[:, bank:bank + 1, :], ACT.Identity,
                                       bias=PRM[:, bass.ds(i * 4 + (b + c), 1)], scale=PRM[:, bass.ds(i * 4 + (w + c), 1)]
                                       ).then_inc(x_acc, 1)
            evacuate("z", ZS, ACT.Silu)
            t, c = TILE0["small"], CHUNK0["small"]
            hi_at(t + 1)
            act.wait_ge(s_bank_free, 4 + c)
            act.activation(XBC[:], XBC[:], ACT.Silu)
            act.wait_ge(s_chunk, c + 1)
            act.activation(SMC[0:SMALL_W, :], PS[0:SMALL_W, c % 4, :], ACT.Copy).then_inc(s_bank_free, 1)
            act.drain().then_inc(ss_act, 2)

            act.wait_ge(ss_dve, SS_DVE["v"])
            act.activation(SMT[0:SMALL_W, 1, :], SMT[0:SMALL_W, 0, :], ACT.Abs)
            act.drain()
            act.activation(SMT[0:SMALL_W, 1, :], SMT[0:SMALL_W, 1, :], ACT.Exp, scale=-1.0)
            act.activation(SMB[64:80, 2:3], SMB[64:80, 2:3], ACT.Exp)
            act.drain().then_inc(ss_act, 1)
            act.wait_ge(ss_dve, SS_DVE["dl"])
            act.activation(SMT[64:80, 3, :], SMT[64:80, 3, :], ACT.Exp)
            act.activation(PACK[96:112, :], CUM[64:80, :], ACT.Exp)
            act.drain().then_inc(ss_act, 1)
            act.wait_ge(s_dec, 16)
            act.activation(DEC[:], DEC[:], ACT.Exp)
            act.drain().then_inc(ss_act, 1)
            for g in range(2):
                act.wait_ge(ss_pe, SS_PE[f"turned{g}"])
                act.activation(BT[:], PS[:, 1, :].rearrange("p (q n) -> p q n", n=P), ACT.Copy).then_inc(ss_act, 1)
                with act.Fori(0, 4) as i:
                    for b in range(2):
                        act.wait_ge(h_d, i * 2 + (8 * g + b + 1))
                        act.activation(DM[:, b, :], DM[:, b, :], ACT.Exp).then_inc(h_e, 1)
            norm("ssm", lambda c: XBC[:, c, :], lambda c: (ss_dve, SS_DVE["y1"]), NS, SSM, YSHI)

            def attention(at):
                def out_of_bank(u):
                    nk = (u % 4 + 1) * P
                    act.wait_ge(a_t, at(u + 1))
                    if u >= 2:
                        act.wait_ge(a_pv, at(u - 1))
                    act.activation(PT[:, u % 2, 0:nk], PS[:, 4 + u % 2, 0:nk], ACT.Copy).then_inc(a_pt, 1)

                for u in range(8):
                    nk = (u % 4 + 1) * P
                    act.wait_ge(a_mx, at(u + 1))
                    if u >= 2:
                        act.wait_ge(a_t, at(u - 1))
                    act.activation(PR[:, u % 2, 0:nk], PS[:, u % 4, 0:nk], ACT.Exp, bias=NMX[:, 0, u:u + 1],
                                   accum_out=NMX[:, 1, u:u + 1]).then_inc(a_exp, 1)
                    if u:
                        out_of_bank(u - 1)
                out_of_bank(7)
                act.wait_ge(a_o, at(8))

            def heads_out(hi, first):
                for c in range(4):
                    act.wait_ge(o_t, first + c + 1)
                    act.activation(hi[:, c, :], PS[:, 4 + c, :], ACT.Copy).then_inc(o_hi, 1)
                act.wait_ge(o_lo, first + 4)

            evacuate("foxqk", QKR)
            t0, c0 = TILE0["foxv"], CHUNK0["foxv"]
            for half in range(2):
                hi_at(t0 + half + 1)
                for tc in range(NT):
                    c = c0 + 4 * half + tc
                    act.wait_ge(s_chunk, c + 1)
                    act.activation(VF[:, tc, half * 256:(half + 1) * 256], PS[:, c % 4, 0:256], ACT.Copy
                                   ).then_inc(s_bank_free, 1)
            act.drain().then_inc(v_out, 1)
            with act.Fori(0, 4) as i:
                for b in range(2):
                    act.activation(SQF[:, b:b + 1, :], QKR[:, bass.ds(i + 4 * b, 1), :], ACT.Square).then_inc(q_sq, 1)
                act.wait_ge(q_ms, i + 1)
                act.activation(RS2[:], PS[:, 4:6, :], ACT.Ln, bias=EPSC[:, 0:1], scale=1.0 / HD)
                act.drain()
                act.activation(RS2[:], RS2[:], ACT.Exp, scale=-0.5).then_inc(q_r, 1)
                attention(lambda k: i * 8 + k)
            act.wait_ge(s_spill, 32)
            heads_out(YFHI, 0)

            t0, c0 = TILE0["mlac"], CHUNK0["mlac"]
            for c in range(5):
                if c % 2 == 0:
                    hi_at(t0 + c // 2 + 1)
                act.wait_ge(s_chunk, c0 + c + 1)
                act.activation(CR[:, c, :], PS[:, (c0 + c) % 4, :], ACT.Copy).then_inc(s_bank_free, 1)
            act.drain()
            norm("mlaq", lambda c: CR[:, c, :], lambda c: (s_chunk, c0 + 5), NC, MLA_Q, CQHI)
            norm("mlakv", lambda c: CR[:, 3 + c, :], lambda c: (s_chunk, c0 + 5), NC, MLA_KV, CQHI[:, 3:5, :])
            act.wait_ge(n_lo, LO_BEFORE["ffn2"])
            act.activation(KRR[NOPE:QK, :], SMC[0:ROPE, :], ACT.Copy)
            act.drain().then_inc(mp_act, 1)
            for hh in range(2):
                act.activation(SQM[NOPE:QK, 2 * hh + 1, :], KRR[NOPE:QK, :], ACT.Square)
            act.wait_ge(mp_dve, MP_DVE["angles"])
            act.activation(SIN[NOPE:QK, :], ANG[NOPE:QK, 0, :], ACT.Sin)
            act.activation(ANG[NOPE:QK, 1, :], ANG[NOPE:QK, 1, :], ACT.Sin)
            act.drain().then_inc(mp_act, 1)
            t0 = TILE0["mlahead"]
            with act.Fori(0, 2) as i:
                for j in range(2):
                    def at(k, n=8):
                        return i * (2 * n) + (n * j + k)

                    hi_in_loop(i, 2, t0 + j + 1)
                    act.wait_ge(mh_pe, at(MH_PE["heads"], 3))
                    for hh in range(2):
                        act.activation(SQM[0:QK, 2 * hh, :], PS[0:QK, 2 * hh, :], ACT.Square)
                        act.activation(SQM[0:NOPE, 2 * hh + 1, :], PS[0:NOPE, 2 * hh + 1, :], ACT.Square)
                        act.activation(QR[0:QK, hh, :], PS[0:QK, 2 * hh, :], ACT.Copy)
                    act.activation(VM[:], PS[:, 7, :].rearrange("p (q n) -> p q n", n=P), ACT.Copy)
                    act.drain().then_inc(mh_act, 1)
                    for hh in range(2):
                        act.wait_ge(mh_pe, at(MH_PE[f"ms{hh}"], 3))
                        if hh:
                            act.wait_ge(mh_dve, at(MH_DVE["qk0"], 2))
                        act.activation(RS2[0:QK, :, :], PS[0:QK, 4:6, :], ACT.Ln, bias=EPSC[0:QK, 0:1], scale=1.0 / QK)
                        act.drain()
                        act.activation(RS2[0:QK, :, :], RS2[0:QK, :, :], ACT.Exp, scale=-0.5)
                        act.drain().then_inc(mh_act, 1)
                    attention(lambda k: at(k + 32))
            heads_out(YMHI, 4)

            t0, c0, gate = TILE0["merge"], CHUNK0["merge"], pc("b_gate_2")
            with act.Fori(0, 2) as i:
                for pair in range(2):
                    t, c, chunk = t0 + 5 * pair, c0 + 12 * pair, 2 * pair
                    act.wait_ge(g_lo, i * 4 + (chunk + 1))

                    def sigmoids(branch, to, first):
                        for m in range(2):
                            n = c + first + m
                            act.wait_ge(s_chunk, i * 24 + (n + 1))
                            act.activation(to[:, m, :], PS[:, n % 4, :], ACT.Sigmoid,
                                           bias=PRM[:, bass.ds(i * 4 + (gate + branch * KD + chunk + m), 1)]
                                           ).then_inc(s_bank_free, 1)
                            act.drain().then_inc(g_sig, 1)

                    hi_in_loop(i, 10, t + 1)
                    sigmoids(0, GA, 0)
                    hi_in_loop(i, 10, t + 2)
                    sigmoids(1, GB, 2)
                    hi_in_loop(i, 10, t + 3)
                    hi_in_loop(i, 10, t + 4)
                    act.wait_ge(g_mid, i * 2 + (pair + 1))
                    sigmoids(2, GB, 8)
                    hi_in_loop(i, 10, t + 5)
                    for m in range(2):
                        act.wait_ge(g_sum, i * 4 + (chunk + m + 1))
                        act.activation(MGHI[:, bass.ds(i * 4 + (chunk + m), 1), :], GA[:, m:m + 1, :], ACT.Copy
                                       ).then_inc(g_hi, 1)
            split_ahead("wout2", 2)
            norm("ffn2", lambda c: X[:, c, :], lambda c: (s_x, X_WOUT2 + c + 1), NRM, D, HHI)
            ffn(2)
            for n in range(1, 8, 2):
                act.wait_ge(s_ot, n + 1)
                act.activation(OTOK[:, n // 2, (n % 2) * S:(n % 2 + 1) * S], PS[:, n, :], ACT.Copy).then_inc(s_oa, 1)

        @block.vector
        def _(dve):
            def lo(t, slot):
                dve.wait_ge(s_hi, t + 1)
                dve.tensor_tensor(WLO[:, slot, :], WRAW[:, slot, :], f32(WHI[:, slot, :]), ALU.subtract
                                  ).then_inc(s_lo, 1)

            def add_lo(to, a, hi_part):
                return dve.tensor_tensor(to, a, f32(hi_part), ALU.subtract)

            def stt(out, in0, scalar, in1, op0=ALU.mult, op1=ALU.mult):
                return dve.scalar_tensor_tensor(out=out, in0=in0, scalar=scalar, in1=in1, op0=op0, op1=op1)

            def norm(name, src, gain, scratch, hi_to=None, lo_to=None, out=None):
                use, n = NORM_USE[name], NORM_N[name]
                dve.wait_ge(n_r, use + 1)

                def low(c):
                    dve.wait_ge(n_hi, LO_BEFORE[name] + c + 1)
                    add_lo(lo_to[:, c, :], scratch[:, c, :], hi_to[:, c, :]).then_inc(n_lo, 1)

                for c in range(n):
                    to = scratch[:, c, :] if out is None else out(c)
                    stt(to, src(c), PRM[:, gain + c:gain + c + 1], R[:]).then_inc(n_h, 1)
                    if lo_to is not None and c:
                        low(c - 1)
                if lo_to is not None:
                    low(n - 1)

            def lo_only(name, per):
                t0 = TILE0[name]
                with dve.Fori(0, TILES[name] // per) as i:
                    for j in range(per):
                        lo(i * per + (t0 + j + 1), (t0 + j + 1) % 2)

            def add_to_residual(name, loops, per, ends, last=False):
                t0, c0 = TILE0[name], CHUNK0[name]

                def body(i, offset=0, skip_last=False):
                    done = 0
                    for j in range(per):
                        if not (skip_last and j == per - 1):
                            lo(i * per + (t0 + j + 1), (t0 + j + 1) % 2)
                        if j in ends:
                            for _ in range(2):
                                bank = (c0 + done) % 4
                                xc = X[:, bass.ds(i * 4 + done, 1), :]
                                dve.wait_ge(s_chunk, i * 4 + (c0 + done + 1))
                                dve.tensor_tensor(xc, xc, PS[:, bank:bank + 1, :], ALU.add).then_inc(s_bank_free, 1)
                                dve.drain().then_inc(s_x, 1)
                                done += 1

                with dve.Fori(0, loops - last) as i:
                    body(i)
                if last:
                    body(loops - 1, skip_last=True)

            def ffn(n):
                t0, c0, first = TILE0[f"up{n}"], CHUNK0[f"up{n}"], (n - 1) * NF
                with dve.Fori(0, NF // 2) as i:
                    def taps(c, acc, chunk):
                        bank = (c0 + c) % 4
                        dve.wait_ge(f_acc, i * 4 + (2 * first + c + 1))
                        stt(acc[:, 1:], PS[:, bank, 0:S - 1], PRM[:, bass.ds(chunk + FFN_TAP[n][1], 1)], acc[:, 1:],
                            op1=ALU.add)
                        dve.drain()
                        stt(acc[:, 2:], PS[:, bank, 0:S - 2], PRM[:, bass.ds(chunk + FFN_TAP[n][0], 1)], acc[:, 2:],
                            op1=ALU.add).then_inc(s_bank_free, 1)
                        dve.drain().then_inc(f_tap, 1)

                    lo(i * 2 + (t0 + 1), (t0 + 1) % 2)
                    for m in range(2):
                        taps(m, FG[:, m, :], i * 2 + m)
                    lo(i * 2 + (t0 + 2), t0 % 2)
                    for m in range(2):
                        taps(2 + m, FU[:, m, :], i * 2 + (NF + m))
                        dve.wait_ge(f_silu, i * 2 + (first + m + 1))
                        dve.tensor_tensor(FU[:, m, :], FU[:, m, :], FG[:, m, :], ALU.mult).then_inc(f_prod, 1)
                    for m in range(2):
                        dve.wait_ge(f_hi, i * 2 + (first + m + 1))
                        add_lo(FLO[:, bass.ds(i * 2 + m, 1), :], FU[:, m:m + 1, :], FHI[:, bass.ds(i * 2 + m, 1), :]
                               ).then_inc(f_lo, 1)
                add_to_residual(f"down{n}", 2, 6, (2, 5), last=n == 2)

            def log1p_of(e, s2, p, rd):
                dve.tensor_scalar(rd, e, 2.0, None, ALU.add)
                dve.drain()
                dve.reciprocal(rd, rd)
                dve.drain()
                dve.tensor_tensor(e, e, rd, ALU.mult)
                dve.drain()
                dve.tensor_tensor(s2, e, e, ALU.mult)
                dve.drain()
                dve.tensor_scalar(p, s2, 1.0 / 17, None, ALU.mult)
                dve.drain()
                for k in (15, 13, 11, 9, 7, 5, 3):
                    stt(p, p, 1.0 / k, s2, op0=ALU.add)
                    dve.drain()
                stt(p, p, 1.0, e, op0=ALU.add)
                dve.drain()
                dve.tensor_scalar(p, p, 2.0, None, ALU.mult)
                dve.drain()

            for tile in range(5):
                dve.wait_ge(s_pt, tile + 1)
                dve.tensor_copy(PRM[:, tile * P:tile * P + PUSED[tile]], PS[:, 5 + tile % 2, 0:PUSED[tile]]
                                ).then_inc(s_ptc, 1)
            for c in range(KD):
                dve.wait_ge(s_xt, c + 1)
                dve.tensor_copy(X[:, c, :], PS[:, c % 4, :]).then_inc(s_x, 1)
            lam = PRM[:, pc("rg_lambda"):pc("rg_lambda") + RG]
            dve.wait_ge(s_setup_a, 1)
            log1p_of(SOFT[:, 0, :], SOFT[:, 1, :], SOFT[:, 2, :], SOFT[:, 3, :])
            dve.tensor_scalar(SOFT[:, 0, :], lam, -1.0, 0.0, ALU.mult, ALU.max)
            dve.drain()
            dve.tensor_tensor(SOFT[:, 0, :], SOFT[:, 0, :], SOFT[:, 2, :], ALU.add)
            dve.drain()
            dve.tensor_scalar(CNEG[:, 0, :], SOFT[:, 0, :], -8.0, None, ALU.mult)
            dve.tensor_scalar(CNEG[:, 1, :], SOFT[:, 0, :], -16.0, None, ALU.mult)
            low = PRM[:, pc("hg_lower_bounds"):pc("hg_lower_bounds") + HG]
            dve.tensor_tensor(LOWB[:, 1, :], low, low, ALU.subtract)
            dve.drain().then_inc(s_setup_v, 1)
            dve.wait_ge(s_setup_a, 2)
            dve.reciprocal(SOFT[:, 1, :], LOWB[:, 0, :])
            dve.drain()
            dve.tensor_tensor(SOFT[:, 1, :], SOFT[:, 1, :], LOWB[:, 0, :], ALU.mult)
            dve.drain()
            dve.tensor_tensor(LOWB[:, 0, :], SOFT[:, 1, :], SOFT[:, 1, :], ALU.subtract)
            dve.drain()
            dve.tensor_scalar(LOWB[:, 1, :], LOWB[:, 0, :], -1.0, 1.0, ALU.mult, ALU.add)
            lo(0, 0)
            dve.wait_ge(s_const, 1)
            dve.tensor_tensor(MSCRI[:, 0, :], MSCRI[:, 0, :], MSCRI[:, 1, :], ALU.bitwise_xor)
            dve.drain()
            dve.tensor_copy(MSCR[:, 9, :], MSCRI[:, 0, :]).then_inc(s_mask, 1)
            dve.wait_ge(s_mask, 2)
            for b in range(LEVELS + 1):
                dve.tensor_scalar(MSCR[:, b, :], MSCR[:, 9, :], float(2 ** b), None, ALU.is_ge)
            dve.tensor_scalar(HMASK[:, 0, :], MSCR[:, 9, :], 0.0, None, ALU.is_equal)
            dve.drain()
            for b in range(LEVELS):
                dve.tensor_tensor(HMASK[:, 1 + b, :], MSCR[:, b, :], MSCR[:, b + 1, :], ALU.subtract)

            norm("mix1", lambda c: X[:, c, :], pc("norm_mix_gain"), NRM, HHI, HLO)
            lo_only("proj1", 2)
            dve.wait_ge(s_bank_free, 4 + CHUNK0["wout1"])

            U = YP[:, 0:RG, :]
            w = pc("rg_conv_w")
            for c in range(RG):
                dve.tensor_scalar(U[:, c, :], Z[:, A_U + c, :], PRM[:, w + 3 * RG + c:w + 3 * RG + c + 1],
                                  PRM[:, pc("rg_conv_b") + c:pc("rg_conv_b") + c + 1], ALU.mult, ALU.add)
            for back in (1, 2, 3):
                dve.drain()
                k = w + (3 - back) * RG
                for c in range(RG):
                    stt(U[:, c, back:], Z[:, A_U + c, 0:S - back], PRM[:, k + c:k + c + 1], U[:, c, back:], op1=ALU.add)
            dve.drain().then_inc(rg_dve, 1)
            cv, acc = Z[:, C_C:C_C + SC, :], Z[:, C_V:C_V + SC, :]
            dve.tensor_tensor(cv, cv, acc, ALU.mult)
            dve.drain()
            w = pc("sc_conv_w")
            for c in range(SC):
                dve.tensor_scalar(acc[:, c, :], cv[:, c, :], PRM[:, w + 2 * SC + c:w + 2 * SC + c + 1], None, ALU.mult)
            for back in (1, 2):
                dve.drain()
                k = w + (2 - back) * SC
                for c in range(SC):
                    stt(acc[:, c, back:], cv[:, c, 0:S - back], PRM[:, k + c:k + c + 1], acc[:, c, back:], op1=ALU.add)
            dve.drain()
            dve.tensor_tensor(YP[:, RG + HG:KD, :], acc, Z[:, C_B:C_B + SC, :], ALU.mult)
            dve.drain().then_inc(sc_done, 1)
            dve.wait_ge(rg_act, RG_ACT["exps"])
            stt(TH[:], Z[:, A_U:A_U + RG, :], 1.0, TH[:], op0=ALU.add)
            dve.drain().then_inc(rg_dve, 1)
            dve.tensor_tensor(IG[:], IG[:], U, ALU.mult)
            dve.drain()
            dve.wait_ge(rg_act, RG_ACT["beta"])
            dve.tensor_tensor(IG[:], IG[:], TH[:], ALU.mult)
            dve.drain()
            for c in range(RG):
                dve.tensor_tensor_scan(U[:, c, :], AD[:, c, :], IG[:, c, :], 0.0, ALU.mult, ALU.add)
            dve.drain().then_inc(rg_dve, 1)
            dve.wait_ge(rg_act, RG_ACT["gelus"])
            dve.tensor_tensor(U, U, Z[:, A_GATE:A_GATE + RG, :], ALU.mult)
            dve.memset(HS[:], 0.0)
            dve.drain().then_inc(rg_dve, 1)

            with dve.Fori(0, HG) as i:
                def act(name):
                    dve.wait_ge(hg_act, i * len(HG_ACT) + HG_ACT[name])

                def pe(name):
                    dve.wait_ge(hg_pe, i * len(HG_PE) + HG_PE[name])

                def halves(t, b):
                    v = t.rearrange("p (n two h) -> p n two h", two=2, h=2 ** b)
                    return v[:, :, 0, :], v[:, :, 1, :]

                def level_exponents(b):
                    even, odd = halves(HG_[:], b)
                    d_even, d_odd = halves(HDD[:, b % 2, :], b)
                    mid = even[:, :, 2 ** b - 1:2 ** b].broadcast_to(list(even.shape))
                    dve.tensor_tensor(d_even, mid, even, ALU.subtract)
                    dve.tensor_tensor(d_odd, odd, mid, ALU.subtract)
                    dve.drain().then_inc(hg_dve, 1)

                def level_product(b):
                    act(f"e{b}")
                    if b >= 1:
                        pe(f"g{b - 1}")
                    e_even, e_odd = halves(HDD[:, b % 2, :], b)
                    m_even, m_odd = halves(HM[:, b % 2, :], b)
                    dve.tensor_tensor(m_even, e_even, halves(HK[:], b)[0], ALU.mult)
                    dve.tensor_tensor(m_odd, e_odd, halves(HQ[:], b)[1], ALU.mult)
                    dve.drain().then_inc(hg_dve, 1)

                def take(level):
                    for h in range(2):
                        dve.copy_predicated(
                            out=HST[:, h, :].rearrange("p (q n) -> p q n", n=P),
                            mask=HMASK[:, level, :].unsqueeze(1).broadcast_to([P, NT, P]),
                            data=PS[:, 4 + 2 * (level % 2) + h, :].rearrange("p (q n) -> p q n", n=P))
                    dve.drain().then_inc(hg_dve, 1)

                act("q_sigmoid")
                dve.memset(HST[:], 0.0)
                dve.tensor_scalar(HQ[:], HQ[:], HD ** -0.5, None, ALU.mult)
                dve.tensor_scalar(HG_[:], HG_[:], LOWB[:, 1, bass.ds(i, 1)], LOWB[:, 0, bass.ds(i, 1)], ALU.mult, ALU.add)
                dve.drain()
                dve.tensor_scalar(HK[:], HG_[:], -1.0, 1.0, ALU.mult, ALU.add)
                dve.drain().then_inc(hg_dve, 1)
                act("logf")
                dve.tensor_tensor_scan(HG_[:], RESET[:], HG_[:], 0.0, ALU.mult, ALU.add)
                dve.drain()
                for b in range(LEVELS + 1):
                    if b < LEVELS:
                        level_exponents(b)
                    if b >= 1:
                        level_product(b - 1)
                    if b >= 2:
                        take(b - 2)
                pe(f"g{LEVELS - 1}")
                gv = HG_[:].rearrange("p (q n) -> p q n", n=P)
                dve.tensor_tensor(HKD[:].rearrange("p (q n) -> p q n", n=P), gv[:, :, P - 1:P].broadcast_to([P, NT, P]), gv,
                                  ALU.subtract)
                dve.drain().then_inc(hg_dve, 1)
                take(LEVELS - 1)
                act("decays")
                pe(f"g{LEVELS}")
                dve.tensor_tensor(HKD[:], HKD[:], HK[:], ALU.mult)
                dve.tensor_tensor(HQG[:], HQG[:], HQ[:], ALU.mult)
                dve.drain().then_inc(hg_dve, 1)
                take(LEVELS)
                pe("states")
                for q in range(3):
                    for h in range(2):
                        b = slice(h * HD, (h + 1) * HD)
                        new = PS[b, 2, q * P + h * HD:q * P + (h + 1) * HD]
                        if q == 0:
                            dve.tensor_copy(HS[b, q, b], new)
                        else:
                            stt(HS[b, q, b], HS[b, q - 1, b], HEGL[b, q:q + 1], new, op1=ALU.add)
                    dve.drain()
                dve.drain().then_inc(hg_dve, 1)

            for c in range(KD):
                dve.wait_ge(hn_r, c // 4 + 1)
                g = pc("mix_out_gain") + c
                stt(YP[:, c, :], YP[:, c, :], PRM[:, g:g + 1], SQ1[:, c, :])
                if RG <= c < RG + HG:
                    dve.wait_ge(hn_g, 1)
                    dve.drain()
                    dve.tensor_tensor(YP[:, c, :], YP[:, c, :], Z[:, B_G + c - RG, :], ALU.mult)
                dve.drain().then_inc(hn_y, 1)
                if c:
                    dve.wait_ge(hn_hi, c)
                    add_lo(HLO[:, c - 1, :], YP[:, c - 1, :], HHI[:, c - 1, :])
            dve.wait_ge(hn_hi, KD)
            add_lo(HLO[:, KD - 1, :], YP[:, KD - 1, :], HHI[:, KD - 1, :]).then_inc(hn_lo, 1)

            add_to_residual("wout1", 2, 2, (0, 1))
            norm("ffn1", lambda c: X[:, c, :], pc("norm_ffn_gain"), NRM, HHI, HLO)
            ffn(1)

            for c in range(KD):
                dve.wait_ge(e_hi, c + 1)
                add_lo(HLO[:, c, :], X[:, c, :], HHI[:, c, :]).then_inc(e_lo, 1)
            dve.wait_ge(e_phi, 1)
            add_lo(PLO[:], PS[:, 6:8, :], PHI[:]).then_inc(e_plo, 1)
            t0 = TILE0["plegate"]
            lo(t0, t0 % 2)
            dve.wait_ge(e_pp, 1)
            for c in range(KD):
                t = t0 + c // 2 + 1
                if c % 2 == 0:
                    lo(t, t % 2)
                dve.wait_ge(e_g, c + 1)
                dve.tensor_tensor(PG[:, c % 2, :], PG[:, c % 2, :], PP[:, c, :], ALU.mult)
                dve.drain()
                dve.tensor_tensor(X[:, c, :], X[:, c, :], PG[:, c % 2, :], ALU.add)
                dve.drain().then_inc(s_x, 1)
            norm("final", lambda c: X[:, c, :], pc("final_norm_gain"), NRM, out=lambda c: X[:, c, :])
            norm("mix2", lambda c: X[:, c, :], pc("norm_mix_g_2"), NRM, HHI, HLO)
            dve.drain().then_inc(h_dfree, 2)
            t0, c0, w = TILE0["xbc"], CHUNK0["xbc"], pc("ssm_conv_w_2")
            with dve.Fori(0, 3) as i:
                for j in range(2):
                    lo(i * 2 + (t0 + j + 1), (t0 + j + 1) % 2)
                    for m in range(2):
                        c = 2 * j + m
                        dve.wait_ge(x_acc, i * 4 + (c + 1))
                        for back in (1, 2, 3):
                            acc = XBC[:, bass.ds(i * 4 + c, 1), back:]
                            bank = (c0 + c) % 4
                            last = stt(acc, PS[:, bank:bank + 1, 0:S - back],
                                       PRM[:, bass.ds(i * 4 + (w + (3 - back) * NXBC + c), 1)], acc, op1=ALU.add)
                            if back < 3:
                                dve.drain()
                        last.then_inc(s_bank_free, 1)
            lo_only("z", 2)
            t = TILE0["small"]
            lo(t + 1, (t + 1) % 2)

            small, decay_rows, last_col = slice(0, SMALL_W), slice(64, 80), slice(P - 1, S, P)
            dve.memset(PACK[:], 0.0)
            dve.wait_ge(ss_act, SS_ACT["raw"])
            dve.wait_ge(s_small, SMALL_LOADS)
            dve.tensor_scalar(SMT[small, 0, :], SMC[small, :], SMB[small, 0:1], SMB[small, 1:2], ALU.add, ALU.mult)
            dve.drain().then_inc(ss_dve, 1)
            dve.wait_ge(ss_act, SS_ACT["e"])
            log1p_of(SMT[small, 1, :], SMT[small, 2, :], SMT[small, 3, :], SMT[small, 4, :])
            stt(SMT[small, 0, :], SMT[small, 0, :], 0.0, SMT[small, 3, :], ALU.max, ALU.add)
            dve.tensor_scalar(SMB[decay_rows, 2:3], SMB[decay_rows, 2:3], -1.0, None, ALU.mult)
            dve.drain()
            dve.tensor_scalar(SMT[small, 2, :], SMT[small, 0, :], SMB[small, 2:3], None, ALU.mult)
            dve.tensor_copy(PACK[0:16, :], SMT[decay_rows, 0, :])
            dve.drain()
            dve.tensor_tensor_scan(CUM[32:64, :], ONES[32:64, 0:1].broadcast_to([32, S]), SMT[32:64, 2, :], 0.0, ALU.mult, ALU.add)
            dve.tensor_tensor_scan(CUM[decay_rows, :], RESET[decay_rows, :], SMT[decay_rows, 2, :], 0.0, ALU.mult, ALU.add)
            dve.drain()
            dve.tensor_copy(PACK[32:48, :], CUM[decay_rows, :])
            dve.tensor_scalar(SMT[32:64, 4, :], CUM[32:64, :], -1.0, None, ALU.mult)
            by_tile = CUM[decay_rows, :].rearrange("p (q n) -> p q n", n=P)
            dve.tensor_tensor(SMT[decay_rows, 3, :].rearrange("p (q n) -> p q n", n=P),
                              by_tile[:, :, P - 1:P].broadcast_to([16, NT, P]), by_tile, ALU.subtract)
            dve.drain().then_inc(ss_dve, 1)
            dve.wait_ge(ss_act, SS_ACT["pexp"])
            dve.tensor_tensor(PACK[64:80, :], SMT[decay_rows, 3, :], SMT[decay_rows, 0, :], ALU.mult)
            dve.drain().then_inc(ss_dve, 1)
            dve.wait_ge(ss_pe, SS_PE["tok"])
            dve.tensor_copy(TOK[:], PS[:, 0, :].rearrange("p (q n) -> p q n", n=P))
            dve.drain().then_inc(ss_dve, 1)
            dve.wait_ge(s_rows, 64)
            for g in range(2):
                heads = slice(8 * g, 8 * g + 8)

                def per_head(t, q=slice(None)):
                    return t[:, q, :].rearrange("p q (h d) -> p q h d", d=HD)

                def by_token(first, q0=0):
                    return TOK[:, q0:, first + 8 * g:first + 8 * g + 8].unsqueeze(3).broadcast_to([P, NT - q0, 8, HD])

                dve.wait_ge(ss_pe, SS_PE[f"turned{g}"])
                dve.tensor_tensor(CBM[:].rearrange("p (q n) -> p q n", n=P), PS[:, 2, :].rearrange("p (q n) -> p q n", n=P),
                                  TRI[:].unsqueeze(1).broadcast_to([P, NT, P]), ALU.mult)
                dve.tensor_tensor(per_head(XD), per_head(PS, slice(4, 8)), by_token(0), ALU.mult)
                dve.tensor_tensor(per_head(XW), per_head(PS, slice(4, 8)), by_token(64), ALU.mult)
                dve.drain().then_inc(ss_dve, 1)
                dve.wait_ge(ss_pe, SS_PE[f"states{g}"])
                dve.wait_ge(ss_act, SS_ACT["dec"])
                dve.tensor_copy(SH[:, 0, :], PS[:, 4, :])
                for q in (1, 2):
                    dve.drain()
                    dve.tensor_tensor(per_head(SH, slice(q, q + 1)), per_head(SH, slice(q - 1, q)),
                                      DEC[:, heads, q:q + 1].unsqueeze(1).broadcast_to([P, 1, 8, HD]), ALU.mult)
                    dve.drain()
                    dve.tensor_tensor(SH[:, q, :], SH[:, q, :], PS[:, 4 + q, :], ALU.add)
                dve.drain().then_inc(ss_dve, 1)
                dve.wait_ge(ss_pe, SS_PE[f"yoff{g}"])
                dve.tensor_tensor(per_head(YT, slice(1, 4)), per_head(PS, slice(1, 4)), by_token(96, 1), ALU.mult)
                dve.drain().then_inc(ss_dve, 1)
                with dve.Fori(0, 4) as i:
                    def at(b):
                        return i * 2 + (8 * g + b + 1)

                    def masked(b):
                        dve.wait_ge(h_e, at(b))
                        dve.tensor_tensor(DM[:, b, :], DM[:, b, :], CBM[:], ALU.mult)
                        dve.drain().then_inc(h_m, 1)

                    for b in range(2):
                        dve.wait_ge(s_abc[b], i * 16 + (64 * g + 16))
                        dve.wait_ge(h_y, at(b))
                        for q in range(NT):
                            cols = slice(q * P, (q + 1) * P)
                            dve.tensor_scalar(DM[:, b, cols], ABC[:, b, cols], TOK[:, q, bass.ds(i * 2 + (32 + 8 * g + b), 1)],
                                              0.0, ALU.subtract, ALU.min)
                        dve.drain().then_inc(h_dfree, 1)
                        dve.drain().then_inc(h_d, 1)
                        if b:
                            masked(0)
                    masked(1)
                dve.wait_ge(h_y, 8 * g + 10)
                dve.tensor_copy(YT[:, 0, :], PS[:, 0, :])
                dve.tensor_tensor(YT[:, 1:4, :], YT[:, 1:4, :], PS[:, 1:4, :], ALU.add)
                dve.drain().then_inc(ss_dve, 1)
                dve.wait_ge(ss_pe, SS_PE[f"yturned{g}"])
                for j in range(4):
                    c = 4 * g + j
                    stt(XBC[:, c, :], XBC[:, c, :], DSKIP[:, c:c + 1], PS[:, 4 + j, :], op1=ALU.add)
                dve.drain()
                y = slice(4 * g, 4 * g + 4)
                dve.tensor_tensor(XBC[:, y, :], XBC[:, y, :], ZS[:, y, :], ALU.mult)
                dve.drain().then_inc(ss_dve, 1)
            norm("ssm", lambda c: XBC[:, c, :], pc("ssm_norm_g_2"), NS, YSHI, YSLO)

            def scores(mask, u, at):
                qb = u % 4
                diagonal = PS[:, u % 4, qb * P:(qb + 1) * P]
                dve.wait_ge(a_s, at(u + 1))
                dve.tensor_tensor(diagonal, diagonal, mask[:], ALU.add)
                dve.drain()
                dve.tensor_reduce(out=NMX[:, 0, u:u + 1], in_=PS[:, u % 4, 0:(qb + 1) * P], axis=AX, op=ALU.max, negate=True)
                dve.drain().then_inc(a_mx, 1)

            def output(u, at, col):
                dve.wait_ge(a_pv, at(u + 1))
                dve.reciprocal(NMX[:, 2, u:u + 1], NMX[:, 1, u:u + 1])
                dve.drain()
                dve.tensor_scalar(OH[:, u % 4, bass.ds(col(u // 4), HD)], PS[:, 6 + u % 2, 0:HD], NMX[:, 2, u:u + 1], None,
                                  ALU.mult).then_inc(a_o, 1)

            def attend(mask, at, col):
                for u in range(8):
                    scores(mask, u, at)
                    if u >= 3:
                        output(u - 3, at, col)
                for u in (5, 6, 7):
                    output(u, at, col)

            def heads_out(hi, lo_to, first):
                for c in range(4):
                    dve.wait_ge(o_hi, first + c + 1)
                    add_lo(lo_to[:, c, :], PS[:, 4 + c, :], hi[:, c, :]).then_inc(o_lo, 1)

            lo_only("foxqk", 2)
            t0 = TILE0["foxv"]
            for t in (t0 + 1, t0 + 2):
                lo(t, t % 2)
            dve.tensor_scalar(QKG[:, 0:1], QKG[:, 0:1], HD ** -0.5, None, ALU.mult)
            dve.tensor_scalar(QKG[:, 2:3], QKG[:, 2:3], QK ** -0.5, None, ALU.mult)
            dve.memset(QS[64:96, :, :], 1.0)
            dve.memset(KS[64:96, :, :], 1.0)
            dve.drain().then_inc(q_rowfree, 1)
            with dve.Fori(0, 4) as i:
                dve.wait_ge(q_r, i + 1)
                for hh in range(2):
                    b = slice(hh * HD, (hh + 1) * HD)
                    for to, n in ((QS, 0), (KS, 1)):
                        stt(to[0:HD, hh:hh + 1, :], QKR[b, bass.ds(i + 4 * n, 1), :], QKG[b, n:n + 1], RS2[b, n:n + 1, :])
                dve.drain().then_inc(a_qk, 1)
                attend(CAUSAL, lambda k: i * 8 + k, lambda hh: i * P + hh * HD)
                dve.drain().then_inc(q_rowfree, 1)
            heads_out(YFHI, YFLO, 0)

            t0 = TILE0["mlac"]
            for t in (t0 + 1, t0 + 2, t0 + 3):
                lo(t, t % 2)
            norm("mlaq", lambda c: CR[:, c, :], pc("mla_q_norm_g_2"), NC, CQHI, CQLO)
            norm("mlakv", lambda c: CR[:, 3 + c, :], pc("mla_kv_norm_g_2"), NC, CQHI[:, 3:5, :], CQLO[:, 3:5, :])
            half, rope = ROPE // 2, slice(NOPE, QK)
            for n in range(2):
                dve.tensor_scalar(SW[rope, n, 0:half], IDENT[rope, NOPE + half:QK], -1.0, QKG[rope, 2 + n:3 + n], ALU.mult, ALU.mult)
                dve.tensor_scalar(SW[rope, n, half:ROPE], IDENT[rope, NOPE:NOPE + half], QKG[rope, 2 + n:3 + n], None, ALU.mult)
            dve.drain().then_inc(mp_dve, 1)
            ang, cos, n, t = (ANG[rope, k, :] for k in range(4))
            dve.wait_ge(s_pos, 16)
            dve.tensor_copy(ang, POSI[rope, :])
            dve.drain()
            dve.tensor_scalar(ang, ang, INVF[rope, 0:1], None, ALU.mult)
            dve.drain()
            dve.tensor_scalar(n, ang, 1 / TWO_PI, None, ALU.mult)
            dve.drain()
            dve.tensor_scalar(n, n, ROUNDING, None, ALU.add)
            dve.drain()
            dve.tensor_scalar(n, n, ROUNDING, None, ALU.subtract)
            dve.drain()
            for part in TWO_PI_PARTS:
                stt(ang, n, -part, ang, op1=ALU.add)
                dve.drain()
            dve.tensor_scalar(t, ang, np.pi / 2, -TWO_PI, ALU.is_gt, ALU.mult)
            dve.drain()
            stt(cos, t, np.pi / 2, ang, ALU.add, ALU.add)
            dve.drain()
            for v in (ang, cos):
                dve.tensor_scalar(v, v, PI_BELOW, -PI_BELOW, ALU.min, ALU.max)
            dve.drain().then_inc(mp_dve, 1)
            dve.tensor_scalar(CG[0:NOPE, :], ONES[0:NOPE, 0:1].broadcast_to([NOPE, S]), QKG[0:NOPE, 2:3], None, ALU.mult)
            dve.wait_ge(mp_act, MP_ACT["trig"])
            dve.tensor_scalar(CG[rope, :], cos, QKG[rope, 2:3], None, ALU.mult)
            stt(KROT[rope, :], KRR[rope, :], QKG[rope, 3:4], cos)
            dve.wait_ge(mp_pe, MP_PE["kswap"])
            dve.tensor_tensor(MR[rope, :], PS[rope, 6, :], SIN[rope, :], ALU.mult)
            dve.drain()
            dve.tensor_tensor(KROT[rope, :], KROT[rope, :], MR[rope, :], ALU.add)
            dve.drain().then_inc(mp_dve, 1)
            t0 = TILE0["mlahead"]
            with dve.Fori(0, 2) as i:
                for j in range(2):
                    def at(k, n=8):
                        return i * (2 * n) + (n * j + k)

                    lo(i * 2 + (t0 + j + 1), (t0 + j + 1) % 2)
                    for hh in range(2):
                        dve.wait_ge(mh_act, at(MH_ACT[f"r{hh}"], 3))
                        dve.tensor_tensor(MR[rope, :], PS[rope, 6, :], SIN[rope, :], ALU.mult)
                        dve.tensor_tensor(QS[0:QK, hh, :], QR[0:QK, hh, :], CG[0:QK, :], ALU.mult)
                        stt(KS[0:NOPE, hh, :], PS[0:NOPE, 2 * hh + 1, :], QKG[0:NOPE, 3:4], RS2[0:NOPE, 1, :])
                        dve.tensor_tensor(KS[rope, hh, :], KROT[rope, :], RS2[rope, 1, :], ALU.mult)
                        dve.drain()
                        dve.tensor_tensor(QS[rope, hh, :], QS[rope, hh, :], MR[rope, :], ALU.add)
                        dve.drain()
                        dve.tensor_tensor(QS[0:QK, hh, :], QS[0:QK, hh, :], RS2[0:QK, 0, :], ALU.mult)
                        dve.drain().then_inc(mh_dve, 1)
                    attend(CHUNKED, lambda k: at(k + 32), lambda hh: i * (2 * P) + (j * P + hh * HD))
            heads_out(YMHI, YMLO, 4)

            dve.drain().then_inc(g_lo, 1)
            t0, c0 = TILE0["merge"], CHUNK0["merge"]
            with dve.Fori(0, 2) as i:
                for pair in range(2):
                    t, c, chunk = t0 + 5 * pair, c0 + 12 * pair, 2 * pair

                    def gated(gate, to, first):
                        for m in range(2):
                            n = c + first + m
                            dve.wait_ge(g_sig, i * 12 + (6 * pair + gate + m + 1))
                            dve.wait_ge(s_chunk, i * 24 + (n + 1))
                            dve.tensor_tensor(to[:, m, :], to[:, m, :], PS[:, n % 4, :], ALU.mult).then_inc(s_bank_free, 1)
                        dve.drain()
                        if first != 4:
                            dve.tensor_tensor(GA[:], GA[:], GB[:], ALU.add)
                            dve.drain().then_inc(g_mid if first == 6 else g_sum, 1 if first == 6 else 2)

                    for k in (1, 2, 3):
                        lo(i * 10 + (t + k), (t + k) % 2)
                    gated(0, GA, 4)
                    gated(2, GB, 6)
                    lo(i * 10 + (t + 4), (t + 4) % 2)
                    lo(i * 10 + (t + 5), (t + 5) % 2)
                    gated(4, GB, 10)
                    for m in range(2):
                        dve.wait_ge(g_hi, i * 4 + (chunk + m + 1))
                        add_lo(MGLO[:, bass.ds(i * 4 + (chunk + m), 1), :], GA[:, m:m + 1, :],
                               MGHI[:, bass.ds(i * 4 + (chunk + m), 1), :]).then_inc(g_lo, 1)
            add_to_residual("wout2", 2, 2, (0, 1))
            norm("ffn2", lambda c: X[:, c, :], pc("norm_ffn_g_2"), NRM, HHI, HLO)
            ffn(2)
            for n in range(0, 8, 2):
                dve.wait_ge(s_ot, n + 1)
                dve.tensor_copy(OTOK[:, n // 2, 0:S], PS[:, n, :]).then_inc(s_oc, 1)

        @block.tensor
        def _(pe):
            def mm(out, lhsT, rhs, start=True, stop=True):
                return pe.matmul(out, lhsT, rhs, start=start, stop=stop)

            def exact(out, w_hi, w_lo, r_hi, r_lo, kts, start=True, stop=True, opening=False):
                for k in range(kts):
                    last = mm(out, w_hi(k), r_hi(k), start=start and k == 0, stop=False)
                    if opening and k == 0:
                        last.then_inc(s_started, 1)
                    mm(out, w_hi(k), r_lo(k), start=False, stop=False)
                    last = mm(out, w_lo(k), r_hi(k), start=False, stop=stop and k == kts - 1)
                return last

            def weights(slot, kts, cols, m, offset=0, width=P):
                hi, lo = (wtile(t, slot, kts, cols, offset) for t in (WHI, WLO))
                return lambda k: hi[:, k, m:m + width], lambda k: lo[:, k, m:m + width]

            def moving(hi, lo, k0=0):
                return lambda k: hi[:, k0 + k, :], lambda k: lo[:, k0 + k, :]

            def columns(name, rhs):
                t0, c0 = TILE0[name], CHUNK0[name]
                with pe.Fori(0, TILES[name] // 2) as i:
                    for j in range(2):
                        pe.wait_ge(s_lo, i * 2 + (t0 + j + 1))
                        for m in range(2):
                            c = 2 * j + m
                            pe.wait_ge(s_bank_free, i * 4 + (c0 + c + 1))
                            exact(PS[:, (c0 + c) % 4, :], *weights((t0 + j) % 2, KD, 256, m * P), *moving(*rhs), KD,
                                  opening=m == 0).then_inc(s_chunk, 1)

            def down(name):
                t0, c0 = TILE0[name], CHUNK0[name]
                with pe.Fori(0, 2) as i:
                    for half in range(2):
                        for part, (k0, kts) in enumerate(DOWN_PARTS):
                            j = 3 * half + part
                            pe.wait_ge(s_lo, i * 6 + (t0 + j + 1))
                            for m in range(2):
                                c = 2 * half + m
                                if part == 0:
                                    pe.wait_ge(s_bank_free, i * 4 + (c0 + c + 1))
                                last = exact(PS[:, (c0 + c) % 4, :], *weights((t0 + j) % 2, kts, 256, m * P),
                                             *moving(FHI, FLO, k0), kts, start=part == 0, stop=part == 2,
                                             opening=m == 0)
                                if part == 2:
                                    last.then_inc(s_chunk, 1)

            def norm(name, scratch):
                use, first, n = NORM_USE[name], NORM_BASE[name], NORM_N[name]
                if use:
                    pe.wait_ge(n_r, use)
                for c in range(n):
                    pe.wait_ge(n_sq, first + c + 1)
                    last = mm(PS[:, 4, :], ONES[:], scratch[:, c, :], start=c == 0, stop=c == n - 1)
                last.then_inc(n_ms, 1)

            pe.wait_ge(s_const, 1)
            pe.wait_ge(s_params, 16 * len(PARAM_ROWS))
            for tile in range(5):
                if tile >= 2:
                    pe.wait_ge(s_ptc, tile - 1)
                n = PUSED[tile]
                pe.transpose(PS[:, 5 + tile % 2, 0:n], PROWS[0:n, tile, :], IDENT[0:n, 0:n]).then_inc(s_pt, 1)
            pe.wait_ge(s_xin, 16 * NT)
            for c in range(KD):
                if c >= 4:
                    pe.wait_ge(s_x, c - 3)
                for q in range(NT):
                    last = pe.transpose(PS[:, c % 4, q * P:(q + 1) * P], XTOK[:, q, c * P:(c + 1) * P], IDENT[:])
                last.then_inc(s_xt, 1)
            norm("mix1", NRM)
            pe.wait_ge(n_lo, KD)
            columns("proj1", (HHI, HLO))

            pe.wait_ge(s_small, SMALL_LOADS)
            pe.wait_ge(rg_dve, RG_DVE["u"])
            for c in range(RG):
                last = mm(PS[:, 4 + c, :], WR[:, c, :], YP[:, c, :])
            last.then_inc(rg_pe, 1)
            for c, bank in zip(range(RG), (7, 0, 1)):
                last = mm(PS[:, bank, :], WI[:, c, :], YP[:, c, :])
            last.then_inc(rg_pe, 1)

            pe.wait_ge(rg_act, RG_ACT["sigmoids"])
            with pe.Fori(0, HG) as i:
                def act(name):
                    pe.wait_ge(hg_act, i * len(HG_ACT) + HG_ACT[name])

                def dve(name):
                    pe.wait_ge(hg_dve, i * len(HG_DVE) + HG_DVE[name])

                for level in range(LEVELS + 1):
                    dve("qk" if level == 0 else f"m{level - 1}")
                    if level >= 2:
                        dve(f"c{level - 2}")
                    for h in range(2):
                        for q in range(NT):
                            b, cols = slice(h * HD, (h + 1) * HD), slice(q * P, (q + 1) * P)
                            keys = HK[b, cols] if level == 0 else HM[b, (level - 1) % 2, cols]
                            queries = HQ[b, cols] if level == 0 else HM[b, (level - 1) % 2, cols]
                            last = mm(PS[:, 4 + 2 * (level % 2) + h, cols], keys, queries)
                    last.then_inc(hg_pe, 1)
                dve("gated")
                for q in range(NT):
                    cols = slice(q * P, (q + 1) * P)
                    pe.transpose(PS[:, 0, cols], HVS[:, cols], IDENT[:])
                    last = pe.transpose(PS[:, 1, cols], HKD[:, cols], IDENT[:])
                last.then_inc(hg_pe, 1)
                act("v_turned")
                for q in range(3):
                    last = mm(PS[:, 2, q * P:(q + 1) * P], HKDT[:, q, :], HVT[:, q, :])
                last.then_inc(hg_pe, 1)
                dve("state")
                for q in range(NT):
                    cols = slice(q * P, (q + 1) * P)
                    if q:
                        mm(PS[:, 3, cols], HS[:, q - 1, :], HQG[:, cols], stop=False)
                    for h in range(2):
                        b = slice(h * HD, (h + 1) * HD)
                        last = mm(PS[b, 3, cols], HVT[:, q, b], HST[:, h, cols], start=q == 0)
                last.then_inc(hg_pe, 1)

            for half in range(2):
                pe.wait_ge(hn_sq, 1)
                if half:
                    pe.wait_ge(hn_r, 1)
                for c in range(4):
                    last = mm(PS[:, 4 + c, :], BONES[:], SQ1[:, 4 * half + c, :])
                last.then_inc(hn_ps, 1)
            pe.wait_ge(hn_lo, 1)
            columns("wout1", (HHI, HLO))
            norm("ffn1", NRM)
            pe.wait_ge(n_lo, LO_BEFORE["ffn1"] + KD)
            columns("up1", (HHI, HLO))
            pe.wait_ge(f_lo, NF)
            down("down1")

            pe.wait_ge(e_p, 16 * NT)
            for k in range(PLE // P):
                for q in range(NT):
                    last = pe.transpose(PS[:, 6 + k, q * P:(q + 1) * P], PTOK[:, q, k * P:(k + 1) * P], IDENT[:])
            last.then_inc(e_pt, 1)
            t0, c0 = TILE0["pleproj"], CHUNK0["pleproj"]
            pe.wait_ge(e_plo, 1)
            pe.wait_ge(s_lo, t0 + 1)
            for c in range(KD):
                pe.wait_ge(s_bank_free, c0 + c + 1)
                exact(PS[:, (c0 + c) % 4, :], *weights(t0 % 2, 2, D, c * P), *moving(PHI, PLO), 2,
                      opening=c == 0).then_inc(s_chunk, 1)
            pe.wait_ge(e_lo, KD)
            columns("plegate", (HHI, HLO))
            norm("final", NRM)
            norm("mix2", NRM)
            pe.wait_ge(n_lo, LO_BEFORE["mix2"] + KD)
            columns("xbc", (HHI, HLO))
            columns("z", (HHI, HLO))
            t, c = TILE0["small"], CHUNK0["small"]
            pe.wait_ge(s_lo, t + 1)
            pe.wait_ge(s_bank_free, c + 1)
            exact(PS[0:SMALL_W, c % 4, :], *weights(t % 2, KD, SMALL_W, 0, width=SMALL_W), *moving(HHI, HLO), KD,
                  opening=True).then_inc(s_chunk, 1)

            pe.drain().then_inc(h_y, 2)
            pe.wait_ge(s_bank_free, 4 + CHUNK0["foxqk"])
            pe.wait_ge(ss_dve, SS_DVE["packed"])
            for q in range(NT):
                cols = slice(q * P, (q + 1) * P)
                last = pe.transpose(PS[:, 0, cols], PACK[:, cols], IDENT[:])
            last.then_inc(ss_pe, 1)
            pe.wait_ge(ss_act, SS_ACT["silu"])
            for g in range(2):
                if g:
                    pe.wait_ge(ss_dve, SS_DVE["y0"])
                for q in range(NT):
                    cols = slice(q * P, (q + 1) * P)
                    for j in range(4):
                        pe.transpose(PS[:, 4 + q, j * P:(j + 1) * P], XBC[:, 4 * g + j, cols], IDENT[:])
                    pe.transpose(PS[:, 1, cols], XBC[:, 8 + g, cols], IDENT[:])
                    last = mm(PS[:, 2, cols], XBC[:, 8 + g, cols], XBC[:, 10 + g, cols])
                last.then_inc(ss_pe, 1)
                pe.wait_ge(ss_dve, SS_DVE[f"xdw{g}"])
                pe.wait_ge(ss_act, SS_ACT[f"bt{g}"])
                for q in range(3):
                    last = mm(PS[:, 4 + q, :], BT[:, q, :], XW[:, q, :])
                last.then_inc(ss_pe, 1)
                pe.wait_ge(ss_dve, SS_DVE[f"h{g}"])
                for q in range(1, NT):
                    last = mm(PS[:, q, :], XBC[:, 10 + g, q * P:(q + 1) * P], SH[:, q - 1, :])
                last.then_inc(ss_pe, 1)
                pe.wait_ge(ss_dve, SS_DVE[f"yt{g}"])
                with pe.Fori(0, 4) as i:
                    for b in range(2):
                        pe.wait_ge(h_m, i * 2 + (8 * g + b + 1))
                        for q in range(NT):
                            head = bass.ds(i * P + b * HD, HD)
                            last = mm(PS[:, q, head], DM[:, b, q * P:(q + 1) * P], XD[:, q, head])
                        last.then_inc(h_y, 1)
                pe.wait_ge(ss_dve, SS_DVE[f"ysum{g}"])
                for q in range(NT):
                    for j in range(4):
                        last = pe.transpose(PS[:, 4 + j, q * P:(q + 1) * P], YT[:, q, j * P:(j + 1) * P], IDENT[:])
                last.then_inc(ss_pe, 1)
            norm("ssm", NS)

            def attention(k_rows, at, values):
                def score(u):
                    hh, qb = u // 4, u % 4
                    if u >= 4:
                        pe.wait_ge(a_exp, at(u - 3))
                    mm(PS[:, u % 4, 0:(qb + 1) * P], QS[0:k_rows, hh, qb * P:(qb + 1) * P],
                       KS[0:k_rows, hh, 0:(qb + 1) * P]).then_inc(a_s, 1)

                def weighted(u):
                    pe.wait_ge(a_pt, at(u + 1))
                    if u >= 2:
                        pe.wait_ge(a_o, at(u - 1))
                    for kb in range(u % 4 + 1):
                        last = mm(PS[:, 6 + u % 2, 0:HD], PT[:, u % 2, kb * P:(kb + 1) * P], values(kb, u // 4),
                                  start=kb == 0, stop=kb == u % 4)
                    last.then_inc(a_pv, 1)

                for u in range(4):
                    score(u)
                for u in range(8):
                    pe.wait_ge(a_exp, at(u + 1))
                    if u >= 2:
                        pe.wait_ge(a_pt, at(u - 1))
                    for kb in range(u % 4 + 1):
                        last = pe.transpose(PS[:, 4 + u % 2, kb * P:(kb + 1) * P], PR[:, u % 2, kb * P:(kb + 1) * P], IDENT[:])
                    last.then_inc(a_t, 1)
                    if u < 4:
                        score(u + 4)
                    if u:
                        weighted(u - 1)
                weighted(7)
                pe.wait_ge(a_o, at(8))

            def heads_out():
                for c in range(4):
                    for q in range(NT):
                        last = pe.transpose(PS[:, 4 + c, q * P:(q + 1) * P], OH[:, q, c * P:(c + 1) * P], IDENT[:])
                    last.then_inc(o_t, 1)

            columns("foxqk", (HHI, HLO))
            t0, c0 = TILE0["foxv"], CHUNK0["foxv"]
            for half in range(2):
                t = t0 + half
                pe.wait_ge(s_lo, t + 1)
                w_hi, w_lo = weights(t % 2, KD, 256, 0, width=256)
                for tc in range(NT):
                    c, cols = c0 + 4 * half + tc, slice(tc * P, (tc + 1) * P)
                    pe.wait_ge(s_bank_free, c + 1)
                    exact(PS[:, c % 4, 0:256], lambda k: HHI[:, k, cols], lambda k: HLO[:, k, cols], w_hi, w_lo, KD,
                          opening=tc == 0).then_inc(s_chunk, 1)
            pe.wait_ge(s_bank_free, 4 + CHUNK0["mlac"])
            pe.wait_ge(v_out, 1)
            with pe.Fori(0, 4) as i:
                for b in range(2):
                    pe.wait_ge(q_sq, i * 2 + (b + 1))
                    last = mm(PS[:, 4 + b, :], BONES[:], SQF[:, b, :])
                last.then_inc(q_ms, 1)
                pe.wait_ge(a_qk, i + 1)
                pe.wait_ge(s_frow, i * 32 + 32)
                attention(HD + 2, lambda k: i * 8 + k, lambda kb, hh: VF[:, kb, bass.ds(i * P + hh * HD, HD)])
            heads_out()

            t0, c0 = TILE0["mlac"], CHUNK0["mlac"]
            for c in range(5):
                t, cols = t0 + c // 2, 256 if c < 4 else 128
                if c % 2 == 0:
                    pe.wait_ge(s_lo, t + 1)
                pe.wait_ge(s_bank_free, c0 + c + 1)
                exact(PS[:, (c0 + c) % 4, :], *weights(t % 2, KD, cols, (c % 2) * P), *moving(HHI, HLO), KD,
                      opening=c % 2 == 0).then_inc(s_chunk, 1)
            pe.wait_ge(o_lo, 4)
            norm("mlaq", NC)
            norm("mlakv", NC)
            rope = slice(NOPE, QK)
            pe.wait_ge(mp_dve, MP_DVE["swaps"])
            pe.wait_ge(mp_act, MP_ACT["krope"])
            mm(PS[rope, 6, :], SW[rope, 1, :], KRR[rope, :]).then_inc(mp_pe, 1)
            pe.wait_ge(mp_dve, MP_DVE["krot"])
            pe.wait_ge(mp_act, MP_ACT["trig"])
            pe.wait_ge(n_lo, LO_BEFORE["ffn2"])
            pe.wait_ge(s_bank_free, 4 + CHUNK0["merge"])
            t0 = TILE0["mlahead"]
            with pe.Fori(0, 2) as i:
                for j in range(2):
                    def at(k, n=8):
                        return i * (2 * n) + (n * j + k)

                    slot = (t0 + j) % 2
                    pe.wait_ge(s_lo, i * 2 + (t0 + j + 1))
                    for hh in range(2):
                        exact(PS[0:QK, 2 * hh, :], *weights(slot, 3, 192, hh * QK, width=QK), *moving(CQHI, CQLO), 3,
                              opening=hh == 0)
                        exact(PS[:, 2 * hh + 1, :], *weights(slot, 2, 256, hh * P, offset=576), *moving(CQHI, CQLO, 3), 2)
                    v_hi, v_lo = (wtile(w, slot, 2, 256, 576).rearrange("p k (h n) -> p k h n", n=P)[:, :, :, HD:P]
                                  for w in (WHI, WLO))
                    for tc in range(NT):
                        cols = slice(tc * P, (tc + 1) * P)
                        last = exact(PS[:, 7, cols].rearrange("p (h n) -> p h n", n=HD), lambda k: CQHI[:, 3 + k, cols],
                                     lambda k: CQLO[:, 3 + k, cols], lambda k: v_hi[:, k], lambda k: v_lo[:, k], 2)
                    last.then_inc(mh_pe, 1)
                    pe.wait_ge(mh_act, at(MH_ACT["raw"], 3))
                    for hh in range(2):
                        if hh:
                            pe.wait_ge(mh_act, at(MH_ACT["r0"], 3))
                            pe.wait_ge(mh_dve, at(MH_DVE["qk0"], 2))
                        for b in range(2):
                            mm(PS[0:QK, 4 + b, :], ONES[0:QK, 0:QK], SQM[0:QK, 2 * hh + b, :])
                        mm(PS[rope, 6, :], SW[rope, 0, :], QR[rope, hh, :]).then_inc(mh_pe, 1)
                    pe.wait_ge(mh_dve, at(MH_DVE["qk1"], 2))
                    attention(QK, lambda k: at(k + 32), lambda kb, hh: VM[:, kb, hh * HD:(hh + 1) * HD])
            heads_out()

            t0, c0 = TILE0["merge"], CHUNK0["merge"]
            pe.wait_ge(o_lo, 8)
            with pe.Fori(0, 2) as i:
                for pair in range(2):
                    t, c = t0 + 5 * pair, c0 + 12 * pair
                    plan = ((0, 0, KD, 0, (HHI, HLO)), (1, 2, KD, 0, (HHI, HLO)), (2, 4, 4, 0, (YMHI, YMLO)),
                            (2, 6, 4, 1024, (YFHI, YFLO)), (3, 8, KD, 0, (HHI, HLO)), (4, 10, KD, 0, (YS2HI, YS2LO)))
                    for j, first, kts, offset, rhs in plan:
                        if offset == 0:
                            pe.wait_ge(s_lo, i * 10 + (t + j + 1))
                        if j == 4:
                            pe.wait_ge(s_reload, 32)
                        for m in range(2):
                            n = c + first + m
                            pe.wait_ge(s_bank_free, i * 24 + (n + 1))
                            exact(PS[:, n % 4, :], *weights((t + j) % 2, kts, 256, m * P, offset=offset), *moving(*rhs), kts,
                                  opening=m == 0 and offset == 0).then_inc(s_chunk, 1)
            pe.wait_ge(g_lo, 9)
            columns("wout2", (MGHI, MGLO))
            norm("ffn2", NRM)
            pe.wait_ge(n_lo, LO_BEFORE["ffn2"] + KD)
            columns("up2", (HHI, HLO))
            pe.wait_ge(f_lo, 2 * NF)
            down("down2")
            pe.wait_ge(s_x, X_DOWN2 + KD)
            for n in range(8):
                for c in range(4):
                    last = pe.transpose(PS[:, n, c * P:(c + 1) * P], X[:, 4 * (n % 2) + c, (n // 2) * P:(n // 2 + 1) * P],
                                        IDENT[:])
                last.then_inc(s_ot, 1)


def kernel(**inputs):
    import concourse.bacc as bacc
    from concourse.bass_utils import run_bass_kernel_spmd

    nc = bacc.Bacc("TRN2", target_bir_lowering=False, num_devices=1)
    arrays = {name: np.ascontiguousarray(inputs[name]) for name in INPUTS}
    arrays["inv_freq"] = inv_freq()
    dram = {name: nc.dram_tensor(name, a.shape, mybir.dt.from_np(a.dtype), kind="ExternalInput").ap()
            for name, a in arrays.items()}
    out = nc.dram_tensor("out", (1, S, D), F32, kind="ExternalOutput").ap()
    build(nc, dram, out)
    result = run_bass_kernel_spmd(nc, [arrays], core_ids=[0])
    return result.results[0]["out"]
```

```python
from contextlib import ExitStack

import numpy as np
import concourse.bass as bass
from concourse import mybir

F32 = mybir.dt.float32
F32R = mybir.dt.float32r
I32 = mybir.dt.int32
ACT = mybir.ActivationFunctionType
ALU = mybir.AluOpType
AX = mybir.AxisListType.X

P = 128
S = 512
NT = S // P
D = 1024
KD = D // P
DFF = 2816
NF = DFF // P
EPS = 1e-6
HD = 64
RG, HG, SC = 3, 3, 2
A_U, A_GATE, B_Q, B_F, B_V, B_G, C_B, C_C, C_V = 0, 3, 6, 9, 12, 15, 18, 20, 22
N_PROJ = 24
PLE = 256
MLA_Q, MLA_KV, ROPE = 384, 256, 32
NOPE, QK = 64, 96
COL_KROPE = MLA_Q + MLA_KV
COL_FOX = COL_KROPE + ROPE
FOX = 512
COL_F = COL_FOX + 3 * FOX
COL_Z = COL_F + 8
SSM = 1024
COL_XBC = COL_Z + SSM
NXBC = 12
COL_DT = COL_XBC + NXBC * P
COL_GATE = COL_DT + 16
HEADS = 16
NEG = -1e30
WT = 2048

INPUTS = [
    "x", "p", "norm_mix_gain", "w_in", "rg_conv_w", "rg_conv_b", "rg_w_r", "rg_b_r", "rg_w_i", "rg_b_i",
    "rg_lambda", "hg_lower_bounds", "sc_conv_w", "mix_out_gain", "w_out", "norm_ffn_gain", "ffn_w_up",
    "ffn_conv_w", "ffn_w_down", "ple_w_proj", "ple_w_gate", "final_norm_gain", "positions_2", "norm_mix_g_2",
    "w_in_2", "b_gate_2", "mla_q_norm_g_2", "mla_w_uq_2", "mla_kv_norm_g_2", "mla_w_ukv_2", "mla_q_gain_2",
    "mla_k_gain_2", "fox_q_gain_2", "fox_k_gain_2", "fox_b_f_2", "ssm_conv_w_2", "ssm_conv_b_2",
    "ssm_dt_bias_2", "ssm_A_log_2", "ssm_D_2", "ssm_norm_g_2", "w_br_mla_2", "w_br_fox_2", "w_br_ssm_2",
    "w_out_2", "norm_ffn_g_2", "ffn_w_up_2", "ffn_conv_w_2", "ffn_conv_b_2", "ffn_w_down_2",
]

PARAM_ROWS = [
    (0, "norm_mix_gain", 8, 0), (0, "rg_conv_w", 12, 0), (0, "rg_conv_b", 3, 0), (0, "rg_b_r", 3, 0),
    (0, "rg_b_i", 3, 0), (0, "rg_lambda", 3, 0), (0, "hg_lower_bounds", 3, 0), (0, "sc_conv_w", 6, 0),
    (0, "mix_out_gain", 8, 0), (0, "norm_ffn_gain", 8, 0), (0, "final_norm_gain", 8, 0),
    (0, "norm_mix_g_2", 8, 0), (0, "b_gate_2", 24, 0), (0, "mla_q_norm_g_2", 3, 0), (0, "mla_kv_norm_g_2", 2, 0),
    (0, "ssm_conv_b_2", 12, 0), (0, "ssm_norm_g_2", 8, 0),
    (1, "ssm_conv_w_2", 48, 0), (1, "norm_ffn_g_2", 8, 0), (1, "ffn_conv_b_2", 44, 0),
    (2, "ffn_conv_w", 88, 0), (3, "ffn_conv_w", 44, 88), (3, "ffn_conv_w_2", 44, 0), (4, "ffn_conv_w_2", 88, 44),
]


def param_columns():
    col, used = {}, [0] * 5
    for tile, name, rows, first in PARAM_ROWS:
        col[name, first] = tile * P + used[tile]
        used[tile] += rows
    return col, used


PCOL, PUSED = param_columns()


def pc(name, first=0):
    return PCOL[name, first]


FFN_TAP = {
    1: [pc("ffn_conv_w"), pc("ffn_conv_w") + 44, pc("ffn_conv_w", 88)],
    2: [pc("ffn_conv_w_2"), pc("ffn_conv_w_2", 44), pc("ffn_conv_w_2", 44) + 44],
}

STAGES = [
    ("proj1", 12, 24), ("wout1", 4, 8), ("up1", 22, 44), ("down1", 12, 8), ("pleproj", 1, 8), ("plegate", 4, 8),
    ("small", 1, 1), ("xbc", 6, 12), ("z", 4, 8), ("foxqk", 4, 8), ("foxv", 2, 8), ("mlac", 3, 5),
    ("mlahead", 4, 0), ("merge", 20, 48), ("wout2", 4, 8), ("up2", 22, 44), ("down2", 12, 8),
]


def stage_bases():
    tile, chunk, t, c = {}, {}, 0, 0
    for name, tiles, chunks in STAGES:
        tile[name], chunk[name] = t, c
        t, c = t + tiles, c + chunks
    return tile, chunk, t


TILE0, CHUNK0, N_TILES = stage_bases()
TILES = {name: tiles for name, tiles, _ in STAGES}
PER_LOAD = 32
DOWN_PARTS = ((0, 8), (8, 8), (16, 6))
SUFFIX = {1: "", 2: "_2"}

LEVELS = 7


def counted(names):
    return {n: i + 1 for i, n in enumerate(names.split())}


SMALL_W = 80
SS_DVE = counted("v dl packed tok xdw0 h0 yt0 ysum0 y0 xdw1 h1 yt1 ysum1 y1")
SS_ACT = counted("raw e silu pexp dec bt0 bt1")
SS_PE = counted("tok turned0 states0 yoff0 yturned0 turned1 states1 yoff1 yturned1")
MP_ACT = counted("squares trig")
MP_DVE = counted("swaps angles krot")
MP_PE = counted("kswap")
TWO_PI = 2 * np.pi
TWO_PI_PARTS = [6.28125, 0.0019340515136718750, 1.255665914e-06]
PI_BELOW = 3.1415925
ROUNDING = 12582912.0


def inv_freq():
    inv = (1.0 / (np.float32(10000.0) ** (np.arange(0, ROPE, 2, dtype=np.float32) / np.float32(ROPE)))).astype(np.float32)
    return np.ascontiguousarray(np.concatenate([inv, inv])[:, None])

LOG_EXP = "natural_log_exp_and_others"
SMALL_LOADS = 16 * 16


NORMS = [("mix1", 8), ("ffn1", 8), ("final", 8), ("mix2", 8), ("ssm", 8), ("mlaq", 3), ("mlakv", 2), ("ffn2", 8)]
NORM_USE = {name: i for i, (name, _) in enumerate(NORMS)}
NORM_N = dict(NORMS)
LO_BEFORE = {name: sum(n for m, n in NORMS[:i] if m != "final") for i, (name, _) in enumerate(NORMS)}
STREAMED = ("ffn1", "final", "ffn2")
SQ_BASE = {name: sum(n for m, n in NORMS[:i] if m not in STREAMED) for i, (name, _) in enumerate(NORMS)}
NORM_BASE = {name: sum(n for _, n in NORMS[:i]) for i, (name, _) in enumerate(NORMS)}
X_IN, X_WOUT1, X_DOWN1, X_PLE, X_WOUT2, X_DOWN2 = 0, 8, 16, 24, 32, 40

RG_DVE = counted("u b2 recurrence gated")
RG_ACT = counted("r_sigmoid sigmoids exps beta gelus")
RG_PE = counted("r_gate i_gate")
HG_ACT = counted("q_sigmoid logf e0 e1 e2 e3 e4 e5 e6 decays v_turned out")
HG_DVE = counted("qk d0 d1 m0 d2 m1 c0 d3 m2 c1 d4 m3 c2 d5 m4 c3 d6 m5 c4 m6 c5 dk c6 gated c7 state")
HG_PE = counted("g0 g1 g2 g3 g4 g5 g6 g7 turned states out")


def build(nc, dram, out):
    ctx = ExitStack()
    with ctx:
        def sem(name):
            return ctx.enter_context(nc.semaphore(name))

        base = -(-nc.sbuf_base // 64) * 64
        place = {"at": base}

        def fixed(name, shape, dt=F32):
            words = int(np.prod(shape[1:]))
            t = nc.alloc_sbuf_tensor_at(name, shape, dt, offset=place["at"])
            place["at"] += -(-words * 4 // 64) * 64
            return t

        X = fixed("X", [P, KD, S])
        WRAW = fixed("WRAW", [P, 2, WT])
        WHI = fixed("WHI", [P, 2, WT], F32R)
        WLO = fixed("WLO", [P, 2, WT], F32R)
        HHI = fixed("HHI", [P, KD, S], F32R)
        HLO = fixed("HLO", [P, KD, S], F32R)
        IDENT = fixed("IDENT", [P, P])
        ONES = fixed("ONES", [P, P])
        gb_at = place["at"]
        BONES = fixed("BONES", [P, P])
        TRI = fixed("TRI", [P, P])
        CAUSAL = fixed("CAUSAL", [P, P])
        CHUNKED = fixed("CHUNKED", [P, P])
        reset_at = place["at"]
        RESET = fixed("RESET", [P, S])
        PRM = fixed("PRM", [P, 5 * P])
        EPSC = fixed("EPSC", [P, 1])
        CNEG = fixed("CNEG", [P, 2, RG])
        LOWB = fixed("LOWB", [P, 2, HG])
        SOFT = fixed("SOFT", [P, 4, RG])
        QKG = fixed("QKG", [P, 4])
        DSKIP = fixed("DSKIP", [P, KD])
        SMB = fixed("SMB", [P, 3])
        INVF = fixed("INVF", [P, 1])
        r_at = place["at"]
        R = fixed("R", [P, S])
        LNT = fixed("LNT", [P, S])
        arena = place["at"]

        def at(name, kb, shape, dt=F32):
            return nc.alloc_sbuf_tensor_at(name, shape, dt, offset=arena + int(kb * 1024))

        NRM = at("NRM", 0, [P, KD, S])
        PROWS = at("PROWS", 16, [P, 5, P])
        XTOK = at("XTOK", 20, [P, NT, D])
        Z = at("Z", 0, [P, N_PROJ, S])
        YP = at("YP", 48, [P, KD, S])
        HMASK = at("HMASK", 64, [P, LEVELS + 1, P], I32)
        WR = at("WR", 68, [P, RG, P])
        WI = at("WI", 69.5, [P, RG, P])
        RR = at("RR", 71, [P, RG, S])
        IG = at("IG", 77, [P, RG, S])
        TH = at("TH", 83, [P, RG, S])
        AD = at("AD", 89, [P, RG, S])
        MSCR = at("MSCR", 71, [P, 10, P])
        MSCRI = at("MSCRI", 77, [P, 2, P], I32)
        HQ = at("HQ", 71, [P, S])
        HK = at("HK", 73, [P, S])
        HG_ = at("HG_", 75, [P, S])
        HDD = at("HDD", 77, [P, 2, S])
        HM = at("HM", 81, [P, 2, S])
        HST = at("HST", 85, [P, 2, S])
        HVT = at("HVT", 89, [P, NT, P])
        HKD = at("HKD", 91, [P, S])
        HKDT = at("HKDT", 93, [P, NT, P])
        HQG = at("HQG", 95, [P, S])
        HVS = at("HVS", 97, [P, S])
        HS = at("HS", 0, [P, 3, P])
        HEGL = at("HEGL", 1.5, [P, NT])
        SQ1 = at("SQ1", 0, [P, KD, S])
        FHI = at("FHI", 0, [P, NF, S], F32R)
        FLO = at("FLO", 44, [P, NF, S], F32R)
        FG = at("FG", 88, [P, 2, S])
        FU = at("FU", 92, [P, 2, S])
        PTOK = at("PTOK", 92, [P, NT, PLE])
        PHI = at("PHI", 16, [P, 2, S], F32R)
        PLO = at("PLO", 20, [P, 2, S], F32R)
        PP = at("PP", 24, [P, KD, S])
        PG = at("PG", 40, [P, 2, S])
        OTOK = at("OTOK", 16, [P, NT, D])

        YSHI = at("YSHI", 0, [P, KD, S], F32R)
        YSLO = at("YSLO", 16, [P, KD, S], F32R)
        XD = at("XD", 0, [P, NT, S])
        XW = at("XW", 8, [P, NT, S])
        SH = at("SH", 16, [P, 3, S])
        YT = at("YT", 22, [P, NT, S])
        SMT = at("SMT", 0, [P, 5, S])
        XBC = at("XBC", 32, [P, NXBC, S])
        ZS = at("ZS", 56, [P, KD, S])
        CBM = at("CBM", 72, [P, S])
        BT = at("BT", 74, [P, NT, P])
        ABC = at("ABC", 76, [P, 2, S])
        DM = at("DM", 80, [P, 2, S])
        TOK = at("TOK", 84, [P, NT, P])
        PACK = at("PACK", 86, [P, S])
        DEC = at("DEC", 88, [P, HEADS, NT])
        SMC = at("SMC", 90, [P, S])
        CUM = at("CUM", 92, [P, S])
        NS = at("NS", 72, [P, KD, S])
        YFHI = at("YFHI", 0, [P, 4, S], F32R)
        YFLO = at("YFLO", 8, [P, 4, S], F32R)
        YMHI = at("YMHI", 32, [P, 4, S], F32R)
        YMLO = at("YMLO", 40, [P, 4, S], F32R)
        PR = at("PR", 16, [P, 2, S])
        PT = at("PT", 20, [P, 2, S])
        OH = at("OH", 24, [P, NT, S])
        QS = at("QS", 76, [P, 4, S])
        KS = at("KS", 84, [P, 4, S])
        NMX = at("NMX", 98.5, [P, 3, 8])
        QKR = at("QKR", 32, [P, 8, S])
        VF = at("VF", 48, [P, NT, S])
        SQF = at("SQF", 56, [P, 2, S])
        RF = at("RF", 60, [P, 2, S])
        CQHI = at("CQHI", 16, [P, 5, S], F32R)
        CQLO = at("CQLO", 26, [P, 5, S], F32R)
        CR = at("CR", 36, [P, 5, S])
        ANG = at("ANG", 56, [P, 4, S])
        NC = at("NC", 84, [P, 3, S])
        QA = at("QA", 36, [P, 8, S])
        KA = at("KA", 52, [P, 8, S])
        VA = at("VA", 68, [P, NT, S])
        SQM = at("SQM", 76, [P, 4, S])
        QR = at("QR", 84, [P, 2, S])
        KR = at("KR", 88, [P, 2, S])
        CG = at("CG", 92, [P, S])
        POSI = at("POSI", 94, [P, S], I32)
        SIN = at("SIN", 94, [P, S])
        KROT = at("KROT", 96, [P, S])
        SW = at("SW", 98, [P, 2, ROPE])
        MR = nc.alloc_sbuf_tensor_at("MR", [P, S], F32, offset=reset_at)
        RS2 = nc.alloc_sbuf_tensor_at("RS2", [P, 2, S], F32, offset=r_at)
        YS2HI = at("YS2HI", 48, [P, KD, S], F32R)
        YS2LO = at("YS2LO", 64, [P, KD, S], F32R)
        MGHI = at("MGHI", 80, [P, KD, S], F32R)
        MGLO = at("MGLO", 16, [P, KD, S], F32R)
        GA = nc.alloc_sbuf_tensor_at("GA", [P, 2, S], F32, offset=r_at)
        GB = nc.alloc_sbuf_tensor_at("GB", [P, 2, S], F32, offset=gb_at)

        acum_d = nc.dram_tensor("acum_d", (HEADS, S), F32).ap()
        alast_d = nc.dram_tensor("alast_d", (HEADS, NT), F32).ap()
        fsum_d = nc.dram_tensor("fsum_d", (2, 8, S), F32).ap()
        yshi_d = nc.dram_tensor("yshi_d", (P, KD, S), F32R).ap()
        yslo_d = nc.dram_tensor("yslo_d", (P, KD, S), F32R).ap()

        x_acc, s_signs = sem("x_acc"), sem("s_signs")
        ss_dve, ss_act, ss_pe = sem("ss_dve"), sem("ss_act"), sem("ss_pe")
        s_rows, s_dec, s_spill, s_pos = sem("s_rows"), sem("s_dec"), sem("s_spill"), sem("s_pos")
        s_abc = [sem("s_abc0"), sem("s_abc1")]
        h_dfree, h_d, h_e, h_m, h_y = (sem(f"h_{x}") for x in "dfree d e m y".split())
        a_s, a_mx, a_exp, a_t, a_pt, a_pv, a_o = (sem(f"a_{x}") for x in "s mx exp t pt pv o".split())
        a_ready = sem("a_ready")
        s_frow = [sem("s_frow0"), sem("s_frow1")]
        q_sq, q_ms, q_r, q_done, v_out = (sem(x) for x in "q_sq q_ms q_r q_done v_out".split())
        o_t, o_hi, o_lo = sem("o_t"), sem("o_hi"), sem("o_lo")
        mp_act, mp_dve, mp_pe = sem("mp_act"), sem("mp_dve"), sem("mp_pe")
        mh_p, mh_sq, mh_free, mh_ms, mh_r, mh_qk, mh_v, mh_va = (sem(f"mh_{x}") for x in "p sq free ms r qk v va".split())
        g_sig, g_mid, g_sum, g_hi, g_lo = (sem(f"g_{x}") for x in "sig mid sum hi lo".split())
        s_oa = sem("s_oa")
        s_reload, s_fcols = sem("s_reload"), sem("s_fcols")

        PS = ctx.enter_context(nc.psum_tensor("PS", [P, 8, S], F32))

        s_raw = [sem("s_raw0"), sem("s_raw1")]
        s_hi, s_lo, s_started = sem("s_hi"), sem("s_lo"), sem("s_started")
        s_chunk, s_bank_free = sem("s_chunk"), sem("s_bank_free")
        n_sq, n_ms, n_r, n_h, n_hi, n_lo = (sem(f"n_{x}") for x in "sq ms r h hi lo".split())
        s_x, n_sum = sem("s_x"), sem("n_sum")
        s_const, s_mask, s_zeroed, s_params, s_pt, s_ptc, s_setup_a, s_setup_v = (
            sem(x) for x in "s_const s_mask s_zeroed s_params s_pt s_ptc s_setup_a s_setup_v".split())
        s_xin, s_xt, s_small = sem("s_xin"), sem("s_xt"), sem("s_small")
        rg_dve, rg_act, rg_pe = sem("rg_dve"), sem("rg_act"), sem("rg_pe")
        sc_done = sem("sc_done")
        hg_act, hg_dve, hg_pe = sem("hg_act"), sem("hg_dve"), sem("hg_pe")
        hn_sq, hn_ps, hn_r, hn_g, hn_y, hn_hi, hn_lo = (sem(f"hn_{x}") for x in "sq ps r g y hi lo".split())
        f_acc, f_tap, f_silu, f_prod, f_hi, f_lo = (sem(f"f_{x}") for x in "acc tap silu prod hi lo".split())
        e_hi, e_lo, e_p, e_pt, e_phi, e_plo, e_pp, e_g = (
            sem(f"e_{x}") for x in "hi lo p pt phi plo pp g".split())
        s_ot, s_oc, s_out = sem("s_ot"), sem("s_oc"), sem("s_out")

        def f32(t):
            return t.bitcast(F32)

        def wtile(tensor, slot, kts, cols, offset=0):
            return tensor[:, slot, offset:offset + kts * cols].rearrange("p (k n) -> p k n", n=cols)

        def rows(w):
            return w.rearrange("o (k p) n -> p (o k) n", p=P)

        block = ctx.enter_context(nc.Block())

        @block.sync
        def _(sp):
            def load(t, slot, kts, cols, src):
                if not isinstance(t, int) or t >= 2:
                    sp.wait_ge(s_lo, t - 1)
                half = kts // 2
                for k in (slice(0, half), slice(half, kts)):
                    sp.dma_start(wtile(WRAW, slot, kts, cols)[:, k, :], src[:, k, :]).then_inc(s_raw[slot], 16)

            def columns(name, w, at=0, skip=0):
                t0 = TILE0[name]
                with sp.Fori(skip // 2, TILES[name] // 2) as i:
                    for j in range(2):
                        col = sp.snap(i * 512 + (at + j * 256))
                        load(i * 2 + (t0 + j), (t0 + j) % 2, KD, 256, w[:, :, bass.ds(col, 256)])

            def ffn(n):
                up, down = rows(dram["ffn_w_up" + SUFFIX[n]]), rows(dram["ffn_w_down" + SUFFIX[n]])
                t0 = TILE0[f"up{n}"]
                with sp.Fori(0, NF // 2) as i:
                    for j in range(2):
                        col = sp.snap(i * 256 + j * DFF)
                        load(i * 2 + (t0 + j), (t0 + j) % 2, KD, 256, up[:, :, bass.ds(col, 256)])
                t0 = TILE0[f"down{n}"]
                with sp.Fori(0, 2) as i:
                    for half in range(2):
                        for part, (k0, kts) in enumerate(DOWN_PARTS):
                            j = 3 * half + part
                            col = sp.snap(i * 512 + half * 256)
                            load(i * 6 + (t0 + j), (t0 + j) % 2, kts, 256, down[:, k0:k0 + kts, bass.ds(col, 256)])

            for tile, name, n, first in PARAM_ROWS:
                a = dram[name]
                form, sizes = {1: "(r p) -> r p", 2: "o (c p) -> (o c) p", 3: "o k (c p) -> (o k c) p"}[len(a.shape)], {"p": P}
                if name in ("rg_b_r", "rg_b_i"):
                    form, sizes = "o (c a) d -> (o c) (a d)", {"a": 2}
                row = pc(name, first) - tile * P
                sp.dma_start(PROWS[row:row + n, tile, :], a.rearrange(form, **sizes)[first:first + n, :]
                             ).then_inc(s_params, 16)
            for q in range(NT):
                sp.dma_start(XTOK[:, q, :], dram["x"][0, q * P:(q + 1) * P, :]).then_inc(s_xin, 16)
            w_in = rows(dram["w_in"])
            sp.wait_ge(s_zeroed, 1)
            for t in range(2):
                load(t, t, KD, 256, w_in[:, :, t * 256:(t + 1) * 256])
            for h in range(2):
                for to, name in ((WR, "rg_w_r"), (WI, "rg_w_i")):
                    sp.dma_start(to[h * HD:(h + 1) * HD, :, h * HD:(h + 1) * HD],
                                 dram[name].rearrange("o (c a) d e -> a d (o c) e", a=2)[h]).then_inc(s_small, 16)
            sp.wait_ge(s_signs, 1)
            one_column = "o d -> d o"
            for to, name in ((SMB[32:40, 0:1], "fox_b_f_2"), (SMB[64:80, 0:1], "ssm_dt_bias_2"), (SMB[64:80, 2:3], "ssm_A_log_2"),
                             (QKG[0:64, 0:1], "fox_q_gain_2"), (QKG[64:128, 0:1], "fox_q_gain_2"),
                             (QKG[0:64, 1:2], "fox_k_gain_2"), (QKG[64:128, 1:2], "fox_k_gain_2"),
                             (QKG[0:QK, 2:3], "mla_q_gain_2"), (QKG[0:QK, 3:4], "mla_k_gain_2")):
                sp.dma_start(to, dram[name].rearrange(one_column)).then_inc(s_small, 16)
            for h in range(2):
                with nc.allow_non_contiguous_dma("16 words in all"):
                    sp.dma_start(DSKIP[h * HD:(h + 1) * HD, :],
                                 dram["ssm_D_2"].rearrange("o (c h) -> h o c", h=2)[h].broadcast_to([HD, KD])
                                 ).then_inc(s_small, 16)
            sp.dma_start(INVF[NOPE:QK, :], dram["inv_freq"]).then_inc(s_small, 16)
            columns("proj1", w_in, skip=2)
            columns("wout1", rows(dram["w_out"]))
            ffn(1)
            for q in range(NT):
                sp.dma_start(PTOK[:, q, :], dram["p"][0, 0, q * P:(q + 1) * P, :]).then_inc(e_p, 16)
            t = TILE0["pleproj"]
            load(t, t % 2, 2, D, rows(dram["ple_w_proj"]))
            columns("plegate", rows(dram["ple_w_gate"]))
            w_in2 = rows(dram["w_in_2"])
            t = TILE0["small"]
            sp.wait_ge(s_lo, t - 1)
            small = wtile(WRAW, t % 2, KD, SMALL_W)
            sp.dma_start(small[:, :, ROPE:64], w_in2[:, :, COL_F:COL_F + 32]).then_inc(s_fcols, 16)
            sp.wait_ge(s_fcols, 16)
            sp.dma_start(small[:, :, 0:ROPE], w_in2[:, :, COL_KROPE:COL_KROPE + ROPE]).then_inc(s_raw[t % 2], 16)
            sp.dma_start(small[:, :, 64:80], w_in2[:, :, COL_DT:COL_DT + 16]).then_inc(s_raw[t % 2], 16)
            columns("xbc", w_in2, at=COL_XBC)
            columns("z", w_in2, at=COL_Z)
            columns("foxqk", w_in2, at=COL_FOX)
            columns("foxv", w_in2, at=COL_FOX + 2 * FOX)
            t = TILE0["mlac"]
            for j, width in enumerate((256, 256, 128)):
                load(t + j, (t + j) % 2, KD, width, w_in2[:, :, j * 256:j * 256 + width])
            uq, ukv = rows(dram["mla_w_uq_2"]), rows(dram["mla_w_ukv_2"])
            t0 = TILE0["mlahead"]
            with sp.Fori(0, 2) as i:
                for j in range(2):
                    t, slot = i * 2 + (t0 + j), (t0 + j) % 2
                    q_col, kv_col = sp.snap(i * 384 + j * 192), sp.snap(i * 512 + j * 256)
                    t_free = sp.snap(t - 1)
                    sp.wait_ge(s_lo, t_free)
                    sp.dma_start(wtile(WRAW, slot, 3, 192), uq[:, :, bass.ds(q_col, 192)]).then_inc(s_raw[slot], 16)
                    sp.dma_start(wtile(WRAW, slot, 2, 256, offset=576), ukv[:, :, bass.ds(kv_col, 256)]
                                 ).then_inc(s_raw[slot], 16)
            br_mla, br_fox, br_ssm = (rows(dram[f"w_br_{n}_2"]) for n in ("mla", "fox", "ssm"))
            t0 = TILE0["merge"]
            with sp.Fori(1, 3) as i:
                for pair in range(2):
                    col = sp.snap(i * 512 + (pair * 256 - 512))
                    for j, b in ((0, 0), (1, 1), (2, None), (3, 2), (4, None)):
                        n = t0 + 5 * pair + j
                        t, slot = i * 10 + (n - 10), n % 2
                        if b is not None:
                            gate_col = sp.snap(i * 512 + (COL_GATE + b * D + pair * 256 - 512))
                            load(t, slot, KD, 256, w_in2[:, :, bass.ds(gate_col, 256)])
                        elif j == 4:
                            load(t, slot, KD, 256, br_ssm[:, :, bass.ds(col, 256)])
                        else:
                            sp.wait_ge(s_lo, t - 1)
                            for k, w in enumerate((br_mla, br_fox)):
                                sp.dma_start(wtile(WRAW, slot, 4, 256, offset=k * 1024), w[:, :, bass.ds(col, 256)]
                                             ).then_inc(s_raw[slot], 16)
            columns("wout2", rows(dram["w_out_2"]))
            ffn(2)
            for q in range(NT):
                sp.wait_ge(s_oc, q + 1)
                sp.wait_ge(s_oa, q + 1)
                sp.dma_start(out[0, q * P:(q + 1) * P, :], OTOK[:, q, :]).then_inc(s_out, 16)
            sp.wait_ge(s_out, 16 * NT)

        @block.gpsimd
        def _(pool):
            def select(t, pattern, fill, op=ALU.is_ge, cm=1, base=0):
                return pool.affine_select(out=t, in_=t, compare_op=op, fill=fill, base=base, pattern=pattern,
                                          channel_multiplier=cm)

            for t in (WRAW, WR, WI, SMB, QKG, INVF, DSKIP):
                pool.memset(t[:], 0.0)
            pool.drain().then_inc(s_zeroed, 1)
            for t, v in ((SMB[0:64, 1:3], -1.0), (SMB[64:P, 1:2], 1.0)):
                pool.memset(t, v)
                pool.drain()
            pool.drain().then_inc(s_signs, 1)
            pool.drain().then_inc(s_bank_free, 4)
            for t, v in ((IDENT, 0.0), (ONES, 1.0), (BONES, 0.0), (TRI, 1.0), (CAUSAL, 0.0), (CHUNKED, 0.0),
                         (RESET, 1.0), (EPSC, EPS)):
                pool.memset(t[:], v)
            pool.iota(MSCRI[:, 0, :], pattern=[[1, P]], base=0, channel_multiplier=0)
            pool.iota(MSCRI[:, 1, :], pattern=[[0, P]], base=0, channel_multiplier=1)
            pool.drain()
            select(IDENT[:], [[-1, P]], 1.0, op=ALU.not_equal)
            select(TRI[:], [[1, P]], 0.0, cm=-1)
            select(CAUSAL[:], [[-1, P]], NEG)
            for t, v in ((CHUNKED[0:HD, HD:P], NEG), (BONES[0:HD, 0:HD], 1.0), (BONES[HD:P, HD:P], 1.0)):
                pool.drain()
                pool.memset(t, v)
            pool.drain()
            for q in range(NT):
                pool.memset(RESET[:, q * P:q * P + 1], 0.0)
            pool.drain().then_inc(s_const, 1)
            pool.wait_ge(s_mask, 1)
            select(MSCR[:, 9, :], [[1, P]], 4096.0, cm=-1).then_inc(s_mask, 1)

            def sum_squares(name, first):
                pool.wait_ge(n_h, NORM_BASE[name])
                pool.wait_ge(s_x, first + 1)
                pool.tensor_tensor(R[:], X[:, 0, :], X[:, 0, :], ALU.mult)
                with pool.Fori(0, KD - 1) as i:
                    xc = X[:, bass.ds(i + 1, 1), :]
                    pool.wait_ge(s_x, i + (first + 2))
                    pool.tensor_tensor(LNT[:].unsqueeze(1), xc, xc, ALU.mult)
                    pool.drain()
                    pool.tensor_tensor(R[:], R[:], LNT[:], ALU.add)
                    pool.drain()
                pool.drain().then_inc(n_sum, 1)

            sum_squares("ffn1", X_WOUT1)
            sum_squares("final", X_PLE)

            pool.wait_ge(e_pt, 1)
            pool.dma_start(POSI[NOPE:QK, :], dram["positions_2"].broadcast_to([ROPE, S])).then_inc(s_pos, 16)
            pool.wait_ge(ss_dve, SS_DVE["dl"])
            pool.dma_start(acum_d, CUM[64:80, :]).then_inc(s_rows, 16)
            with nc.allow_non_contiguous_dma("64 words"):
                pool.dma_start(alast_d, CUM[64:80, P - 1:S:P]).then_inc(s_rows, 16)
            pool.dma_start(fsum_d[0], CUM[32:40, :]).then_inc(s_rows, 16)
            pool.dma_start(fsum_d[1], SMT[32:40, 4, :]).then_inc(s_rows, 16)
            pool.wait_ge(s_rows, 64)
            pool.dma_start(DEC[:].rearrange("p h q -> p (h q)"),
                           alast_d.rearrange("h q -> (h q)").unsqueeze(0).broadcast_to([P, HEADS * NT])
                           ).then_inc(s_dec, 16)
            with pool.Fori(0, HEADS // 2) as i:
                for b in range(2):
                    pool.wait_ge(h_dfree, i * 2 + (b + 1))
                    pool.dma_start(ABC[:, b, :], acum_d[bass.ds(i * 2 + b, 1), :].broadcast_to([P, S])).then_inc(s_abc[b], 16)
            pool.wait_ge(n_lo, LO_BEFORE["ssm"] + KD)
            pool.dma_start(yshi_d, YSHI[:]).then_inc(s_spill, 16)
            pool.dma_start(yslo_d, YSLO[:]).then_inc(s_spill, 16)
            pool.memset(QS[64:96, :, :], 1.0)
            pool.memset(KS[64:96, :, :], 1.0)
            pool.drain()
            with pool.Fori(0, 2) as i:
                for j in range(2):
                    slots = slice(2 * j, 2 * j + 2)
                    pool.wait_ge(a_s, i * 16 + (8 * j + 8))
                    pool.wait_ge(q_done, i * 2 + (j + 7))
                    pool.dma_start(QS[65:66, slots, :], fsum_d[0:1, bass.ds(i * 4 + 2 * j, 2), :]).then_inc(s_frow[j], 16)
                    pool.dma_start(KS[64:65, slots, :], fsum_d[1:2, bass.ds(i * 4 + 2 * j, 2), :]).then_inc(s_frow[j], 16)
                    for hh in range(2):
                        b = slice(hh * HD, (hh + 1) * HD)
                        for to, first in ((QS, j), (KS, 4 + j)):
                            pool.tensor_copy(to[0:HD, 2 * j + hh:2 * j + hh + 1, :], QKR[b, bass.ds(i * 2 + first, 1), :])
                    pool.drain().then_inc(a_ready, 1)
            pool.wait_ge(mh_qk, 10)
            pool.wait_ge(mh_ms, 10)
            with pool.Fori(0, 2) as i:
                for j in range(2):
                    pool.wait_ge(a_s, i * 16 + (8 * j + 40))
                    for hh in range(2):
                        for to, of in ((QS, QA), (KS, KA)):
                            pool.tensor_copy(to[0:QK, 2 * j + hh:2 * j + hh + 1, :], of[0:QK, bass.ds(i * 4 + (2 * j + hh), 1), :])
                    pool.drain().then_inc(a_ready, 1)
            pool.wait_ge(a_o, 64)
            pool.wait_ge(s_spill, 32)
            pool.dma_start(YS2HI[:], yshi_d).then_inc(s_reload, 16)
            pool.dma_start(YS2LO[:], yslo_d).then_inc(s_reload, 16)
            sum_squares("ffn2", X_WOUT2)

        @block.scalar
        def _(act):
            def hi_at(t):
                act.wait_ge(s_raw[t % 2], PER_LOAD * (t // 2 + 1))
                if t:
                    act.wait_ge(s_started, t)
                act.activation(WHI[:, t % 2, :], WRAW[:, t % 2, :], ACT.Copy).then_inc(s_hi, 1)

            def hi_in_loop(i, per, t):
                act.wait_ge(s_raw[t % 2], i * (per // 2 * PER_LOAD) + PER_LOAD * (t // 2 + 1))
                act.wait_ge(s_started, i * per + t)
                act.activation(WHI[:, t % 2, :], WRAW[:, t % 2, :], ACT.Copy).then_inc(s_hi, 1)

            def norm(name, src, ready, scratch, width, to=None):
                use, first, n = NORM_USE[name], NORM_BASE[name], NORM_N[name]
                if first:
                    act.wait_ge(n_h, first)
                    act.wait_ge(n_lo, LO_BEFORE[name])
                act.preload_act_table_set(LOG_EXP)
                for c in range(0 if name in STREAMED else n):
                    act.wait_ge(*ready(c))
                    act.activation(scratch[:, c, :], src(c), ACT.Square).then_inc(n_sq, 1)
                act.wait_ge(n_ms, use + 1)
                act.activation(LNT[:], PS[:, 4, :], ACT.Ln, bias=EPSC[:, 0:1], scale=1.0 / width)
                act.drain()
                act.activation(R[:], LNT[:], ACT.Exp, scale=-0.5).then_inc(n_r, 1)
                if to is not None:
                    for c in range(n):
                        act.wait_ge(n_h, first + c + 1)
                        act.activation(to[:, c, :], scratch[:, c, :], ACT.Copy).then_inc(n_hi, 1)

            def evacuate(name, to, func=ACT.Copy, part=None):
                t0, c0 = TILE0[name], CHUNK0[name]
                with act.Fori(*(part or (0, TILES[name] // 2))) as i:
                    for j in range(2):
                        hi_in_loop(i, 2, t0 + j + 1)
                        for m in range(2):
                            c = 2 * j + m
                            bank = (c0 + c) % 4
                            act.wait_ge(s_chunk, i * 4 + (c0 + c + 1))
                            act.activation(to[:, bass.ds(i * 4 + c, 1), :], PS[:, bank:bank + 1, :], func
                                           ).then_inc(s_bank_free, 1)

            def split_ahead(name, per):
                with act.Fori(0, TILES[name] // per) as i:
                    for j in range(per):
                        hi_in_loop(i, per, TILE0[name] + j + 1)

            def ffn(n):
                t0, c0, tap, first = TILE0[f"up{n}"], CHUNK0[f"up{n}"], FFN_TAP[n][2], (n - 1) * NF
                bias = pc("ffn_conv_b_2")
                with act.Fori(0, NF // 2) as i:
                    def newest(c, acc, chunk):
                        act.wait_ge(s_chunk, i * 4 + (c0 + c + 1))
                        act.activation(acc, PS[:, (c0 + c) % 4, :], ACT.Identity,
                                       bias=PRM[:, bass.ds(chunk + bias, 1)] if n == 2 else 0.0,
                                       scale=PRM[:, bass.ds(chunk + tap, 1)]).then_inc(f_acc, 1)

                    hi_in_loop(i, 2, t0 + 1)
                    for m in range(2):
                        newest(m, FG[:, m, :], i * 2 + m)
                    hi_in_loop(i, 2, t0 + 2)
                    for m in range(2):
                        act.wait_ge(f_tap, i * 4 + (2 * first + m + 1))
                        act.activation(FG[:, m, :], FG[:, m, :], ACT.Silu).then_inc(f_silu, 1)
                    for m in range(2):
                        newest(2 + m, FU[:, m, :], i * 2 + (NF + m))
                    for m in range(2):
                        act.wait_ge(f_prod, i * 2 + (first + m + 1))
                        act.activation(FHI[:, bass.ds(i * 2 + m, 1), :], FU[:, m:m + 1, :], ACT.Copy).then_inc(f_hi, 1)
                    act.wait_ge(f_lo, i * 2 + (first + 2))
                t0 = TILE0[f"down{n}"]
                if n == 1:
                    split_ahead("down1", 6)
                else:
                    for t in range(t0 + 1, t0 + TILES["down2"]):
                        hi_at(t)

            act.wait_ge(s_const, 1)
            hi_at(0)
            act.wait_ge(s_ptc, 5)
            act.activation(SOFT[:, 0, :], PRM[:, pc("rg_lambda"):pc("rg_lambda") + RG], ACT.Abs)
            act.drain()
            act.activation(SOFT[:, 0, :], SOFT[:, 0, :], ACT.Exp, scale=-1.0).then_inc(s_setup_a, 1)
            act.wait_ge(s_setup_v, 1)
            act.activation(LOWB[:, 0, :], LOWB[:, 1, :], ACT.Exp).then_inc(s_setup_a, 1)

            norm("mix1", lambda c: X[:, c, :], lambda c: (s_x, X_IN + c + 1), NRM, D, HHI)
            act.wait_ge(n_lo, KD)
            evacuate("proj1", Z, part=(0, 3))
            act.wait_ge(rg_pe, RG_PE["r_gate"])
            for c in range(RG):
                last = act.activation(RR[:, c, :], PS[:, 4 + c, :], ACT.Sigmoid,
                                      bias=PRM[:, pc("rg_b_r") + c:pc("rg_b_r") + c + 1])
            last.then_inc(rg_act, 1)
            evacuate("proj1", Z, part=(3, 4))
            act.wait_ge(rg_pe, RG_PE["i_gate"])
            for c in range(RG):
                last = act.activation(IG[:, c, :], PS[:, 4 + c, :], ACT.Sigmoid,
                                      bias=PRM[:, pc("rg_b_i") + c:pc("rg_b_i") + c + 1])
            last.then_inc(rg_act, 1)
            act.drain()
            for c in range(RG):
                act.activation(TH[:, c, :], RR[:, c, :], ACT.Tanh, scale=CNEG[:, 0, c:c + 1])
                act.activation(AD[:, c, :], RR[:, c, :], ACT.Exp, scale=CNEG[:, 0, c:c + 1])
                last = act.activation(Z[:, A_U + c, :], RR[:, c, :], ACT.Exp, scale=CNEG[:, 1, c:c + 1])
            last.then_inc(rg_act, 1)
            evacuate("proj1", Z, part=(4, 5))
            act.wait_ge(rg_dve, RG_DVE["b2"])
            act.activation(TH[:], TH[:], ACT.Sqrt, scale=-1.0).then_inc(rg_act, 1)
            act.activation(Z[:, A_GATE:A_GATE + RG, :], Z[:, A_GATE:A_GATE + RG, :], ACT.Gelu_apprx_tanh
                           ).then_inc(rg_act, 1)
            evacuate("proj1", Z, part=(5, 6))

            act.wait_ge(rg_dve, RG_DVE["gated"])
            with act.Fori(0, HG) as i:
                def dve(name):
                    act.wait_ge(hg_dve, i * len(HG_DVE) + HG_DVE[name])

                def pe(name):
                    act.wait_ge(hg_pe, i * len(HG_PE) + HG_PE[name])

                act.activation(HG_[:], Z[:, bass.ds(i + B_F, 1), :], ACT.Sigmoid)
                act.activation(HQ[:], Z[:, bass.ds(i + B_Q, 1), :], ACT.Silu)
                act.activation(HVS[:], Z[:, bass.ds(i + B_V, 1), :], ACT.Copy).then_inc(hg_act, 1)
                act.preload_act_table_set(LOG_EXP)
                dve("qk")
                act.activation(HG_[:], HG_[:], ACT.Ln).then_inc(hg_act, 1)
                for b in range(LEVELS):
                    dve(f"d{b}")
                    act.activation(HDD[:, b % 2, :], HDD[:, b % 2, :], ACT.Exp).then_inc(hg_act, 1)
                dve("dk")
                act.activation(HKD[:], HKD[:], ACT.Exp)
                act.activation(HQG[:], HG_[:], ACT.Exp)
                act.activation(HEGL[:], HG_[:, P - 1:S:P], ACT.Exp).then_inc(hg_act, 1)
                pe("turned")
                act.activation(HVT[:], PS[:, 0, :].rearrange("p (q n) -> p q n", n=P), ACT.Copy)
                act.activation(HKDT[:], PS[:, 1, :].rearrange("p (q n) -> p q n", n=P), ACT.Copy
                               ).then_inc(hg_act, 1)
                pe("out")
                act.activation(YP[:, bass.ds(i + RG, 1), :], PS[:, 3:4, :], ACT.Copy).then_inc(hg_act, 1)

            act.activation(Z[:, B_G:B_G + HG, :], Z[:, B_G:B_G + HG, :], ACT.Silu).then_inc(hn_g, 1)
            act.preload_act_table_set(LOG_EXP)
            act.wait_ge(sc_done, 1)
            act.drain()
            act.activation(SQ1[:], YP[:], ACT.Square).then_inc(hn_sq, 1)
            for half in range(2):
                four = slice(4 * half, 4 * half + 4)
                act.wait_ge(hn_ps, half + 1)
                act.activation(SQ1[:, four, :], PS[:, 4:8, :], ACT.Ln, bias=EPSC[:, 0:1], scale=1.0 / HD)
                act.drain()
                act.activation(SQ1[:, four, :], SQ1[:, four, :], ACT.Exp, scale=-0.5).then_inc(hn_r, 1)
            for c in range(KD):
                act.wait_ge(hn_y, c + 1)
                act.activation(HHI[:, c, :], YP[:, c, :], ACT.Copy).then_inc(hn_hi, 1)

            split_ahead("wout1", 2)
            norm("ffn1", lambda c: X[:, c, :], lambda c: (s_x, X_WOUT1 + c + 1), NRM, D, HHI)
            ffn(1)

            for c in range(KD):
                act.wait_ge(s_x, X_DOWN1 + c + 1)
                act.activation(HHI[:, c, :], X[:, c, :], ACT.Copy).then_inc(e_hi, 1)
            act.wait_ge(e_pt, 1)
            act.activation(PHI[:], PS[:, 6:8, :], ACT.Copy).then_inc(e_phi, 1)
            t0, c0 = TILE0["pleproj"], CHUNK0["pleproj"]
            hi_at(t0 + 1)
            for c in range(KD):
                act.wait_ge(s_chunk, c0 + c + 1)
                act.activation(PP[:, c, :], PS[:, (c0 + c) % 4, :], ACT.Copy).then_inc(s_bank_free, 1)
            act.drain().then_inc(e_pp, 1)
            t0, c0 = TILE0["plegate"], CHUNK0["plegate"]
            for c in range(KD):
                if c % 2 == 0:
                    hi_at(t0 + c // 2 + 1)
                act.wait_ge(s_chunk, c0 + c + 1)
                if c >= 2:
                    act.wait_ge(s_x, X_PLE + c - 1)
                act.activation(PG[:, c % 2, :], PS[:, (c0 + c) % 4, :], ACT.Sigmoid).then_inc(s_bank_free, 1)
                act.drain().then_inc(e_g, 1)
            norm("final", lambda c: X[:, c, :], lambda c: (s_x, X_PLE + c + 1), NRM, D)
            norm("mix2", lambda c: X[:, c, :], lambda c: (n_h, NORM_BASE["mix2"]), NRM, D, HHI)
            t, c = TILE0["small"], CHUNK0["small"]
            hi_at(t + 1)
            act.wait_ge(s_chunk, c + 1)
            act.activation(SMC[0:SMALL_W, :], PS[0:SMALL_W, c % 4, :], ACT.Copy)
            act.activation(KROT[NOPE:QK, :], PS[0:ROPE, c % 4, :], ACT.Copy).then_inc(s_bank_free, 1)
            act.drain().then_inc(ss_act, 1)
            act.wait_ge(ss_dve, SS_DVE["v"])
            act.activation(SMT[0:SMALL_W, 1, :], SMT[0:SMALL_W, 0, :], ACT.Abs)
            act.drain()
            act.activation(SMT[0:SMALL_W, 1, :], SMT[0:SMALL_W, 1, :], ACT.Exp, scale=-1.0)
            act.activation(SMB[64:80, 2:3], SMB[64:80, 2:3], ACT.Exp)
            act.drain().then_inc(ss_act, 1)
            t0, c0 = TILE0["xbc"], CHUNK0["xbc"]
            w, b = pc("ssm_conv_w_2") + 3 * NXBC, pc("ssm_conv_b_2")
            with act.Fori(0, 3) as i:
                for j in range(2):
                    hi_in_loop(i, 2, t0 + j + 1)
                    for m in range(2):
                        c = 2 * j + m
                        bank = (c0 + c) % 4
                        act.wait_ge(s_chunk, i * 4 + (c0 + c + 1))
                        act.activation(XBC[:, bass.ds(i * 4 + c, 1), :], PS[:, bank:bank + 1, :], ACT.Identity,
                                       bias=PRM[:, bass.ds(i * 4 + (b + c), 1)], scale=PRM[:, bass.ds(i * 4 + (w + c), 1)]
                                       ).then_inc(x_acc, 1)
            t0, c0 = TILE0["z"], CHUNK0["z"]
            for c in range(KD):
                if c % 2 == 0:
                    hi_at(t0 + c // 2 + 1)
                if c == 0:
                    act.wait_ge(s_bank_free, 4 + c0)
                    act.activation(XBC[:], XBC[:], ACT.Silu).then_inc(ss_act, 1)
                if c == 6:
                    act.wait_ge(ss_dve, SS_DVE["dl"])
                    act.activation(SMT[64:80, 3, :], SMT[64:80, 3, :], ACT.Exp)
                    act.activation(PACK[96:112, :], CUM[64:80, :], ACT.Exp)
                    act.drain().then_inc(ss_act, 1)
                act.wait_ge(s_chunk, c0 + c + 1)
                act.activation(ZS[:, c, :], PS[:, (c0 + c) % 4, :], ACT.Silu).then_inc(s_bank_free, 1)

            act.preload_act_table_set(LOG_EXP)
            act.wait_ge(s_dec, 16)
            act.activation(DEC[:], DEC[:], ACT.Exp)
            act.drain().then_inc(ss_act, 1)
            for g in range(2):
                act.wait_ge(ss_pe, SS_PE[f"turned{g}"])
                act.activation(BT[:], PS[:, 1, :].rearrange("p (q n) -> p q n", n=P), ACT.Copy).then_inc(ss_act, 1)
                with act.Fori(0, 4) as i:
                    for b in range(2):
                        act.wait_ge(h_d, i * 2 + (8 * g + b + 1))
                        act.activation(DM[:, b, :], DM[:, b, :], ACT.Exp).then_inc(h_e, 1)
            norm("ssm", lambda c: XBC[:, c, :], lambda c: (ss_dve, SS_DVE["y1"]), NS, SSM, YSHI)

            def attention(at):
                def out_of_bank(u):
                    nk = (u % 4 + 1) * P
                    act.wait_ge(a_t, at(u + 1))
                    if u >= 2:
                        act.wait_ge(a_pv, at(u - 1))
                    act.activation(PT[:, u % 2, 0:nk], PS[:, 4 + u % 2, 0:nk], ACT.Copy).then_inc(a_pt, 1)

                for u in range(8):
                    nk = (u % 4 + 1) * P
                    act.wait_ge(a_mx, at(u + 1))
                    if u >= 2:
                        act.wait_ge(a_t, at(u - 1))
                    act.activation(PR[:, u % 2, 0:nk], PS[:, u % 4, 0:nk], ACT.Exp, bias=NMX[:, 0, u:u + 1],
                                   accum_out=NMX[:, 1, u:u + 1]).then_inc(a_exp, 1)
                    if u:
                        out_of_bank(u - 1)
                out_of_bank(7)
                act.wait_ge(a_o, at(8))

            def heads_out(hi, first):
                for c in range(4):
                    act.wait_ge(o_t, first + c + 1)
                    act.activation(hi[:, c, :], PS[:, 4 + c, :], ACT.Copy).then_inc(o_hi, 1)
                act.wait_ge(o_lo, first + 4)

            t0, c0 = TILE0["foxqk"], CHUNK0["foxqk"]
            with act.Fori(0, 2) as i:
                def root(c):
                    act.wait_ge(q_ms, i * 4 + (c + 1))
                    act.wait_ge(q_done, i * 4 + (c + 1))
                    act.activation(RF[:, c % 2, :], PS[:, 4 + c % 2, :], ACT.Ln, bias=EPSC[:, 0:1], scale=1.0 / HD)
                    act.drain()
                    act.activation(RF[:, c % 2, :], RF[:, c % 2, :], ACT.Exp, scale=-0.5).then_inc(q_r, 1)

                for j in range(2):
                    hi_in_loop(i, 2, t0 + j + 1)
                    for m in range(2):
                        c = 2 * j + m
                        bank = (c0 + c) % 4
                        act.wait_ge(s_chunk, i * 4 + (c0 + c + 1))
                        if c >= 2:
                            act.wait_ge(q_ms, i * 4 + (c - 1))
                        act.activation(SQF[:, c % 2, :], PS[:, bank, :], ACT.Square).then_inc(q_sq, 1)
                        act.activation(QKR[:, bass.ds(i * 4 + c, 1), :], PS[:, bank:bank + 1, :], ACT.Copy
                                       ).then_inc(s_bank_free, 1)
                        if c:
                            root(c - 1)
                root(3)
            t0, c0 = TILE0["foxv"], CHUNK0["foxv"]
            for half in range(2):
                hi_at(t0 + half + 1)
                for tc in range(NT):
                    c = c0 + 4 * half + tc
                    act.wait_ge(s_chunk, c + 1)
                    act.activation(VF[:, tc, half * 256:(half + 1) * 256], PS[:, c % 4, 0:256], ACT.Copy
                                   ).then_inc(s_bank_free, 1)
            act.drain().then_inc(v_out, 1)
            act.wait_ge(s_spill, 32)
            with act.Fori(0, 4) as i:
                attention(lambda k: i * 8 + k)
            heads_out(YFHI, 0)

            t0, c0 = TILE0["mlac"], CHUNK0["mlac"]
            for c in range(5):
                if c % 2 == 0:
                    hi_at(t0 + c // 2 + 1)
                act.wait_ge(s_chunk, c0 + c + 1)
                act.activation(CR[:, c, :], PS[:, (c0 + c) % 4, :], ACT.Copy).then_inc(s_bank_free, 1)
            act.drain()
            norm("mlaq", lambda c: CR[:, c, :], lambda c: (s_chunk, c0 + 5), NC, MLA_Q, CQHI)
            norm("mlakv", lambda c: CR[:, 3 + c, :], lambda c: (s_chunk, c0 + 5), NC, MLA_KV, CQHI[:, 3:5, :])
            act.wait_ge(n_lo, LO_BEFORE["ffn2"])
            for hh in range(2):
                act.activation(SQM[NOPE:QK, 2 * hh + 1, :], KROT[NOPE:QK, :], ACT.Square)
            act.drain().then_inc(mp_act, 1)
            act.wait_ge(mp_dve, MP_DVE["angles"])
            act.activation(SIN[NOPE:QK, :], ANG[NOPE:QK, 0, :], ACT.Sin)
            act.activation(ANG[NOPE:QK, 1, :], ANG[NOPE:QK, 1, :], ACT.Sin)
            act.drain().then_inc(mp_act, 1)
            act.preload_act_table_set(LOG_EXP)
            for credit, n in ((mh_free, 2), (mh_va, 1), (mh_r, 1)):
                act.drain().then_inc(credit, n)
            t0 = TILE0["mlahead"]
            with act.Fori(0, 2) as i:
                for j in range(2):
                    def head(k):
                        return i * 4 + (2 * j + k)

                    def root(hh):
                        act.wait_ge(mh_ms, head(hh + 3))
                        act.wait_ge(mh_qk, head(hh + 2))
                        act.activation(RS2[0:QK, :, :], PS[0:QK, 4:6, :], ACT.Ln, bias=EPSC[0:QK, 0:1], scale=1.0 / QK)
                        act.drain()
                        act.activation(RS2[0:QK, :, :], RS2[0:QK, :, :], ACT.Exp, scale=-0.5).then_inc(mh_r, 1)

                    hi_in_loop(i, 2, t0 + j + 1)
                    for hh in range(2):
                        act.wait_ge(mh_p, head(hh + 1))
                        act.wait_ge(mh_ms, head(hh + 1))
                        act.activation(SQM[0:QK, 2 * hh, :], PS[0:QK, 2 * hh, :], ACT.Square)
                        act.activation(SQM[0:NOPE, 2 * hh + 1, :], PS[0:NOPE, 2 * hh + 1, :], ACT.Square).then_inc(mh_sq, 1)
                        act.wait_ge(mh_qk, head(hh + 1))
                        act.activation(QR[0:QK, hh, :], PS[0:QK, 2 * hh, :], ACT.Copy)
                        act.activation(KR[0:NOPE, hh, :], PS[0:NOPE, 2 * hh + 1, :], ACT.Copy).then_inc(mh_free, 1)
                    root(0)
                    act.wait_ge(mh_v, i * 2 + (j + 1))
                    act.activation(VA[:, :, bass.ds(i * 2 * P + j * P, P)], PS[:, 7, :].rearrange("p (q n) -> p q n", n=P),
                                   ACT.Copy).then_inc(mh_va, 1)
                    root(1)
            with act.Fori(0, 4) as i:
                attention(lambda k: i * 8 + (k + 32))
            heads_out(YMHI, 4)

            t0, c0, gate = TILE0["merge"], CHUNK0["merge"], pc("b_gate_2")
            with act.Fori(0, 2) as i:
                for pair in range(2):
                    t, c, chunk = t0 + 5 * pair, c0 + 12 * pair, 2 * pair
                    act.wait_ge(g_lo, i * 4 + (chunk + 1))

                    def sigmoids(branch, to, first):
                        for m in range(2):
                            n = c + first + m
                            act.wait_ge(s_chunk, i * 24 + (n + 1))
                            act.activation(to[:, m, :], PS[:, n % 4, :], ACT.Sigmoid,
                                           bias=PRM[:, bass.ds(i * 4 + (gate + branch * KD + chunk + m), 1)]
                                           ).then_inc(s_bank_free, 1)
                            act.drain().then_inc(g_sig, 1)

                    hi_in_loop(i, 10, t + 1)
                    sigmoids(0, GA, 0)
                    hi_in_loop(i, 10, t + 2)
                    sigmoids(1, GB, 2)
                    hi_in_loop(i, 10, t + 3)
                    hi_in_loop(i, 10, t + 4)
                    act.wait_ge(g_mid, i * 2 + (pair + 1))
                    sigmoids(2, GB, 8)
                    hi_in_loop(i, 10, t + 5)
                    for m in range(2):
                        act.wait_ge(g_sum, i * 4 + (chunk + m + 1))
                        act.activation(MGHI[:, bass.ds(i * 4 + (chunk + m), 1), :], GA[:, m:m + 1, :], ACT.Copy
                                       ).then_inc(g_hi, 1)
            split_ahead("wout2", 2)
            norm("ffn2", lambda c: X[:, c, :], lambda c: (s_x, X_WOUT2 + c + 1), NRM, D, HHI)
            ffn(2)
            for n in range(1, 8, 2):
                act.wait_ge(s_ot, n + 1)
                act.activation(OTOK[:, n // 2, (n % 2) * S:(n % 2 + 1) * S], PS[:, n, :], ACT.Copy).then_inc(s_oa, 1)

        @block.vector
        def _(dve):
            def lo(t, slot):
                dve.wait_ge(s_hi, t + 1)
                dve.tensor_tensor(WLO[:, slot, :], WRAW[:, slot, :], f32(WHI[:, slot, :]), ALU.subtract
                                  ).then_inc(s_lo, 1)

            def add_lo(to, a, hi_part):
                return dve.tensor_tensor(to, a, f32(hi_part), ALU.subtract)

            def stt(out, in0, scalar, in1, op0=ALU.mult, op1=ALU.mult):
                return dve.scalar_tensor_tensor(out=out, in0=in0, scalar=scalar, in1=in1, op0=op0, op1=op1)

            def norm(name, src, gain, scratch, hi_to=None, lo_to=None, out=None):
                use, n = NORM_USE[name], NORM_N[name]
                dve.wait_ge(n_r, use + 1)

                def low(c):
                    dve.wait_ge(n_hi, LO_BEFORE[name] + c + 1)
                    add_lo(lo_to[:, c, :], scratch[:, c, :], hi_to[:, c, :]).then_inc(n_lo, 1)

                for c in range(n):
                    to = scratch[:, c, :] if out is None else out(c)
                    stt(to, src(c), PRM[:, gain + c:gain + c + 1], R[:]).then_inc(n_h, 1)
                    if lo_to is not None and c:
                        low(c - 1)
                if lo_to is not None:
                    low(n - 1)

            def lo_only(name, per, part=None):
                t0 = TILE0[name]
                with dve.Fori(*(part or (0, TILES[name] // per))) as i:
                    for j in range(per):
                        lo(i * per + (t0 + j + 1), (t0 + j + 1) % 2)

            def add_to_residual(name, loops, per, ends, last=False):
                t0, c0 = TILE0[name], CHUNK0[name]

                def body(i, offset=0, skip_last=False):
                    done = 0
                    for j in range(per):
                        if not (skip_last and j == per - 1):
                            lo(i * per + (t0 + j + 1), (t0 + j + 1) % 2)
                        if j in ends:
                            for _ in range(2):
                                bank = (c0 + done) % 4
                                xc = X[:, bass.ds(i * 4 + done, 1), :]
                                dve.wait_ge(s_chunk, i * 4 + (c0 + done + 1))
                                dve.tensor_tensor(xc, xc, PS[:, bank:bank + 1, :], ALU.add).then_inc(s_bank_free, 1)
                                dve.drain().then_inc(s_x, 1)
                                done += 1

                with dve.Fori(0, loops - last) as i:
                    body(i)
                if last:
                    body(loops - 1, skip_last=True)

            def ffn(n):
                t0, c0, first = TILE0[f"up{n}"], CHUNK0[f"up{n}"], (n - 1) * NF
                with dve.Fori(0, NF // 2) as i:
                    def taps(c, acc, chunk):
                        bank = (c0 + c) % 4
                        dve.wait_ge(f_acc, i * 4 + (2 * first + c + 1))
                        stt(acc[:, 1:], PS[:, bank, 0:S - 1], PRM[:, bass.ds(chunk + FFN_TAP[n][1], 1)], acc[:, 1:],
                            op1=ALU.add)
                        dve.drain()
                        stt(acc[:, 2:], PS[:, bank, 0:S - 2], PRM[:, bass.ds(chunk + FFN_TAP[n][0], 1)], acc[:, 2:],
                            op1=ALU.add).then_inc(s_bank_free, 1)
                        dve.drain().then_inc(f_tap, 1)

                    lo(i * 2 + (t0 + 1), (t0 + 1) % 2)
                    for m in range(2):
                        taps(m, FG[:, m, :], i * 2 + m)
                    lo(i * 2 + (t0 + 2), t0 % 2)
                    for m in range(2):
                        taps(2 + m, FU[:, m, :], i * 2 + (NF + m))
                        dve.wait_ge(f_silu, i * 2 + (first + m + 1))
                        dve.tensor_tensor(FU[:, m, :], FU[:, m, :], FG[:, m, :], ALU.mult).then_inc(f_prod, 1)
                    for m in range(2):
                        dve.wait_ge(f_hi, i * 2 + (first + m + 1))
                        add_lo(FLO[:, bass.ds(i * 2 + m, 1), :], FU[:, m:m + 1, :], FHI[:, bass.ds(i * 2 + m, 1), :]
                               ).then_inc(f_lo, 1)
                add_to_residual(f"down{n}", 2, 6, (2, 5), last=n == 2)

            def log1p_of(e, s2, p, rd):
                dve.tensor_scalar(rd, e, 2.0, None, ALU.add)
                dve.drain()
                dve.reciprocal(rd, rd)
                dve.drain()
                dve.tensor_tensor(e, e, rd, ALU.mult)
                dve.drain()
                dve.tensor_tensor(s2, e, e, ALU.mult)
                dve.drain()
                dve.tensor_scalar(p, s2, 1.0 / 17, None, ALU.mult)
                dve.drain()
                for k in (15, 13, 11, 9, 7, 5, 3):
                    stt(p, p, 1.0 / k, s2, op0=ALU.add)
                    dve.drain()
                stt(p, p, 1.0, e, op0=ALU.add)
                dve.drain()
                dve.tensor_scalar(p, p, 2.0, None, ALU.mult)
                dve.drain()

            for tile in range(5):
                dve.wait_ge(s_pt, tile + 1)
                dve.tensor_copy(PRM[:, tile * P:tile * P + PUSED[tile]], PS[:, 5 + tile % 2, 0:PUSED[tile]]
                                ).then_inc(s_ptc, 1)
            for c in range(KD):
                dve.wait_ge(s_xt, c + 1)
                dve.tensor_copy(X[:, c, :], PS[:, c % 4, :]).then_inc(s_x, 1)
            lam = PRM[:, pc("rg_lambda"):pc("rg_lambda") + RG]
            dve.wait_ge(s_setup_a, 1)
            log1p_of(SOFT[:, 0, :], SOFT[:, 1, :], SOFT[:, 2, :], SOFT[:, 3, :])
            dve.tensor_scalar(SOFT[:, 0, :], lam, -1.0, 0.0, ALU.mult, ALU.max)
            dve.drain()
            dve.tensor_tensor(SOFT[:, 0, :], SOFT[:, 0, :], SOFT[:, 2, :], ALU.add)
            dve.drain()
            dve.tensor_scalar(CNEG[:, 0, :], SOFT[:, 0, :], -8.0, None, ALU.mult)
            dve.tensor_scalar(CNEG[:, 1, :], SOFT[:, 0, :], -16.0, None, ALU.mult)
            low = PRM[:, pc("hg_lower_bounds"):pc("hg_lower_bounds") + HG]
            dve.tensor_tensor(LOWB[:, 1, :], low, low, ALU.subtract)
            dve.drain().then_inc(s_setup_v, 1)
            dve.wait_ge(s_setup_a, 2)
            dve.reciprocal(SOFT[:, 1, :], LOWB[:, 0, :])
            dve.drain()
            dve.tensor_tensor(SOFT[:, 1, :], SOFT[:, 1, :], LOWB[:, 0, :], ALU.mult)
            dve.drain()
            dve.tensor_tensor(LOWB[:, 0, :], SOFT[:, 1, :], SOFT[:, 1, :], ALU.subtract)
            dve.drain()
            dve.tensor_scalar(LOWB[:, 1, :], LOWB[:, 0, :], -1.0, 1.0, ALU.mult, ALU.add)
            lo(0, 0)
            dve.wait_ge(s_const, 1)
            dve.tensor_tensor(MSCRI[:, 0, :], MSCRI[:, 0, :], MSCRI[:, 1, :], ALU.bitwise_xor)
            dve.drain()
            dve.tensor_copy(MSCR[:, 9, :], MSCRI[:, 0, :]).then_inc(s_mask, 1)
            dve.wait_ge(s_mask, 2)
            for b in range(LEVELS + 1):
                dve.tensor_scalar(MSCR[:, b, :], MSCR[:, 9, :], float(2 ** b), None, ALU.is_ge)
            dve.tensor_scalar(HMASK[:, 0, :], MSCR[:, 9, :], 0.0, None, ALU.is_equal)
            dve.drain()
            for b in range(LEVELS):
                dve.tensor_tensor(HMASK[:, 1 + b, :], MSCR[:, b, :], MSCR[:, b + 1, :], ALU.subtract)

            norm("mix1", lambda c: X[:, c, :], pc("norm_mix_gain"), NRM, HHI, HLO)
            lo_only("proj1", 2, (0, 2))
            dve.wait_ge(s_bank_free, 4 + CHUNK0["proj1"] + 2 * RG)
            U = YP[:, 0:RG, :]
            w = pc("rg_conv_w")
            for c in range(RG):
                dve.tensor_scalar(U[:, c, :], Z[:, A_U + c, :], PRM[:, w + 3 * RG + c:w + 3 * RG + c + 1],
                                  PRM[:, pc("rg_conv_b") + c:pc("rg_conv_b") + c + 1], ALU.mult, ALU.add)
            for back in (1, 2, 3):
                dve.drain()
                k = w + (3 - back) * RG
                for c in range(RG):
                    stt(U[:, c, back:], Z[:, A_U + c, 0:S - back], PRM[:, k + c:k + c + 1], U[:, c, back:], op1=ALU.add)
            dve.drain().then_inc(rg_dve, 1)
            lo_only("proj1", 2, (2, 5))
            dve.wait_ge(rg_act, RG_ACT["exps"])
            stt(TH[:], Z[:, A_U:A_U + RG, :], 1.0, TH[:], op0=ALU.add)
            dve.drain().then_inc(rg_dve, 1)
            lo_only("proj1", 2, (5, 6))
            dve.tensor_tensor(IG[:], IG[:], U, ALU.mult)
            dve.drain()
            dve.wait_ge(rg_act, RG_ACT["beta"])
            dve.tensor_tensor(IG[:], IG[:], TH[:], ALU.mult)
            dve.drain()
            for c in range(RG):
                dve.tensor_tensor_scan(U[:, c, :], AD[:, c, :], IG[:, c, :], 0.0, ALU.mult, ALU.add)
            dve.drain().then_inc(rg_dve, 1)
            dve.wait_ge(s_bank_free, 4 + CHUNK0["wout1"])
            cv, acc = Z[:, C_C:C_C + SC, :], Z[:, C_V:C_V + SC, :]
            dve.tensor_tensor(cv, cv, acc, ALU.mult)
            dve.drain()
            w = pc("sc_conv_w")
            for c in range(SC):
                dve.tensor_scalar(acc[:, c, :], cv[:, c, :], PRM[:, w + 2 * SC + c:w + 2 * SC + c + 1], None, ALU.mult)
            for back in (1, 2):
                dve.drain()
                k = w + (2 - back) * SC
                for c in range(SC):
                    stt(acc[:, c, back:], cv[:, c, 0:S - back], PRM[:, k + c:k + c + 1], acc[:, c, back:], op1=ALU.add)
            dve.drain()
            dve.tensor_tensor(YP[:, RG + HG:KD, :], acc, Z[:, C_B:C_B + SC, :], ALU.mult)
            dve.drain().then_inc(sc_done, 1)
            dve.wait_ge(rg_act, RG_ACT["gelus"])
            dve.tensor_tensor(U, U, Z[:, A_GATE:A_GATE + RG, :], ALU.mult)
            dve.memset(HS[:], 0.0)
            dve.drain().then_inc(rg_dve, 1)

            with dve.Fori(0, HG) as i:
                def act(name):
                    dve.wait_ge(hg_act, i * len(HG_ACT) + HG_ACT[name])

                def pe(name):
                    dve.wait_ge(hg_pe, i * len(HG_PE) + HG_PE[name])

                def halves(t, b):
                    v = t.rearrange("p (n two h) -> p n two h", two=2, h=2 ** b)
                    return v[:, :, 0, :], v[:, :, 1, :]

                def level_exponents(b):
                    even, odd = halves(HG_[:], b)
                    d_even, d_odd = halves(HDD[:, b % 2, :], b)
                    mid = even[:, :, 2 ** b - 1:2 ** b].broadcast_to(list(even.shape))
                    dve.tensor_tensor(d_even, mid, even, ALU.subtract)
                    dve.tensor_tensor(d_odd, odd, mid, ALU.subtract)
                    dve.drain().then_inc(hg_dve, 1)

                def level_product(b):
                    act(f"e{b}")
                    if b >= 1:
                        pe(f"g{b - 1}")
                    e_even, e_odd = halves(HDD[:, b % 2, :], b)
                    m_even, m_odd = halves(HM[:, b % 2, :], b)
                    dve.tensor_tensor(m_even, e_even, halves(HK[:], b)[0], ALU.mult)
                    dve.tensor_tensor(m_odd, e_odd, halves(HQ[:], b)[1], ALU.mult)
                    dve.drain().then_inc(hg_dve, 1)

                def take(level):
                    for h in range(2):
                        dve.copy_predicated(
                            out=HST[:, h, :].rearrange("p (q n) -> p q n", n=P),
                            mask=HMASK[:, level, :].unsqueeze(1).broadcast_to([P, NT, P]),
                            data=PS[:, 4 + 2 * (level % 2) + h, :].rearrange("p (q n) -> p q n", n=P))
                    dve.drain().then_inc(hg_dve, 1)

                act("q_sigmoid")
                dve.memset(HST[:], 0.0)
                dve.tensor_scalar(HQ[:], HQ[:], HD ** -0.5, None, ALU.mult)
                dve.tensor_scalar(HG_[:], HG_[:], LOWB[:, 1, bass.ds(i, 1)], LOWB[:, 0, bass.ds(i, 1)], ALU.mult, ALU.add)
                dve.drain()
                dve.tensor_scalar(HK[:], HG_[:], -1.0, 1.0, ALU.mult, ALU.add)
                dve.drain().then_inc(hg_dve, 1)
                act("logf")
                dve.tensor_tensor_scan(HG_[:], RESET[:], HG_[:], 0.0, ALU.mult, ALU.add)
                dve.drain()
                for b in range(LEVELS + 1):
                    if b < LEVELS:
                        level_exponents(b)
                    if b >= 1:
                        level_product(b - 1)
                    if b >= 2:
                        take(b - 2)
                pe(f"g{LEVELS - 1}")
                gv = HG_[:].rearrange("p (q n) -> p q n", n=P)
                dve.tensor_tensor(HKD[:].rearrange("p (q n) -> p q n", n=P), gv[:, :, P - 1:P].broadcast_to([P, NT, P]), gv,
                                  ALU.subtract)
                dve.drain().then_inc(hg_dve, 1)
                take(LEVELS - 1)
                act("decays")
                pe(f"g{LEVELS}")
                dve.tensor_tensor(HKD[:], HKD[:], HK[:], ALU.mult)
                dve.tensor_tensor(HQG[:], HQG[:], HQ[:], ALU.mult)
                dve.drain().then_inc(hg_dve, 1)
                take(LEVELS)
                pe("states")
                for q in range(3):
                    for h in range(2):
                        b = slice(h * HD, (h + 1) * HD)
                        new = PS[b, 2, q * P + h * HD:q * P + (h + 1) * HD]
                        if q == 0:
                            dve.tensor_copy(HS[b, q, b], new)
                        else:
                            stt(HS[b, q, b], HS[b, q - 1, b], HEGL[b, q:q + 1], new, op1=ALU.add)
                    dve.drain()
                dve.drain().then_inc(hg_dve, 1)

            for c in range(KD):
                dve.wait_ge(hn_r, c // 4 + 1)
                g = pc("mix_out_gain") + c
                stt(YP[:, c, :], YP[:, c, :], PRM[:, g:g + 1], SQ1[:, c, :])
                if RG <= c < RG + HG:
                    dve.wait_ge(hn_g, 1)
                    dve.drain()
                    dve.tensor_tensor(YP[:, c, :], YP[:, c, :], Z[:, B_G + c - RG, :], ALU.mult)
                dve.drain().then_inc(hn_y, 1)
                if c:
                    dve.wait_ge(hn_hi, c)
                    add_lo(HLO[:, c - 1, :], YP[:, c - 1, :], HHI[:, c - 1, :])
            dve.wait_ge(hn_hi, KD)
            add_lo(HLO[:, KD - 1, :], YP[:, KD - 1, :], HHI[:, KD - 1, :]).then_inc(hn_lo, 1)

            add_to_residual("wout1", 2, 2, (0, 1))
            norm("ffn1", lambda c: X[:, c, :], pc("norm_ffn_gain"), NRM, HHI, HLO)
            ffn(1)

            for c in range(KD):
                dve.wait_ge(e_hi, c + 1)
                add_lo(HLO[:, c, :], X[:, c, :], HHI[:, c, :]).then_inc(e_lo, 1)
            dve.wait_ge(e_phi, 1)
            add_lo(PLO[:], PS[:, 6:8, :], PHI[:]).then_inc(e_plo, 1)
            t0 = TILE0["plegate"]
            lo(t0, t0 % 2)
            dve.wait_ge(e_pp, 1)
            for c in range(KD):
                t = t0 + c // 2 + 1
                if c % 2 == 0:
                    lo(t, t % 2)
                dve.wait_ge(e_g, c + 1)
                dve.tensor_tensor(PG[:, c % 2, :], PG[:, c % 2, :], PP[:, c, :], ALU.mult)
                dve.drain()
                dve.tensor_tensor(X[:, c, :], X[:, c, :], PG[:, c % 2, :], ALU.add)
                dve.drain().then_inc(s_x, 1)
            norm("final", lambda c: X[:, c, :], pc("final_norm_gain"), NRM, out=lambda c: X[:, c, :])
            norm("mix2", lambda c: X[:, c, :], pc("norm_mix_g_2"), NRM, HHI, HLO)
            dve.drain().then_inc(h_dfree, 2)
            small, decay_rows = slice(0, SMALL_W), slice(64, 80)
            t = TILE0["small"]
            lo(t + 1, (t + 1) % 2)
            dve.memset(PACK[:], 0.0)
            dve.wait_ge(ss_act, SS_ACT["raw"])
            dve.wait_ge(s_small, SMALL_LOADS)
            dve.tensor_scalar(SMT[small, 0, :], SMC[small, :], SMB[small, 0:1], SMB[small, 1:2], ALU.add, ALU.mult)
            dve.drain().then_inc(ss_dve, 1)
            t0, c0, w = TILE0["xbc"], CHUNK0["xbc"], pc("ssm_conv_w_2")
            with dve.Fori(0, 3) as i:
                for j in range(2):
                    lo(i * 2 + (t0 + j + 1), (t0 + j + 1) % 2)
                    for m in range(2):
                        c = 2 * j + m
                        dve.wait_ge(x_acc, i * 4 + (c + 1))
                        for back in (1, 2, 3):
                            acc = XBC[:, bass.ds(i * 4 + c, 1), back:]
                            bank = (c0 + c) % 4
                            last = stt(acc, PS[:, bank:bank + 1, 0:S - back],
                                       PRM[:, bass.ds(i * 4 + (w + (3 - back) * NXBC + c), 1)], acc, op1=ALU.add)
                            if back < 3:
                                dve.drain()
                        last.then_inc(s_bank_free, 1)
            t0 = TILE0["z"]
            lo(t0 + 1, (t0 + 1) % 2)
            dve.wait_ge(ss_act, SS_ACT["e"])
            log1p_of(SMT[small, 1, :], SMT[small, 2, :], SMT[small, 3, :], SMT[small, 4, :])
            lo(t0 + 2, (t0 + 2) % 2)
            stt(SMT[small, 0, :], SMT[small, 0, :], 0.0, SMT[small, 3, :], ALU.max, ALU.add)
            dve.tensor_scalar(SMB[decay_rows, 2:3], SMB[decay_rows, 2:3], -1.0, None, ALU.mult)
            dve.drain()
            dve.tensor_scalar(SMT[small, 2, :], SMT[small, 0, :], SMB[small, 2:3], None, ALU.mult)
            dve.tensor_copy(PACK[0:16, :], SMT[decay_rows, 0, :])
            dve.drain()
            dve.tensor_tensor_scan(CUM[32:64, :], ONES[32:64, 0:1].broadcast_to([32, S]), SMT[32:64, 2, :], 0.0, ALU.mult, ALU.add)
            dve.tensor_tensor_scan(CUM[decay_rows, :], RESET[decay_rows, :], SMT[decay_rows, 2, :], 0.0, ALU.mult, ALU.add)
            dve.drain()
            dve.tensor_copy(PACK[32:48, :], CUM[decay_rows, :])
            dve.tensor_scalar(SMT[32:64, 4, :], CUM[32:64, :], -1.0, None, ALU.mult)
            by_tile = CUM[decay_rows, :].rearrange("p (q n) -> p q n", n=P)
            dve.tensor_tensor(SMT[decay_rows, 3, :].rearrange("p (q n) -> p q n", n=P),
                              by_tile[:, :, P - 1:P].broadcast_to([16, NT, P]), by_tile, ALU.subtract)
            dve.drain().then_inc(ss_dve, 1)
            lo(t0 + 3, (t0 + 3) % 2)
            dve.wait_ge(ss_act, SS_ACT["pexp"])
            dve.tensor_tensor(PACK[64:80, :], SMT[decay_rows, 3, :], SMT[decay_rows, 0, :], ALU.mult)
            dve.drain().then_inc(ss_dve, 1)
            lo(t0 + 4, (t0 + 4) % 2)
            dve.wait_ge(ss_pe, SS_PE["tok"])
            dve.tensor_copy(TOK[:], PS[:, 0, :].rearrange("p (q n) -> p q n", n=P))
            dve.drain().then_inc(ss_dve, 1)
            dve.wait_ge(s_rows, 64)
            for g in range(2):
                heads = slice(8 * g, 8 * g + 8)

                def per_head(t, q=slice(None)):
                    return t[:, q, :].rearrange("p q (h d) -> p q h d", d=HD)

                def by_token(first, q0=0):
                    return TOK[:, q0:, first + 8 * g:first + 8 * g + 8].unsqueeze(3).broadcast_to([P, NT - q0, 8, HD])

                dve.wait_ge(ss_pe, SS_PE[f"turned{g}"])
                dve.tensor_tensor(CBM[:].rearrange("p (q n) -> p q n", n=P), PS[:, 2, :].rearrange("p (q n) -> p q n", n=P),
                                  TRI[:].unsqueeze(1).broadcast_to([P, NT, P]), ALU.mult)
                dve.tensor_tensor(per_head(XD), per_head(PS, slice(4, 8)), by_token(0), ALU.mult)
                dve.tensor_tensor(per_head(XW), per_head(PS, slice(4, 8)), by_token(64), ALU.mult)
                dve.drain().then_inc(ss_dve, 1)
                dve.wait_ge(ss_pe, SS_PE[f"states{g}"])
                dve.wait_ge(ss_act, SS_ACT["dec"])
                dve.tensor_copy(SH[:, 0, :], PS[:, 4, :])
                for q in (1, 2):
                    dve.drain()
                    dve.tensor_tensor(per_head(SH, slice(q, q + 1)), per_head(SH, slice(q - 1, q)),
                                      DEC[:, heads, q:q + 1].unsqueeze(1).broadcast_to([P, 1, 8, HD]), ALU.mult)
                    dve.drain()
                    dve.tensor_tensor(SH[:, q, :], SH[:, q, :], PS[:, 4 + q, :], ALU.add)
                dve.drain().then_inc(ss_dve, 1)
                dve.wait_ge(ss_pe, SS_PE[f"yoff{g}"])
                dve.tensor_tensor(per_head(YT, slice(1, 4)), per_head(PS, slice(1, 4)), by_token(96, 1), ALU.mult)
                dve.drain().then_inc(ss_dve, 1)
                with dve.Fori(0, 4) as i:
                    def at(b):
                        return i * 2 + (8 * g + b + 1)

                    def masked(b):
                        dve.wait_ge(h_e, at(b))
                        dve.tensor_tensor(DM[:, b, :], DM[:, b, :], CBM[:], ALU.mult)
                        dve.drain().then_inc(h_m, 1)

                    for b in range(2):
                        dve.wait_ge(s_abc[b], i * 16 + (64 * g + 16))
                        dve.wait_ge(h_y, at(b))
                        for q in range(NT):
                            cols = slice(q * P, (q + 1) * P)
                            dve.tensor_scalar(DM[:, b, cols], ABC[:, b, cols], TOK[:, q, bass.ds(i * 2 + (32 + 8 * g + b), 1)],
                                              0.0, ALU.subtract, ALU.min)
                        dve.drain().then_inc(h_dfree, 1)
                        dve.drain().then_inc(h_d, 1)
                        if b:
                            masked(0)
                    masked(1)
                dve.wait_ge(h_y, 8 * g + 10)
                dve.tensor_copy(YT[:, 0, :], PS[:, 0, :])
                dve.tensor_tensor(YT[:, 1:4, :], YT[:, 1:4, :], PS[:, 1:4, :], ALU.add)
                dve.drain().then_inc(ss_dve, 1)
                dve.wait_ge(ss_pe, SS_PE[f"yturned{g}"])
                for j in range(4):
                    c = 4 * g + j
                    stt(XBC[:, c, :], XBC[:, c, :], DSKIP[:, c:c + 1], PS[:, 4 + j, :], op1=ALU.add)
                dve.drain()
                y = slice(4 * g, 4 * g + 4)
                dve.tensor_tensor(XBC[:, y, :], XBC[:, y, :], ZS[:, y, :], ALU.mult)
                dve.drain().then_inc(ss_dve, 1)
            norm("ssm", lambda c: XBC[:, c, :], pc("ssm_norm_g_2"), NS, YSHI, YSLO)

            def scores(mask, u, at):
                qb = u % 4
                diagonal = PS[:, u % 4, qb * P:(qb + 1) * P]
                dve.wait_ge(a_s, at(u + 17))
                dve.tensor_tensor(diagonal, diagonal, mask[:], ALU.add)
                dve.drain()
                dve.tensor_reduce(out=NMX[:, 0, u:u + 1], in_=PS[:, u % 4, 0:(qb + 1) * P], axis=AX, op=ALU.max, negate=True)
                dve.drain().then_inc(a_mx, 1)

            def output(u, at, col):
                dve.wait_ge(a_pv, at(u + 1))
                dve.reciprocal(NMX[:, 2, u:u + 1], NMX[:, 1, u:u + 1])
                dve.drain()
                dve.tensor_scalar(OH[:, u % 4, bass.ds(col(u // 4), HD)], PS[:, 6 + u % 2, 0:HD], NMX[:, 2, u:u + 1], None,
                                  ALU.mult).then_inc(a_o, 1)

            def attend(mask, at, col):
                for u in range(8):
                    scores(mask, u, at)
                    if u >= 3:
                        output(u - 3, at, col)
                for u in (5, 6, 7):
                    output(u, at, col)

            def heads_out(hi, lo_to, first):
                for c in range(4):
                    dve.wait_ge(o_hi, first + c + 1)
                    add_lo(lo_to[:, c, :], PS[:, 4 + c, :], hi[:, c, :]).then_inc(o_lo, 1)

            dve.tensor_scalar(QKG[:, 0:1], QKG[:, 0:1], HD ** -0.5, None, ALU.mult)
            dve.tensor_scalar(QKG[:, 2:3], QKG[:, 2:3], QK ** -0.5, None, ALU.mult)
            dve.drain().then_inc(q_done, 2)
            t0, c0 = TILE0["foxqk"], CHUNK0["foxqk"]
            with dve.Fori(0, 2) as i:
                def scaled(c):
                    qk = QKR[:, bass.ds(i * 4 + c, 1), :]
                    dve.wait_ge(q_r, i * 4 + (c + 1))
                    stt(qk, qk, QKG[:, bass.ds(i, 1)], RF[:, c % 2:c % 2 + 1, :])
                    dve.drain().then_inc(q_done, 1)

                for j in range(2):
                    lo(i * 2 + (t0 + j + 1), (t0 + j + 1) % 2)
                    for c in ((0,) if j == 0 else (1, 2)):
                        scaled(c)
                scaled(3)
            t0 = TILE0["foxv"]
            for t in (t0 + 1, t0 + 2):
                lo(t, t % 2)
            dve.wait_ge(s_spill, 32)
            with dve.Fori(0, 4) as i:
                attend(CAUSAL, lambda k: i * 8 + k, lambda hh: i * P + hh * HD)
            heads_out(YFHI, YFLO, 0)

            t0 = TILE0["mlac"]
            for t in (t0 + 1, t0 + 2, t0 + 3):
                lo(t, t % 2)
            norm("mlaq", lambda c: CR[:, c, :], pc("mla_q_norm_g_2"), NC, CQHI, CQLO)
            norm("mlakv", lambda c: CR[:, 3 + c, :], pc("mla_kv_norm_g_2"), NC, CQHI[:, 3:5, :], CQLO[:, 3:5, :])
            half, rope = ROPE // 2, slice(NOPE, QK)
            for n in range(2):
                dve.tensor_scalar(SW[rope, n, 0:half], IDENT[rope, NOPE + half:QK], -1.0, QKG[rope, 2 + n:3 + n], ALU.mult, ALU.mult)
                dve.tensor_scalar(SW[rope, n, half:ROPE], IDENT[rope, NOPE:NOPE + half], QKG[rope, 2 + n:3 + n], None, ALU.mult)
            dve.drain().then_inc(mp_dve, 1)
            ang, cos, n, t = (ANG[rope, k, :] for k in range(4))
            dve.wait_ge(s_pos, 16)
            dve.tensor_copy(ang, POSI[rope, :])
            dve.drain()
            dve.tensor_scalar(ang, ang, INVF[rope, 0:1], None, ALU.mult)
            dve.drain()
            dve.tensor_scalar(n, ang, 1 / TWO_PI, None, ALU.mult)
            dve.drain()
            dve.tensor_scalar(n, n, ROUNDING, None, ALU.add)
            dve.drain()
            dve.tensor_scalar(n, n, ROUNDING, None, ALU.subtract)
            dve.drain()
            for part in TWO_PI_PARTS:
                stt(ang, n, -part, ang, op1=ALU.add)
                dve.drain()
            dve.tensor_scalar(t, ang, np.pi / 2, -TWO_PI, ALU.is_gt, ALU.mult)
            dve.drain()
            stt(cos, t, np.pi / 2, ang, ALU.add, ALU.add)
            dve.drain()
            for v in (ang, cos):
                dve.tensor_scalar(v, v, PI_BELOW, -PI_BELOW, ALU.min, ALU.max)
            dve.drain().then_inc(mp_dve, 1)
            dve.tensor_scalar(CG[0:NOPE, :], ONES[0:NOPE, 0:1].broadcast_to([NOPE, S]), QKG[0:NOPE, 2:3], None, ALU.mult)
            dve.wait_ge(mp_act, MP_ACT["trig"])
            dve.tensor_scalar(CG[rope, :], cos, QKG[rope, 2:3], None, ALU.mult)
            dve.wait_ge(mp_pe, MP_PE["kswap"])
            stt(KROT[rope, :], KROT[rope, :], QKG[rope, 3:4], cos)
            dve.tensor_tensor(MR[rope, :], PS[rope, 6, :], SIN[rope, :], ALU.mult)
            dve.drain()
            dve.tensor_tensor(KROT[rope, :], KROT[rope, :], MR[rope, :], ALU.add)
            dve.drain().then_inc(mp_dve, 1)
            dve.drain().then_inc(mh_qk, 2)
            t0 = TILE0["mlahead"]
            with dve.Fori(0, 2) as i:
                for j in range(2):
                    lo(i * 2 + (t0 + j + 1), (t0 + j + 1) % 2)
                    for hh in range(2):
                        n = i * 4 + (2 * j + hh)
                        to_q, to_k = (lambda rows_, t=t: t[rows_, bass.ds(n, 1), :] for t in (QA, KA))
                        dve.wait_ge(mh_r, n + 2)
                        dve.tensor_tensor(MR[rope, :], PS[rope, 6, :], SIN[rope, :], ALU.mult)
                        dve.tensor_tensor(QR[0:QK, hh, :], QR[0:QK, hh, :], CG[0:QK, :], ALU.mult)
                        dve.drain()
                        stt(to_k(slice(0, NOPE)), KR[0:NOPE, hh:hh + 1, :], QKG[0:NOPE, 3:4], RS2[0:NOPE, 1:2, :])
                        dve.tensor_tensor(to_k(rope), KROT[rope, :].unsqueeze(1), RS2[rope, 1:2, :], ALU.mult)
                        dve.tensor_tensor(QR[rope, hh, :], QR[rope, hh, :], MR[rope, :], ALU.add)
                        dve.drain()
                        dve.tensor_tensor(to_q(slice(0, QK)), QR[0:QK, hh:hh + 1, :], RS2[0:QK, 0:1, :], ALU.mult)
                        dve.drain().then_inc(mh_qk, 1)
            with dve.Fori(0, 4) as i:
                attend(CHUNKED, lambda k: i * 8 + (k + 32), lambda hh: i * P + hh * HD)
            heads_out(YMHI, YMLO, 4)

            dve.drain().then_inc(g_lo, 1)
            t0, c0 = TILE0["merge"], CHUNK0["merge"]
            with dve.Fori(0, 2) as i:
                for pair in range(2):
                    t, c, chunk = t0 + 5 * pair, c0 + 12 * pair, 2 * pair

                    def gated(gate, to, first):
                        for m in range(2):
                            n = c + first + m
                            dve.wait_ge(g_sig, i * 12 + (6 * pair + gate + m + 1))
                            dve.wait_ge(s_chunk, i * 24 + (n + 1))
                            dve.tensor_tensor(to[:, m, :], to[:, m, :], PS[:, n % 4, :], ALU.mult).then_inc(s_bank_free, 1)
                        dve.drain()
                        if first != 4:
                            dve.tensor_tensor(GA[:], GA[:], GB[:], ALU.add)
                            dve.drain().then_inc(g_mid if first == 6 else g_sum, 1 if first == 6 else 2)

                    for k in (1, 2, 3):
                        lo(i * 10 + (t + k), (t + k) % 2)
                    gated(0, GA, 4)
                    gated(2, GB, 6)
                    lo(i * 10 + (t + 4), (t + 4) % 2)
                    lo(i * 10 + (t + 5), (t + 5) % 2)
                    gated(4, GB, 10)
                    for m in range(2):
                        dve.wait_ge(g_hi, i * 4 + (chunk + m + 1))
                        add_lo(MGLO[:, bass.ds(i * 4 + (chunk + m), 1), :], GA[:, m:m + 1, :],
                               MGHI[:, bass.ds(i * 4 + (chunk + m), 1), :]).then_inc(g_lo, 1)
            add_to_residual("wout2", 2, 2, (0, 1))
            norm("ffn2", lambda c: X[:, c, :], pc("norm_ffn_g_2"), NRM, HHI, HLO)
            ffn(2)
            for n in range(0, 8, 2):
                dve.wait_ge(s_ot, n + 1)
                dve.tensor_copy(OTOK[:, n // 2, 0:S], PS[:, n, :]).then_inc(s_oc, 1)

        @block.tensor
        def _(pe):
            def mm(out, lhsT, rhs, start=True, stop=True):
                return pe.matmul(out, lhsT, rhs, start=start, stop=stop)

            def exact(out, w_hi, w_lo, r_hi, r_lo, kts, start=True, stop=True, opening=False, ready=None):
                for k in range(kts):
                    if ready is not None:
                        pe.wait_ge(n_lo, ready + k + 1)
                    last = mm(out, w_hi(k), r_hi(k), start=start and k == 0, stop=False)
                    if opening and k == 0:
                        last.then_inc(s_started, 1)
                    mm(out, w_hi(k), r_lo(k), start=False, stop=False)
                    last = mm(out, w_lo(k), r_hi(k), start=False, stop=stop and k == kts - 1)
                return last

            def weights(slot, kts, cols, m, offset=0, width=P):
                hi, lo = (wtile(t, slot, kts, cols, offset) for t in (WHI, WLO))
                return lambda k: hi[:, k, m:m + width], lambda k: lo[:, k, m:m + width]

            def moving(hi, lo, k0=0):
                return lambda k: hi[:, k0 + k, :], lambda k: lo[:, k0 + k, :]

            def columns(name, rhs, norm=None, part=None):
                ready = None if norm is None else LO_BEFORE[norm]
                t0, c0 = TILE0[name], CHUNK0[name]
                with pe.Fori(*(part or (0, TILES[name] // 2))) as i:
                    for j in range(2):
                        pe.wait_ge(s_lo, i * 2 + (t0 + j + 1))
                        for m in range(2):
                            c = 2 * j + m
                            pe.wait_ge(s_bank_free, i * 4 + (c0 + c + 1))
                            exact(PS[:, (c0 + c) % 4, :], *weights((t0 + j) % 2, KD, 256, m * P), *moving(*rhs), KD,
                                  opening=m == 0, ready=ready if c == 0 else None).then_inc(s_chunk, 1)

            def down(name):
                t0, c0 = TILE0[name], CHUNK0[name]
                with pe.Fori(0, 2) as i:
                    for half in range(2):
                        for part, (k0, kts) in enumerate(DOWN_PARTS):
                            j = 3 * half + part
                            pe.wait_ge(s_lo, i * 6 + (t0 + j + 1))
                            for m in range(2):
                                c = 2 * half + m
                                if part == 0:
                                    pe.wait_ge(s_bank_free, i * 4 + (c0 + c + 1))
                                last = exact(PS[:, (c0 + c) % 4, :], *weights((t0 + j) % 2, kts, 256, m * P),
                                             *moving(FHI, FLO, k0), kts, start=part == 0, stop=part == 2,
                                             opening=m == 0)
                                if part == 2:
                                    last.then_inc(s_chunk, 1)

            def norm(name, scratch):
                use, first, n = NORM_USE[name], SQ_BASE[name], NORM_N[name]
                if use:
                    pe.wait_ge(n_r, use)
                if name in STREAMED:
                    pe.wait_ge(n_sum, STREAMED.index(name) + 1)
                    last = mm(PS[:, 4, :], ONES[:], R[:])
                else:
                    for c in range(n):
                        pe.wait_ge(n_sq, first + c + 1)
                        last = mm(PS[:, 4, :], ONES[:], scratch[:, c, :], start=c == 0, stop=c == n - 1)
                last.then_inc(n_ms, 1)

            pe.wait_ge(s_const, 1)
            pe.wait_ge(s_params, 16 * len(PARAM_ROWS))
            for tile in range(5):
                if tile >= 2:
                    pe.wait_ge(s_ptc, tile - 1)
                n = PUSED[tile]
                pe.transpose(PS[:, 5 + tile % 2, 0:n], PROWS[0:n, tile, :], IDENT[0:n, 0:n]).then_inc(s_pt, 1)
            pe.wait_ge(s_xin, 16 * NT)
            for c in range(KD):
                if c >= 4:
                    pe.wait_ge(s_x, c - 3)
                for q in range(NT):
                    last = pe.transpose(PS[:, c % 4, q * P:(q + 1) * P], XTOK[:, q, c * P:(c + 1) * P], IDENT[:])
                last.then_inc(s_xt, 1)
            norm("mix1", NRM)
            columns("proj1", (HHI, HLO), "mix1", (0, 3))
            pe.wait_ge(s_small, SMALL_LOADS)
            pe.wait_ge(rg_dve, RG_DVE["u"])
            for c in range(RG):
                last = mm(PS[:, 4 + c, :], WR[:, c, :], YP[:, c, :])
            last.then_inc(rg_pe, 1)
            columns("proj1", (HHI, HLO), part=(3, 4))
            pe.wait_ge(rg_act, RG_ACT["r_sigmoid"])
            for c in range(RG):
                last = mm(PS[:, 4 + c, :], WI[:, c, :], YP[:, c, :])
            last.then_inc(rg_pe, 1)
            columns("proj1", (HHI, HLO), part=(4, 6))

            pe.wait_ge(rg_act, RG_ACT["sigmoids"])
            pe.wait_ge(s_bank_free, 4 + CHUNK0["wout1"])
            with pe.Fori(0, HG) as i:
                def act(name):
                    pe.wait_ge(hg_act, i * len(HG_ACT) + HG_ACT[name])

                def dve(name):
                    pe.wait_ge(hg_dve, i * len(HG_DVE) + HG_DVE[name])

                for level in range(LEVELS + 1):
                    dve("qk" if level == 0 else f"m{level - 1}")
                    if level >= 2:
                        dve(f"c{level - 2}")
                    for h in range(2):
                        for q in range(NT):
                            b, cols = slice(h * HD, (h + 1) * HD), slice(q * P, (q + 1) * P)
                            keys = HK[b, cols] if level == 0 else HM[b, (level - 1) % 2, cols]
                            queries = HQ[b, cols] if level == 0 else HM[b, (level - 1) % 2, cols]
                            last = mm(PS[:, 4 + 2 * (level % 2) + h, cols], keys, queries)
                    last.then_inc(hg_pe, 1)
                dve("gated")
                for q in range(NT):
                    cols = slice(q * P, (q + 1) * P)
                    pe.transpose(PS[:, 0, cols], HVS[:, cols], IDENT[:])
                    last = pe.transpose(PS[:, 1, cols], HKD[:, cols], IDENT[:])
                last.then_inc(hg_pe, 1)
                act("v_turned")
                for q in range(3):
                    last = mm(PS[:, 2, q * P:(q + 1) * P], HKDT[:, q, :], HVT[:, q, :])
                last.then_inc(hg_pe, 1)
                dve("state")
                for q in range(NT):
                    cols = slice(q * P, (q + 1) * P)
                    if q:
                        mm(PS[:, 3, cols], HS[:, q - 1, :], HQG[:, cols], stop=False)
                    for h in range(2):
                        b = slice(h * HD, (h + 1) * HD)
                        last = mm(PS[b, 3, cols], HVT[:, q, b], HST[:, h, cols], start=q == 0)
                last.then_inc(hg_pe, 1)

            for half in range(2):
                pe.wait_ge(hn_sq, 1)
                if half:
                    pe.wait_ge(hn_r, 1)
                for c in range(4):
                    last = mm(PS[:, 4 + c, :], BONES[:], SQ1[:, 4 * half + c, :])
                last.then_inc(hn_ps, 1)
            pe.wait_ge(hn_lo, 1)
            columns("wout1", (HHI, HLO))
            norm("ffn1", NRM)
            columns("up1", (HHI, HLO), "ffn1")
            pe.wait_ge(f_lo, NF)
            down("down1")

            pe.wait_ge(e_p, 16 * NT)
            for k in range(PLE // P):
                for q in range(NT):
                    last = pe.transpose(PS[:, 6 + k, q * P:(q + 1) * P], PTOK[:, q, k * P:(k + 1) * P], IDENT[:])
            last.then_inc(e_pt, 1)
            t0, c0 = TILE0["pleproj"], CHUNK0["pleproj"]
            pe.wait_ge(e_plo, 1)
            pe.wait_ge(s_lo, t0 + 1)
            for c in range(KD):
                pe.wait_ge(s_bank_free, c0 + c + 1)
                exact(PS[:, (c0 + c) % 4, :], *weights(t0 % 2, 2, D, c * P), *moving(PHI, PLO), 2,
                      opening=c == 0).then_inc(s_chunk, 1)
            pe.wait_ge(e_lo, KD)
            columns("plegate", (HHI, HLO))
            norm("final", NRM)
            norm("mix2", NRM)
            t, c = TILE0["small"], CHUNK0["small"]
            pe.wait_ge(s_lo, t + 1)
            pe.wait_ge(s_bank_free, c + 1)
            exact(PS[0:SMALL_W, c % 4, :], *weights(t % 2, KD, SMALL_W, 0, width=SMALL_W), *moving(HHI, HLO), KD,
                  opening=True, ready=LO_BEFORE["mix2"]).then_inc(s_chunk, 1)
            columns("xbc", (HHI, HLO))
            columns("z", (HHI, HLO))

            pe.drain().then_inc(h_y, 2)
            pe.wait_ge(s_bank_free, 4 + CHUNK0["foxqk"])
            pe.wait_ge(ss_dve, SS_DVE["packed"])
            for q in range(NT):
                cols = slice(q * P, (q + 1) * P)
                last = pe.transpose(PS[:, 0, cols], PACK[:, cols], IDENT[:])
            last.then_inc(ss_pe, 1)
            pe.wait_ge(ss_act, SS_ACT["silu"])
            for g in range(2):
                if g:
                    pe.wait_ge(ss_dve, SS_DVE["y0"])
                for q in range(NT):
                    cols = slice(q * P, (q + 1) * P)
                    for j in range(4):
                        pe.transpose(PS[:, 4 + q, j * P:(j + 1) * P], XBC[:, 4 * g + j, cols], IDENT[:])
                    pe.transpose(PS[:, 1, cols], XBC[:, 8 + g, cols], IDENT[:])
                    last = mm(PS[:, 2, cols], XBC[:, 8 + g, cols], XBC[:, 10 + g, cols])
                last.then_inc(ss_pe, 1)
                pe.wait_ge(ss_dve, SS_DVE[f"xdw{g}"])
                pe.wait_ge(ss_act, SS_ACT[f"bt{g}"])
                for q in range(3):
                    last = mm(PS[:, 4 + q, :], BT[:, q, :], XW[:, q, :])
                last.then_inc(ss_pe, 1)
                pe.wait_ge(ss_dve, SS_DVE[f"h{g}"])
                for q in range(1, NT):
                    last = mm(PS[:, q, :], XBC[:, 10 + g, q * P:(q + 1) * P], SH[:, q - 1, :])
                last.then_inc(ss_pe, 1)
                pe.wait_ge(ss_dve, SS_DVE[f"yt{g}"])
                with pe.Fori(0, 4) as i:
                    for b in range(2):
                        pe.wait_ge(h_m, i * 2 + (8 * g + b + 1))
                        for q in range(NT):
                            head = bass.ds(i * P + b * HD, HD)
                            last = mm(PS[:, q, head], DM[:, b, q * P:(q + 1) * P], XD[:, q, head])
                        last.then_inc(h_y, 1)
                pe.wait_ge(ss_dve, SS_DVE[f"ysum{g}"])
                for q in range(NT):
                    for j in range(4):
                        last = pe.transpose(PS[:, 4 + j, q * P:(q + 1) * P], YT[:, q, j * P:(j + 1) * P], IDENT[:])
                last.then_inc(ss_pe, 1)
            norm("ssm", NS)

            def attention(k_rows, slot, at, values):
                def score(u):
                    hh, qb = u // 4, u % 4
                    if u >= 4:
                        pe.wait_ge(a_exp, at(u - 3))
                    mm(PS[:, u % 4, 0:(qb + 1) * P], QS[0:k_rows, slot + hh, qb * P:(qb + 1) * P],
                       KS[0:k_rows, slot + hh, 0:(qb + 1) * P]).then_inc(a_s, 1)

                def weighted(u):
                    pe.wait_ge(a_pt, at(u + 1))
                    if u >= 2:
                        pe.wait_ge(a_o, at(u - 1))
                    for kb in range(u % 4 + 1):
                        last = mm(PS[:, 6 + u % 2, 0:HD], PT[:, u % 2, kb * P:(kb + 1) * P], values(kb, u // 4),
                                  start=kb == 0, stop=kb == u % 4)
                    last.then_inc(a_pv, 1)

                for u in range(4):
                    score(u)
                for u in range(8):
                    pe.wait_ge(a_exp, at(u + 1))
                    if u >= 2:
                        pe.wait_ge(a_pt, at(u - 1))
                    for kb in range(u % 4 + 1):
                        last = pe.transpose(PS[:, 4 + u % 2, kb * P:(kb + 1) * P], PR[:, u % 2, kb * P:(kb + 1) * P], IDENT[:])
                    last.then_inc(a_t, 1)
                    if u < 4:
                        score(u + 4)
                    if u:
                        weighted(u - 1)
                weighted(7)
                pe.wait_ge(a_o, at(8))

            def heads_out():
                for c in range(4):
                    for q in range(NT):
                        last = pe.transpose(PS[:, 4 + c, q * P:(q + 1) * P], OH[:, q, c * P:(c + 1) * P], IDENT[:])
                    last.then_inc(o_t, 1)

            t0, c0 = TILE0["foxqk"], CHUNK0["foxqk"]
            with pe.Fori(0, 2) as i:
                def sums(c):
                    pe.wait_ge(q_sq, i * 4 + (c + 1))
                    if c >= 2:
                        pe.wait_ge(q_r, i * 4 + (c - 1))
                    mm(PS[:, 4 + c % 2, :], BONES[:], SQF[:, c % 2, :]).then_inc(q_ms, 1)

                for j in range(2):
                    pe.wait_ge(s_lo, i * 2 + (t0 + j + 1))
                    for m in range(2):
                        c = 2 * j + m
                        pe.wait_ge(s_bank_free, i * 4 + (c0 + c + 1))
                        exact(PS[:, (c0 + c) % 4, :], *weights((t0 + j) % 2, KD, 256, m * P), *moving(HHI, HLO), KD,
                              opening=m == 0).then_inc(s_chunk, 1)
                        if c:
                            sums(c - 1)
                sums(3)
            t0, c0 = TILE0["foxv"], CHUNK0["foxv"]
            for half in range(2):
                t = t0 + half
                pe.wait_ge(s_lo, t + 1)
                w_hi, w_lo = weights(t % 2, KD, 256, 0, width=256)
                for tc in range(NT):
                    c, cols = c0 + 4 * half + tc, slice(tc * P, (tc + 1) * P)
                    pe.wait_ge(s_bank_free, c + 1)
                    exact(PS[:, c % 4, 0:256], lambda k: HHI[:, k, cols], lambda k: HLO[:, k, cols], w_hi, w_lo, KD,
                          opening=tc == 0).then_inc(s_chunk, 1)
            pe.wait_ge(s_bank_free, 4 + CHUNK0["mlac"])
            pe.wait_ge(v_out, 1)
            pe.drain().then_inc(a_s, 16)
            with pe.Fori(0, 2) as i:
                for j in range(2):
                    pe.wait_ge(a_ready, i * 2 + (j + 1))
                    pe.wait_ge(s_frow[j], i * 32 + 32)
                    attention(HD + 2, 2 * j, lambda k: i * 16 + (8 * j + k),
                              lambda kb, hh: VF[:, kb, bass.ds(i * 2 * P + j * P + hh * HD, HD)])
            heads_out()

            t0, c0 = TILE0["mlac"], CHUNK0["mlac"]
            for c in range(5):
                t, cols = t0 + c // 2, 256 if c < 4 else 128
                if c % 2 == 0:
                    pe.wait_ge(s_lo, t + 1)
                pe.wait_ge(s_bank_free, c0 + c + 1)
                exact(PS[:, (c0 + c) % 4, :], *weights(t % 2, KD, cols, (c % 2) * P), *moving(HHI, HLO), KD,
                      opening=c % 2 == 0).then_inc(s_chunk, 1)
            pe.wait_ge(o_lo, 4)
            norm("mlaq", NC)
            norm("mlakv", NC)
            rope = slice(NOPE, QK)
            pe.wait_ge(mp_dve, MP_DVE["swaps"])
            mm(PS[rope, 6, :], SW[rope, 1, :], KROT[rope, :]).then_inc(mp_pe, 1)
            pe.wait_ge(mp_dve, MP_DVE["krot"])
            pe.wait_ge(mp_act, MP_ACT["trig"])
            pe.wait_ge(n_lo, LO_BEFORE["ffn2"])
            pe.wait_ge(s_bank_free, 4 + CHUNK0["merge"])
            pe.drain().then_inc(mh_ms, 2)
            t0 = TILE0["mlahead"]
            with pe.Fori(0, 2) as i:
                for j in range(2):
                    slot = (t0 + j) % 2

                    def head(k):
                        return i * 4 + (2 * j + k)

                    def sums(hh):
                        pe.wait_ge(mh_sq, head(hh + 1))
                        pe.wait_ge(mh_r, head(hh + 1))
                        pe.wait_ge(mh_free, head(hh + 3))
                        pe.wait_ge(mh_qk, head(hh + 2))
                        for b in range(2):
                            mm(PS[0:QK, 4 + b, :], ONES[0:QK, 0:QK], SQM[0:QK, 2 * hh + b, :])
                        mm(PS[rope, 6, :], SW[rope, 0, :], QR[rope, hh, :]).then_inc(mh_ms, 1)

                    pe.wait_ge(s_lo, i * 2 + (t0 + j + 1))
                    for hh in range(2):
                        pe.wait_ge(mh_free, head(hh + 1))
                        exact(PS[0:QK, 2 * hh, :], *weights(slot, 3, 192, hh * QK, width=QK), *moving(CQHI, CQLO), 3,
                              opening=hh == 0)
                        exact(PS[:, 2 * hh + 1, :], *weights(slot, 2, 256, hh * P, offset=576), *moving(CQHI, CQLO, 3), 2
                              ).then_inc(mh_p, 1)
                    sums(0)
                    v_hi, v_lo = (wtile(w, slot, 2, 256, 576).rearrange("p k (h n) -> p k h n", n=P)[:, :, :, HD:P]
                                  for w in (WHI, WLO))
                    pe.wait_ge(mh_va, i * 2 + (j + 1))
                    for tc in range(NT):
                        cols = slice(tc * P, (tc + 1) * P)
                        last = exact(PS[:, 7, cols].rearrange("p (h n) -> p h n", n=HD), lambda k: CQHI[:, 3 + k, cols],
                                     lambda k: CQLO[:, 3 + k, cols], lambda k: v_hi[:, k], lambda k: v_lo[:, k], 2)
                    last.then_inc(mh_v, 1)
                    sums(1)
            pe.wait_ge(mh_va, 5)
            pe.wait_ge(mh_r, 9)
            pe.wait_ge(mh_qk, 10)
            with pe.Fori(0, 2) as i:
                for j in range(2):
                    pe.wait_ge(a_ready, i * 2 + (j + 5))
                    attention(QK, 2 * j, lambda k: i * 16 + (8 * j + k + 32),
                              lambda kb, hh: VA[:, kb, bass.ds(i * 2 * P + j * P + hh * HD, HD)])
            heads_out()

            t0, c0 = TILE0["merge"], CHUNK0["merge"]
            pe.wait_ge(o_lo, 8)
            with pe.Fori(0, 2) as i:
                for pair in range(2):
                    t, c = t0 + 5 * pair, c0 + 12 * pair
                    plan = ((0, 0, KD, 0, (HHI, HLO)), (1, 2, KD, 0, (HHI, HLO)), (2, 4, 4, 0, (YMHI, YMLO)),
                            (2, 6, 4, 1024, (YFHI, YFLO)), (3, 8, KD, 0, (HHI, HLO)), (4, 10, KD, 0, (YS2HI, YS2LO)))
                    for j, first, kts, offset, rhs in plan:
                        if offset == 0:
                            pe.wait_ge(s_lo, i * 10 + (t + j + 1))
                        if j == 4:
                            pe.wait_ge(s_reload, 32)
                        for m in range(2):
                            n = c + first + m
                            pe.wait_ge(s_bank_free, i * 24 + (n + 1))
                            exact(PS[:, n % 4, :], *weights((t + j) % 2, kts, 256, m * P, offset=offset), *moving(*rhs), kts,
                                  opening=m == 0 and offset == 0).then_inc(s_chunk, 1)
            pe.wait_ge(g_lo, 9)
            columns("wout2", (MGHI, MGLO))
            norm("ffn2", NRM)
            columns("up2", (HHI, HLO), "ffn2")
            pe.wait_ge(f_lo, 2 * NF)
            down("down2")
            pe.wait_ge(s_x, X_DOWN2 + KD)
            for n in range(8):
                for c in range(4):
                    last = pe.transpose(PS[:, n, c * P:(c + 1) * P], X[:, 4 * (n % 2) + c, (n // 2) * P:(n // 2 + 1) * P],
                                        IDENT[:])
                last.then_inc(s_ot, 1)


def kernel(**inputs):
    import concourse.bacc as bacc
    from concourse.bass_utils import run_bass_kernel_spmd

    nc = bacc.Bacc("TRN2", target_bir_lowering=False, num_devices=1)
    arrays = {name: np.ascontiguousarray(inputs[name]) for name in INPUTS}
    arrays["inv_freq"] = inv_freq()
    dram = {name: nc.dram_tensor(name, a.shape, mybir.dt.from_np(a.dtype), kind="ExternalInput").ap()
            for name, a in arrays.items()}
    out = nc.dram_tensor("out", (1, S, D), F32, kind="ExternalOutput").ap()
    build(nc, dram, out)
    result = run_bass_kernel_spmd(nc, [arrays], core_ids=[0])
    return result.results[0]["out"]
```
